# Optimizing a Trainium2 kernel written in Bass

```python
import math
import jax, jax.numpy as jnp
from jax import lax
import numpy as np

D_MODEL = 1024
BATCH = 1
SEQ = 512
DEPTH = 1

N_DIFF_HEADS = 4
DIFF_QK_DIM = 64
DIFF_V_DIM = 2 * DIFF_QK_DIM
DIFF_WIDTH = N_DIFF_HEADS * DIFF_V_DIM
N_RET_HEADS = 4
RET_QK_DIM = 64
RET_V_DIM = 2 * RET_QK_DIM
RET_WIDTH = N_RET_HEADS * RET_V_DIM
MIX_WIDTH = DIFF_WIDTH + RET_WIDTH
PROJ_SIZES = (
    N_DIFF_HEADS * 2 * DIFF_QK_DIM,
    N_DIFF_HEADS * 2 * DIFF_QK_DIM,
    DIFF_WIDTH,
    N_RET_HEADS * RET_QK_DIM,
    N_RET_HEADS * RET_QK_DIM,
    RET_WIDTH,
    RET_WIDTH,
)
PROJ_WIDTH = sum(PROJ_SIZES)
PROJ_SPLITS = tuple(int(s) for s in np.cumsum(PROJ_SIZES)[:-1])

ROPE_THETA = 10000.0
Q_BLOCK = 128
RET_CHUNK = 128
RMS_EPS = 1e-5

N_EXPERTS = 32
TOP_K = 4
D_FF_EXPERT = D_MODEL
SWIGLU_LIMIT = 7.0
SWIGLU_ALPHA = 1.702
MOE_BLOCK = 128

kernel_name = 'hybrid_diffattn_retention_moe'

def rms_norm(x, g):
    xf = x.astype(jnp.float32)
    y = xf * lax.rsqrt(jnp.mean(xf * xf, axis=-1, keepdims=True) + RMS_EPS)
    return (y * g.astype(jnp.float32)).astype(x.dtype)

def rope(x, positions):
    d = x.shape[-1]
    inv_freq = 1.0 / (ROPE_THETA ** (jnp.arange(0, d, 2, dtype=jnp.float32) / d))
    ang = positions.astype(jnp.float32)[..., None] * inv_freq
    ang = ang.reshape(ang.shape[:2] + (1,) * (x.ndim - 3) + (d // 2,))
    cos = jnp.concatenate([jnp.cos(ang), jnp.cos(ang)], axis=-1)
    sin = jnp.concatenate([jnp.sin(ang), jnp.sin(ang)], axis=-1)
    xf = x.astype(jnp.float32)
    x1, x2 = xf[..., : d // 2], xf[..., d // 2:]
    rot = jnp.concatenate([-x2, x1], axis=-1)
    return (xf * cos + rot * sin).astype(x.dtype)

def diff_attention(q, k, v, lam):
    B, S, H, _ = v.shape
    n_blocks = S // Q_BLOCK
    scale = DIFF_QK_DIM ** -0.5
    k_pos = jnp.arange(S)

    def block(i):
        start = i * Q_BLOCK
        qb = lax.dynamic_slice_in_dim(q, start, Q_BLOCK, axis=1)
        s = jnp.einsum('bqhmd,bkhmd->bhmqk', qb, k,
                       preferred_element_type=jnp.float32) * scale
        q_pos = start + jnp.arange(Q_BLOCK)
        causal = k_pos[None, :] <= q_pos[:, None]
        s = jnp.where(causal, s, -jnp.inf)
        p = jax.nn.softmax(s, axis=-1)
        a = p[:, :, 0] - lam * p[:, :, 1]
        return jnp.einsum('bhqk,bkhd->bqhd', a.astype(v.dtype), v)

    out = lax.map(block, jnp.arange(n_blocks))
    return jnp.moveaxis(out, 0, 1).reshape(B, S, H, v.shape[-1])

def retention(q, k, v, log_decay):
    B, S, H, dk = q.shape
    dv = v.shape[-1]
    C = RET_CHUNK
    nc = S // C
    q = q.reshape(B, nc, C, H, dk)
    k = (k * (dk ** -0.5)).reshape(B, nc, C, H, dk)
    v = v.reshape(B, nc, C, H, dv)
    idx = jnp.arange(C, dtype=jnp.float32)
    rel = idx[:, None] - idx[None, :]
    intra_decay = jnp.where(rel >= 0,
                            jnp.exp(log_decay[:, None, None] * jnp.maximum(rel, 0.0)),
                            0.0)
    scores = jnp.einsum('bnihd,bnjhd->bnhij', q, k,
                        preferred_element_type=jnp.float32) * intra_decay
    y_intra = jnp.einsum('bnhij,bnjhe->bnihe', scores, v.astype(jnp.float32))
    k_decay = jnp.exp(log_decay[None, :] * (C - 1 - idx)[:, None])
    kv = jnp.einsum('bnjhd,jh,bnjhe->bnhde', k.astype(jnp.float32), k_decay,
                    v.astype(jnp.float32))
    chunk_decay = jnp.exp(log_decay * C)[None, :, None, None]

    def step(state, kv_c):
        return chunk_decay * state + kv_c, state

    init = jnp.zeros((B, H, dk, dv), jnp.float32)
    _, prev = lax.scan(step, init, jnp.moveaxis(kv, 1, 0))
    prev = jnp.moveaxis(prev, 0, 1)
    q_decay = jnp.exp(log_decay[None, :] * (idx + 1.0)[:, None])
    y_cross = jnp.einsum('bnihd,ih,bnhde->bnihe', q.astype(jnp.float32), q_decay, prev)
    return (y_intra + y_cross).reshape(B, S, H, dv).astype(v.dtype)

def moe(x2d, w_router, b_router, w_in, b_in, w_out, b_out):
    N, D = x2d.shape
    logits = (x2d @ w_router).astype(jnp.float32) + b_router.astype(jnp.float32)
    top_val, top_idx = lax.top_k(logits, TOP_K)
    gates = jax.nn.softmax(top_val, axis=-1)
    NK = N * TOP_K
    e_flat = top_idx.reshape(NK)
    tok = jnp.arange(NK) // TOP_K
    order = jnp.argsort(e_flat)
    e_s = e_flat[order]
    tok_s = tok[order]
    g_s = gates.reshape(NK)[order]
    counts = jnp.bincount(e_flat, length=N_EXPERTS)
    offsets = jnp.cumsum(counts) - counts
    padded = ((counts + MOE_BLOCK - 1) // MOE_BLOCK) * MOE_BLOCK
    pad_end = jnp.cumsum(padded)
    pad_off = pad_end - padded
    dest = pad_off[e_s] + (jnp.arange(NK) - offsets[e_s])
    P = ((NK + MOE_BLOCK - 1) // MOE_BLOCK) * MOE_BLOCK + N_EXPERTS * MOE_BLOCK
    n_blk = P // MOE_BLOCK
    x_buf = jnp.zeros((P, D), x2d.dtype).at[dest].set(x2d[tok_s])
    blk_expert = jnp.minimum(
        jnp.searchsorted(pad_end, jnp.arange(n_blk) * MOE_BLOCK, side='right'),
        N_EXPERTS - 1)

    def expert_block(args):
        xb, e = args
        h = xb @ w_in[e] + b_in[e]
        glu = jnp.minimum(h[:, ::2], SWIGLU_LIMIT)
        lin = jnp.clip(h[:, 1::2], -SWIGLU_LIMIT, SWIGLU_LIMIT)
        act = glu * jax.nn.sigmoid(SWIGLU_ALPHA * glu) * (lin + 1.0)
        return act @ w_out[e] + b_out[e]

    y_buf = lax.map(expert_block,
                    (x_buf.reshape(n_blk, MOE_BLOCK, D), blk_expert)).reshape(P, D)
    y = y_buf[dest] * g_s[:, None].astype(y_buf.dtype)
    return jax.ops.segment_sum(y, tok_s, num_segments=N)

def setup_inputs(seed: int = 0) -> dict:
    key = jax.random.key(seed)
    ks = jax.random.split(key, 20)
    f32 = jnp.float32
    L = DEPTH
    x = jax.random.normal(ks[0], (BATCH, SEQ, D_MODEL), f32)
    positions = jnp.broadcast_to(jnp.arange(SEQ, dtype=jnp.int32), (BATCH, SEQ))
    norm1_g = 1.0 + 0.02 * jax.random.normal(ks[1], (L, D_MODEL), f32)
    w_in = jax.random.normal(ks[2], (L, D_MODEL, PROJ_WIDTH), f32) * D_MODEL ** -0.5
    lambda_q1 = 0.1 * jax.random.normal(ks[3], (L, DIFF_QK_DIM), f32)
    lambda_k1 = 0.1 * jax.random.normal(ks[4], (L, DIFF_QK_DIM), f32)
    lambda_q2 = 0.1 * jax.random.normal(ks[5], (L, DIFF_QK_DIM), f32)
    lambda_k2 = 0.1 * jax.random.normal(ks[6], (L, DIFF_QK_DIM), f32)
    diff_norm_g = 1.0 + 0.02 * jax.random.normal(ks[7], (L, DIFF_V_DIM), f32)
    ret_norm_g = 1.0 + 0.02 * jax.random.normal(ks[8], (L, N_RET_HEADS, RET_V_DIM), f32)
    w_o = jax.random.normal(ks[9], (L, MIX_WIDTH, D_MODEL), f32) * MIX_WIDTH ** -0.5
    norm2_g = 1.0 + 0.02 * jax.random.normal(ks[10], (L, D_MODEL), f32)
    w_router = jax.random.normal(ks[11], (L, D_MODEL, N_EXPERTS), f32) * D_MODEL ** -0.5
    b_router = 0.01 * jax.random.normal(ks[12], (L, N_EXPERTS), f32)
    w_moe_in = jax.random.normal(ks[13], (L, N_EXPERTS, D_MODEL, 2 * D_FF_EXPERT), f32) * D_MODEL ** -0.5
    b_moe_in = 0.01 * jax.random.normal(ks[14], (L, N_EXPERTS, 2 * D_FF_EXPERT), f32)
    w_moe_out = jax.random.normal(ks[15], (L, N_EXPERTS, D_FF_EXPERT, D_MODEL), f32) * D_FF_EXPERT ** -0.5
    b_moe_out = 0.01 * jax.random.normal(ks[16], (L, N_EXPERTS, D_MODEL), f32)
    norm_f_g = 1.0 + 0.02 * jax.random.normal(ks[17], (D_MODEL,), f32)
    return {'x': x, 'positions': positions, 'norm1_g': norm1_g, 'w_in': w_in,
            'lambda_q1': lambda_q1, 'lambda_k1': lambda_k1,
            'lambda_q2': lambda_q2, 'lambda_k2': lambda_k2,
            'diff_norm_g': diff_norm_g, 'ret_norm_g': ret_norm_g, 'w_o': w_o,
            'norm2_g': norm2_g, 'w_router': w_router, 'b_router': b_router,
            'w_moe_in': w_moe_in, 'b_moe_in': b_moe_in,
            'w_moe_out': w_moe_out, 'b_moe_out': b_moe_out, 'norm_f_g': norm_f_g}

def reference(x, positions, norm1_g, w_in, lambda_q1, lambda_k1, lambda_q2, lambda_k2,
              diff_norm_g, ret_norm_g, w_o, norm2_g, w_router, b_router,
              w_moe_in, b_moe_in, w_moe_out, b_moe_out, norm_f_g):
    B, S, D = x.shape
    log_decay = jnp.log(1.0 - 2.0 ** (-5.0 - jnp.arange(N_RET_HEADS, dtype=jnp.float32)))
    for l in range(DEPTH):
        h = rms_norm(x, norm1_g[l])
        proj = h @ w_in[l]
        dq, dk, dv, rq, rk, rv, rg = jnp.split(proj, PROJ_SPLITS, axis=-1)
        dq = rope(dq.reshape(B, S, N_DIFF_HEADS, 2, DIFF_QK_DIM), positions)
        dk = rope(dk.reshape(B, S, N_DIFF_HEADS, 2, DIFF_QK_DIM), positions)
        dv = dv.reshape(B, S, N_DIFF_HEADS, DIFF_V_DIM)
        lam_init = 0.8 - 0.6 * math.exp(-0.3 * l)
        lam = (jnp.exp(jnp.sum(lambda_q1[l].astype(jnp.float32) * lambda_k1[l].astype(jnp.float32)))
               - jnp.exp(jnp.sum(lambda_q2[l].astype(jnp.float32) * lambda_k2[l].astype(jnp.float32)))
               + lam_init)
        d_out = diff_attention(dq, dk, dv, lam)
        d_out = rms_norm(d_out, diff_norm_g[l]) * (1.0 - lam_init)
        rq = rope(rq.reshape(B, S, N_RET_HEADS, RET_QK_DIM), positions)
        rk = rope(rk.reshape(B, S, N_RET_HEADS, RET_QK_DIM), positions)
        rv = rv.reshape(B, S, N_RET_HEADS, RET_V_DIM)
        r_out = rms_norm(retention(rq, rk, rv, log_decay), ret_norm_g[l])
        r_out = r_out.reshape(B, S, RET_WIDTH) * jax.nn.silu(rg)
        mix = jnp.concatenate([d_out.reshape(B, S, DIFF_WIDTH), r_out], axis=-1)
        x = x + mix @ w_o[l]
        h2 = rms_norm(x, norm2_g[l]).reshape(B * S, D)
        y = moe(h2, w_router[l], b_router[l], w_moe_in[l], b_moe_in[l],
                w_moe_out[l], b_moe_out[l])
        x = x + y.reshape(B, S, D)
    return rms_norm(x, norm_f_g)


_drawn_inputs = setup_inputs


def setup_inputs(seed=0):
    import zlib

    import numpy as np

    out = dict(_drawn_inputs(seed))
    spreads = {}
    factors = {'lambda_q2': 8.0, 'b_moe_in': 8.0, 'b_moe_out': 8.0, 'norm_f_g': 2.881}
    for name, (base, spread) in spreads.items():
        noise = np.random.default_rng([zlib.crc32(name.encode()), seed]).standard_normal(out[name].shape)
        drawn = base * np.exp(spread * noise) if base else spread * noise
        out[name] = __import__('jax').numpy.asarray(drawn.astype(out[name].dtype))
    for name, factor in factors.items():
        out[name] = (out[name] * factor).astype(out[name].dtype)
    return out
```

```python
from contextlib import ExitStack
import math

import numpy as np

import concourse.bass as bass
from concourse import mybir

F32 = mybir.dt.float32
BF16 = mybir.dt.bfloat16
I32 = mybir.dt.int32
U32 = mybir.dt.uint32
ALU = mybir.AluOpType
ACT = mybir.ActivationFunctionType
AX_X = mybir.AxisListType.X

P = 128
SEQ = 512
D = 1024
NT = SEQ // P
KT = D // P
PROJ = 3072
EPS = 1e-5
CW = 256
NCHUNK = PROJ // CW
CQ, CK, CV, CRQ, CRK, CRV, CRG = 0, 512, 1024, 1536, 1792, 2048, 2560
NH = 4
DQ = 64
SCALE = DQ ** -0.5
LAM_INIT = 0.8 - 0.6 * math.exp(-0.3 * 0)
NE = 32
TOPK = 4
FF = 1024
LIMIT = 7.0
SWI_ALPHA = 1.702
RING = 12
IN_CHUNKS = 2 * FF // CW
OUT_CHUNKS = D // CW
N_SMALL = 12
STEPS_PER_EXPERT = 25
WIDTHS = (96, 160, SEQ)
NB = SEQ // P
NOWHERE = float(2 * TOPK * SEQ)
ROPE_CHUNKS = (0, 1, 2, 3, 6, 7)
TWO_PI_A = 6.28125
TWO_PI_B = round((2 * math.pi - TWO_PI_A) * 2.0 ** 20) / 2.0 ** 20
TWO_PI_C = 2 * math.pi - TWO_PI_A - TWO_PI_B
PI_F = 3.1415925
MAGIC = 12582912.0
MASKED = -1.0e30

C_IDENT, C_DECAY, C_QDEC, C_KDEC, C_FREQ = 0, 128, 640, 896, 900
C_N = 932


def shape_constants():
    f = np.float32
    c = np.zeros((P, C_N), f)
    r = np.arange(P)
    c[:, C_IDENT:C_IDENT + P] = np.eye(P)
    masks = np.concatenate([np.where(r[None, :] <= r[:, None], 0.0, MASKED), r[:, None] < r[None, :]], axis=1)
    log_decay = np.log(f(1.0) - f(2.0) ** (f(-5.0) - np.arange(NH, dtype=f))).astype(f)
    for h in range(NH):
        rel = (r[None, :] - r[:, None]).astype(f)
        at = C_DECAY + ((h % 2) * 2 + h // 2) * P
        c[:, at:at + P] = np.where(
            rel >= 0, np.exp(log_decay[h] * np.maximum(rel, 0)), 0.0) * SCALE
        rows = slice(64 * (h % 2), 64 * (h % 2) + 64)
        c[rows, C_QDEC + (h // 2) * P:C_QDEC + (h // 2 + 1) * P] = np.exp(log_decay[h] * (r[None, :] + f(1.0)))
        c[:, C_KDEC + h] = np.exp(log_decay[h] * (P - 1 - r)) * SCALE
    c[:, C_FREQ:C_FREQ + 32] = (f(1.0) / (f(10000.0) ** (np.arange(0, DQ, 2, dtype=f) / f(DQ))))[None, :]
    chunk = np.exp(log_decay * P).astype(f)
    return c, masks.astype(f), np.stack([np.repeat(chunk[0:2], 64), np.repeat(chunk[2:4], 64)], axis=1).astype(f)


def build(nc, x, positions, norm1_g, w_in, lambda_q1, lambda_k1, lambda_q2, lambda_k2, diff_norm_g,
          ret_norm_g, w_o, norm2_g, w_router, b_router, w_moe_in, b_moe_in, w_moe_out, b_moe_out,
          norm_f_g, out):
    ctx = ExitStack()
    with ctx:
        def sb(name, shape, dt=F32):
            return ctx.enter_context(nc.sbuf_tensor(name, shape, dt))

        def sem(name):
            return ctx.enter_context(nc.semaphore(name))

        def sems(name, n):
            return [sem(f"{name}{i}") for i in range(n)]

        def wait(eng, semaphore, value):
            if not (isinstance(value, int) and value <= 0):
                eng.wait_ge(semaphore, value)

        consts_np, masks_np, chunk_decay_np = shape_constants()
        consts_dram = nc.inline_tensor(consts_np, "shape_consts").ap()
        masks_dram = nc.inline_tensor(masks_np, "shape_masks").ap()
        chunk_decay_dram = nc.inline_tensor(chunk_decay_np, "chunk_decays").ap()
        h2_dram = nc.dram_tensor("h2_rows", [SEQ, D], F32, kind="Internal").ap()
        y_dram = nc.dram_tensor("expert_rows", [SEQ * TOPK, D], F32, kind="Internal").ap()

        ring = sb("ring", [P, RING, KT, CW])
        resid = sb("resid", [P, NT, D])
        work = sb("work", [P, 21504])
        cst = sb("cst", [P, C_N])
        cos_sin = sb("cos_sin", [P, 2, NT, 32])
        gain_row = sb("gain_row", [P, D])
        ident_bf = sb("ident_bf", [P, P], BF16)
        causal_bf = sb("causal_bf", [P, P], BF16)
        utri_bf = sb("utri_bf", [P, P], BF16)
        ones_bf = sb("ones_bf", [P, P], BF16)
        g1_col = sb("g1_col", [P, KT])
        pos_i = sb("pos_i", [P, NT], I32)
        pos_f = sb("pos_f", [P, NT])
        lam = sb("lam", [P, 8])
        chunk_decay = sb("chunk_decay", [P, 2])
        b_router_row = sb("b_router_row", [P, NE])
        stat = sb("stat", [P, 56])
        eps_col = sb("eps_col", [P, 1])
        row_max = sb("row_max", [P, 2, 2])
        row_bias = sb("row_bias", [P, 2, 2])
        row_sum = sb("row_sum", [P, 2, 2])
        row_rec = sb("row_rec", [P, 2, 2])
        counts = sb("counts", [1, 2 * NE])
        classes = sb("classes", [1, NE], I32)
        extras_before = sb("extras_before", [1, NE], I32)
        pos_cur = sb("pos_cur", [P, NT])
        bias_cur = sb("bias_cur", [P, 2 * KT])
        dest_next = sb("dest_next", [P, NB], I32)
        dest_cur = sb("dest_cur", [P, NB], I32)
        token_next = sb("token_next", [P, NB], I32)
        gate_next = sb("gate_next", [P, NB])
        gate_cur = sb("gate_cur", [P, NB])

        def w(a, n, rows=P):
            return work[0:rows, a:a + n]

        proj = w(0, NT * PROJ).rearrange("p (i c) -> p i c", i=NT)
        xn = w(4096, NT * D).rearrange("p (i c) -> p i c", i=NT)
        junk1 = w(0, NT * D).rearrange("p (i c) -> p i c", i=NT)
        hT = w(12288, KT * SEQ).rearrange("p (k t) -> p k t", k=KT)
        qkT = w(12288, 12 * SEQ).rearrange("p (g t) -> p g t", g=12)
        rope_tmp = w(18432, 4 * 512).rearrange("p (a i g f) -> p a i g f", a=4, i=NT, g=4)
        ang = w(18432, 6 * 128).rearrange("p (a i f) -> p a i f", a=6, i=NT)
        lam_rows = w(19456, 4 * DQ).rearrange("p (a d) -> p a d", a=4)
        raw_masks = w(20480, 2 * P)
        probs = w(18432, 2 * 2 * SEQ).rearrange("p (b m t) -> p b m t", b=2, m=2)
        attT = w(20480, 2 * SEQ).rearrange("p (b t) -> p b t", b=2)
        mix = proj[:, :, 0:D]
        square_tmp = proj[:, :, CRQ:CRQ + P]
        g2_row = proj[:, :, CRQ:CRQ + 256]
        st_s = w(18432, 2 * 512).rearrange("p (b r a n) -> p b r a n", b=2, r=2, a=2)
        state = w(19456, 2 * P).rearrange("p (a n) -> p a n", a=2)
        qdT = w(20480, 2 * SEQ).rearrange("p (a t) -> p a t", a=2)
        mixT = w(12288, 2 * D).rearrange("p (b k t) -> p b k t", b=2, k=KT)
        b_in_rows = w(14336, 2 * FF, NE)
        w_router_sb = w(16384, KT * NE).rearrange("p (k e) -> p k e", k=KT)
        junk2 = w(16896, D)
        h2_row = proj[:, :, 0:D]
        b_out_rows = w(5120, D, NE)
        gateT = w(7168, SEQ, NE)
        route = w(18944, NT * NE * 4).rearrange("p (i e c) -> p i e c", i=NT, e=NE)
        slot_of = w(19456, NT * NE).rearrange("p (i e) -> p i e", i=NT)
        bias_in = w(19584, NE * 2 * KT).rearrange("p (e c) -> p e c", e=NE)
        logits = w(20096, NE)
        top8 = w(20128, 8)
        top8_f = w(20136, 8)
        top8_i = w(20144, 8).bitcast(U32)
        picked = w(20160, NT * NE).rearrange("p (i e) -> p i e", i=NT)
        expo = w(20288, NE)
        gates = w(20320, NT * NE).rearrange("p (i e) -> p i e", i=NT)
        rank = w(20448, NE)
        picked_bf = w(20480, NT * NE // 2).bitcast(BF16).rearrange("p (i e) -> p i e", i=NT)
        ones_row = w(20544, NE)
        token_id = w(20576, NT)
        expert_id = w(20608, NE)
        rstat = w(20640, 16)
        route_cur = w(20672, NT * 4).rearrange("p (i c) -> p i c", i=NT)
        slot_id = w(20992, SEQ)
        junk_out = w(8192, D)
        xT = w(0, KT * SEQ).rearrange("p (k t) -> p k t", k=KT)
        actT = w(4096, KT * SEQ).rearrange("p (k t) -> p k t", k=KT)
        yT = w(8192, KT * SEQ).rearrange("p (k t) -> p k t", k=KT)
        gf_row = w(12288, D)
        x_rows = w(14336, D)
        y_rows = w(15360, D)
        onehot = w(16384, NT * P).rearrange("p (i s) -> p i s", i=NT)
        glu = w(16896, SEQ)
        sig = w(17408, SEQ)
        lins = (w(17920, SEQ), w(13312, SEQ))
        gs = w(18432, SEQ)
        parts = [ring[:, 2 * r:2 * r + 2, :, :].rearrange("p a k c -> p (a k c)")
                 .rearrange("p (i c) -> p i c", i=NT) for r in range(TOPK)]

        pair = [ctx.enter_context(nc.psum_tensor(f"pair{i}", [P, 2, 512], F32)) for i in range(4)]
        bank = [pair[i // 2][:, i % 2, :] for i in range(8)]

        x_loaded = sems("x_loaded", NT)
        small_loaded = sem("small_loaded")
        const_loaded = sem("const_loaded")
        slot_full = sems("slot_full", RING)
        act_step = sem("act_step")
        extra_step = sem("extra_step")
        dve_step = sem("dve_step")
        x_squared = sem("x_squared")
        x_root = sem("x_root")
        head_root_ready = sem("head_root_ready")
        x2_root = sem("x2_root")
        sum_root = sem("sum_root")
        pool_passed = sem("pool_passed")
        eps_set = sem("eps_set")
        xn_ready = sem("xn_ready")
        xn_transposed = sem("xn_transposed")
        hT_by_act = sem("hT_by_act")
        hT_by_dve = sem("hT_by_dve")
        ang_ready = sem("ang_ready")
        trig_ready = sem("trig_ready")
        lam_dots = sem("lam_dots")
        lam_exp = sem("lam_exp")
        proj_ready = sem("proj_ready")
        proj_by_act = sem("proj_by_act")
        proj_by_dve = sem("proj_by_dve")
        rope_done = sem("rope_done")
        cast_done = sem("cast_done")
        qk_transposed = sem("qk_transposed")
        qk_by_act = sem("qk_by_act")
        qk_by_dve = sem("qk_by_dve")
        k_scaled = sem("k_scaled")
        silu_sig = sem("silu_sig")
        silu_done = sem("silu_done")
        scores_ready = sem("scores_ready")
        bias_ready = sem("bias_ready")
        exp_done = sem("exp_done")
        att_ready = sem("att_ready")
        att_transposed = sem("att_transposed")
        attT_ready = sem("attT_ready")
        av_ready = sem("av_ready")
        av_evicted = sem("av_evicted")
        ret_scores = sem("ret_scores")
        ret_decayed = sem("ret_decayed")
        qd_ready = sem("qd_ready")
        ret_out = sem("ret_out")
        ret_kv = sem("ret_kv")
        ret_evicted = sem("ret_evicted")
        state_ready = sem("state_ready")
        mix_gained = sem("mix_gained")
        late_loaded = sems("late_loaded", 4)
        mix_ready = sem("mix_ready")
        mix_transposed = sem("mix_transposed")
        mixT_by_act = sem("mixT_by_act")
        mixT_by_dve = sem("mixT_by_dve")
        wo_done = sem("wo_done")
        x2_ready = sem("x2_ready")
        x2_squared = sem("x2_squared")
        h2_ready = sem("h2_ready")
        h2_stored = sem("h2_stored")
        h2_transposed = sem("h2_transposed")
        h2T_by_act = sem("h2T_by_act")
        h2T_by_dve = sem("h2T_by_dve")
        logits_ready = sem("logits_ready")
        logits_read = sem("logits_read")
        max_ready = sem("max_ready")
        gate_exp = sem("gate_exp")
        picked_ready = sem("picked_ready")
        place_ready = sem("place_ready")
        place_read = sem("place_read")
        b_in_transposed = sem("b_in_transposed")
        b_in_evicted = sem("b_in_evicted")
        classes_ready = sem("classes_ready")
        gates_transposed = sem("gates_transposed")
        gateT_ready = sem("gateT_ready")
        bias_out_product = sem("bias_out_product")
        bias_out_ready = sem("bias_out_ready")
        tokens_named = sem("tokens_named")
        gf_loaded = sem("gf_loaded")
        yT_cleared = sem("yT_cleared")
        onehot_ready = sems("onehot_ready", NB)
        list_ready = sems("list_ready", NB)
        idx_ready = sems("idx_ready", NB)
        gathered = sem("gathered")
        gathered_more = sems("gathered_more", NB)
        extra_gathered = sem("extra_gathered")
        x_transposed = sems("x_transposed", NB)
        xT_by_dve = sems("xT_by_dve", NB)
        xT_by_act = sems("xT_by_act", NB)
        h_ready = sem("h_ready")
        h_read = sem("h_read")
        glu_ready = sem("glu_ready")
        sig_ready = sem("sig_ready")
        act_ready = sem("act_ready")
        y_ready = sem("y_ready")
        y_evicted = sem("y_evicted")
        rows_ready = sems("rows_ready", NB)
        rows_scaled = sems("rows_scaled", NB)
        cur_ready = sem("cur_ready")
        scattered = sem("scattered")
        scattered_more = sems("scattered_more", NB)
        extra_scattered = sem("extra_scattered")
        parts_loaded = sems("parts_loaded", TOPK)
        sum_ready = sem("sum_ready")
        sum_squared = sem("sum_squared")
        out_ready = sem("out_ready")
        out_stored = sem("out_stored")

        class Chain:
            def __init__(self, eng, semaphore):
                self.eng, self.sem, self.before, self.n = eng, semaphore, 0, 0

            def __call__(self, ins):
                ins.then_inc(self.sem, 1)
                self.n += 1

            def settle(self):
                wait(self.eng, self.sem, self.before + self.n)

        def for_all_partitions(row):
            return row.partition_broadcast(P)

        def blocks_of(c):
            return -(-WIDTHS[c] // P)

        def by_class(eng, cls, body):
            with eng.If(cls == 0):
                body(0)
            with eng.Else():
                with eng.If(cls == 1):
                    body(1)
                with eng.Else():
                    body(2)

        x_rows_dram = x.rearrange("a (i p) d -> (a i) p d", p=P)
        w_in_cols = w_in.rearrange("a (k p) c -> (a p) k c", p=P)
        w_o_cols = w_o.rearrange("a (k p) c -> (a p) k c", p=P)

        def at(row, e):
            return row[0:1, e:e + 1] if isinstance(e, int) else row[0:1, bass.ds(e, 1)]

        def of_expert(m, e):
            return m[0, e:e + 1] if isinstance(e, int) else m[0, bass.ds(e, 1)]

        def expert_chunk(e, j):
            if j < IN_CHUNKS:
                m, c = w_moe_in, j
            else:
                m, c = w_moe_out, j - IN_CHUNKS
            return of_expert(m, e).rearrange("e (k p) c -> (e p) k c", p=P)[:, :, c * CW:(c + 1) * CW]

        wo_slot = [IN_CHUNKS + q for q in range(OUT_CHUNKS)]
        LAST = NE - 1
        block = ctx.enter_context(nc.Block())

        @block.sync
        def _(sp):
            for i in range(NT):
                sp.dma_start(resid[:, i, :], x_rows_dram[i]).then_inc(x_loaded[i], 16)
            sp.dma_start(cst[:, :], consts_dram).then_inc(const_loaded, 16)
            sp.dma_start(raw_masks, masks_dram).then_inc(const_loaded, 16)
            sp.dma_start(chunk_decay[:, :], chunk_decay_dram).then_inc(const_loaded, 16)
            for c in range(NCHUNK):
                sp.dma_start(ring[:, c], w_in_cols[:, :, c * CW:(c + 1) * CW]).then_inc(slot_full[c], 16)
            for j in range(IN_CHUNKS):
                sp.wait_ge(proj_ready, NT * (j + 1))
                sp.dma_start(ring[:, j], expert_chunk(0, j)).then_inc(slot_full[j], 16)
            for q, s in enumerate(wo_slot):
                sp.wait_ge(proj_ready, NT * (s + 1))
                sp.dma_start(ring[:, s], w_o_cols[:, :, q * CW:(q + 1) * CW]).then_inc(slot_full[s], 16)
            for s in wo_slot:
                sp.wait_ge(wo_done, NT)
                sp.dma_start(ring[:, s], expert_chunk(0, s)).then_inc(slot_full[s], 16)
            with sp.Fori(1, NE) as e:
                for j in range(IN_CHUNKS):
                    sp.wait_ge(h_ready, KT * (e - 1) + j + 1)
                    sp.dma_start(ring[:, j], expert_chunk(e, j)).then_inc(slot_full[j], 16)
                for q in range(OUT_CHUNKS):
                    j = IN_CHUNKS + q
                    sp.wait_ge(y_ready, KT * (e - 1) + 2 * q + 2)
                    sp.dma_start(ring[:, j], expert_chunk(e, j)).then_inc(slot_full[j], 16)
            sp.wait_ge(h_ready, KT * NE)
            for r in range(TOPK):
                sp.wait_ge(scattered, 16 * (NE - TOPK + r + 1))
                for b in range(1, NB):
                    sp.wait_ge(scattered_more[b], NE - TOPK + r + 1)
                sp.dma_start(parts[r], y_dram.rearrange("(i p r) c -> r p i c", p=P, r=TOPK)[r])\
                    .then_inc(parts_loaded[r], 16)
            for i in range(NT):
                sp.wait_ge(out_ready, i + 1)
                sp.dma_start(out.rearrange("a (i p) d -> (a i) p d", p=P)[i], parts[0][:, i, :])\
                    .then_inc(out_stored, 16)
            sp.wait_ge(out_stored, 16 * NT)
            sp.wait_ge(h2_stored, 16 * NT)

        @block.tensor
        def _(pe):
            ident = cst[:, C_IDENT:C_IDENT + P]
            pe.wait_ge(const_loaded, 48)
            pe.wait_ge(xn_ready, NT)
            for k in range(KT):
                for i in range(NT):
                    mm = pe.transpose(bank[k][:, i * P:(i + 1) * P], xn[:, i, k * P:(k + 1) * P], ident)
                mm.then_inc(xn_transposed, 1)
            pe.wait_ge(hT_by_act, KT // 2)
            pe.wait_ge(hT_by_dve, KT // 2)
            for c in range(NCHUNK):
                pe.wait_ge(slot_full[c], 16)
                for i in range(NT):
                    u = c * NT + i
                    if u >= 4:
                        pe.wait_ge(proj_by_act if u % 2 == 0 else proj_by_dve, (u - 4) // 2 + 1)
                    for k in range(KT):
                        mm = pe.matmul(bank[u % 4][:, 0:CW], hT[:, k, i * P:(i + 1) * P], ring[:, c, k, :],
                                       start=(k == 0), stop=(k == KT - 1))
                    mm.then_inc(proj_ready, 1)
            for g in range(12):
                col = (CQ + g * P if g < 8 else CRQ + (g - 8) * P)
                if g == 0:
                    pe.wait_ge(rope_done, len(ROPE_CHUNKS))
                if g >= 4:
                    pe.wait_ge(qk_by_act if g % 2 == 0 else qk_by_dve, (g - 4) // 2 + 1)
                for i in range(NT):
                    mm = pe.transpose(bank[4 + g % 4][:, i * P:(i + 1) * P], proj[:, i, col:col + P], ident)
                mm.then_inc(qk_transposed, 1)
            pe.wait_ge(qk_by_act, 6)
            pe.wait_ge(qk_by_dve, 6)
            pe.wait_ge(proj_by_act, NCHUNK * NT // 2)
            pe.wait_ge(proj_by_dve, NCHUNK * NT // 2)
            pe.wait_ge(cast_done, 4)

            def scores(u):
                i, h = divmod(u, NH)
                if u >= 2:
                    pe.wait_ge(exp_done, 2 * (u - 1))
                for m in range(2):
                    rows = slice(64 * m, 64 * m + 64)
                    n = (i + 1) * P
                    dst = pair[u % 2][:, m, 0:n]
                    pe.matmul(dst, qkT[rows, h, i * P:(i + 1) * P], qkT[rows, 4 + h, 0:n],
                              start=True, stop=False, skip_group_check=True)
                for m in range(2):
                    mm = pe.matmul(pair[u % 2][:, m, i * P:(i + 1) * P], ident_bf[:, :], causal_bf[:, :],
                                   start=False, stop=True, skip_group_check=True)
                mm.then_inc(scores_ready, 1)

            def att_transposes(u):
                i, h = divmod(u, NH)
                pe.wait_ge(att_ready, u + 1)
                if u >= 2:
                    pe.wait_ge(attT_ready, u - 1)
                for j in range(i + 1):
                    mm = pe.transpose(bank[4 + u % 2][:, j * P:(j + 1) * P],
                                      probs[:, u % 2, 0, j * P:(j + 1) * P], ident)
                mm.then_inc(att_transposed, 1)

            def att_values(u):
                i, h = divmod(u, NH)
                pe.wait_ge(attT_ready, u + 1)
                if h == 0 and i >= 1:
                    pe.wait_ge(av_evicted, i)
                for j in range(i + 1):
                    mm = pe.matmul(bank[6][:, h * P:(h + 1) * P], attT[:, u % 2, j * P:(j + 1) * P],
                                   proj[:, j, CV + h * P:CV + (h + 1) * P], start=(j == 0), stop=(j == i))
                mm.then_inc(av_ready, 1)

            NU = NT * NH
            for s in range(NU + 3):
                if s < NU:
                    scores(s)
                if 2 <= s < NU + 2:
                    att_transposes(s - 2)
                if s >= 3:
                    att_values(s - 3)

            def ret_score(i):
                if i >= 2:
                    pe.wait_ge(state_ready, 2 * (i - 1))
                for h in range(NH):
                    rows = slice(64 * (h % 2), 64 * (h % 2) + 64)
                    mm = pe.matmul(pair[i % 2][:, h % 2, (h // 2) * P:(h // 2 + 1) * P],
                                   qkT[rows, 10 + h // 2, i * P:(i + 1) * P],
                                   qkT[rows, 8 + h // 2, i * P:(i + 1) * P], start=True, stop=True)
                mm.then_inc(ret_scores, 1)

            def ret_output(i):
                pe.wait_ge(ret_decayed, i + 1)
                if i >= 2:
                    pe.wait_ge(ret_evicted, i - 1)
                if i >= 1:
                    pe.wait_ge(state_ready, 2 * i)
                    pe.wait_ge(qd_ready, 2)
                for h in range(NH):
                    rows = slice(64 * (h % 2), 64 * (h % 2) + 64)
                    dst = pair[2 + i % 2][:, h % 2, (h // 2) * P:(h // 2 + 1) * P]
                    if i >= 1:
                        pe.matmul(dst, qdT[rows, h // 2, i * P:(i + 1) * P], state[rows, h // 2, :],
                                  start=True, stop=False)
                    mm = pe.matmul(dst, st_s[:, i % 2, h % 2, h // 2, :],
                                   proj[:, i, CRV + h * P:CRV + (h + 1) * P], start=(i == 0), stop=True)
                mm.then_inc(ret_out, 1)
                if i < NT - 1:
                    if i == 0:
                        pe.wait_ge(k_scaled, NT)
                    for h in range(NH):
                        rows = slice(64 * (h % 2), 64 * (h % 2) + 64)
                        mm = pe.matmul(pair[i % 2][rows, 0, 256 + (h // 2) * P:256 + (h // 2 + 1) * P],
                                       proj[:, i, CRK + h * DQ:CRK + (h + 1) * DQ],
                                       proj[:, i, CRV + h * P:CRV + (h + 1) * P], start=True, stop=True)
                    mm.then_inc(ret_kv, 1)

            pe.wait_ge(exp_done, 2 * NU)
            pe.wait_ge(attT_ready, NU)
            pe.wait_ge(av_evicted, NT)
            ret_score(0)
            for i in range(NT):
                if i + 1 < NT:
                    ret_score(i + 1)
                ret_output(i)

            def mix_product(i):
                pe.wait_ge(mix_ready, i + 1)
                for k in range(KT):
                    if k == 4:
                        mm.then_inc(mix_transposed, 1)
                    mm = pe.transpose(bank[k // 4][:, (k % 4) * P:(k % 4 + 1) * P],
                                      mix[:, i, k * P:(k + 1) * P], ident)
                mm.then_inc(mix_transposed, 1)
                pe.wait_ge(mixT_by_act, i + 1)
                pe.wait_ge(mixT_by_dve, i + 1)
                if i >= 2:
                    pe.wait_ge(x2_ready, 2 * (i - 1))
                for q, s in enumerate(wo_slot):
                    if i == 0:
                        pe.wait_ge(slot_full[s], 32)
                    dst = pair[1 + i % 2][:, q // 2, (q % 2) * CW:(q % 2 + 1) * CW]
                    for k in range(KT):
                        mm = pe.matmul(dst, mixT[:, i % 2, k, :], ring[:, s, k, :],
                                       start=(k == 0), stop=(k == KT - 1))
                mm.then_inc(wo_done, 1)

            def router(i):
                pe.wait_ge(h2_ready, i + 1)
                if i >= 1:
                    pe.wait_ge(logits_read, i)
                    pe.wait_ge(place_read, i)
                for k in range(KT):
                    if k == 4:
                        mm.then_inc(h2_transposed, 1)
                    mm = pe.transpose(bank[6 + k // 4][:, (k % 4) * P:(k % 4 + 1) * P],
                                      h2_row[:, i, k * P:(k + 1) * P], ident)
                mm.then_inc(h2_transposed, 1)
                pe.wait_ge(h2T_by_act, i + 1)
                pe.wait_ge(h2T_by_dve, i + 1)
                if i == 0:
                    pe.wait_ge(late_loaded[1], 16)
                for k in range(KT):
                    mm = pe.matmul(bank[6][:, 0:NE], mixT[:, i % 2, k, :], w_router_sb[:, k, :],
                                   start=(k == 0), stop=(k == KT - 1))
                mm.then_inc(logits_ready, 1)

            def places(i):
                pe.wait_ge(picked_ready, i + 1)
                for j in range(i + 1):
                    mm = pe.matmul(bank[7][:, 0:NE], (utri_bf if j == i else ones_bf)[:, :], picked_bf[:, j, :],
                                   start=(j == 0), stop=(j == i))
                mm.then_inc(place_ready, 1)

            mix_product(0)
            mix_product(1)
            for i in range(NT):
                router(i)
                if i + 2 < NT:
                    mix_product(i + 2)
                places(i)
            pe.wait_ge(place_read, NT)
            for j in range(NT):
                mm = pe.matmul(bank[7][:, 64:64 + NE], ones_bf[:, :], picked_bf[:, j, :],
                               start=(j == 0), stop=(j == NT - 1))
            mm.then_inc(place_ready, 1)

            def token_list(x_e, b):
                wait(pe, onehot_ready[b], x_e + 1)
                for i in range(NT):
                    mm = pe.matmul(bank[6][:, b * 4:b * 4 + 4], onehot[:, i, :], route_cur[:, i, :],
                                   start=(i == 0), stop=(i == NT - 1))
                mm.then_inc(list_ready[b], 1)

            def x_transposes(x_e, b):
                if b == 0:
                    pe.wait_ge(gathered, 16 * (x_e + 1))
                else:
                    pe.wait_ge(gathered_more[b], x_e + 1)
                    pe.wait_ge(xT_by_dve[b - 1], x_e + 1)
                    pe.wait_ge(xT_by_act[b - 1], x_e + 1)
                for k in range(KT):
                    mm = pe.transpose(bank[k // 4][:, (k % 4) * P:(k % 4 + 1) * P],
                                      x_rows[:, k * P:(k + 1) * P], ident)
                mm.then_inc(x_transposed[b], 1)

            def more_blocks(x_e, c):
                for b in range(1, NB):
                    if b < blocks_of(c):
                        token_list(x_e, b)
                        x_transposes(x_e, b)
                    else:
                        pe.sem_inc(list_ready[b], 1)
                        pe.sem_inc(x_transposed[b], 1)

            pe.wait_ge(late_loaded[2], 16)
            pe.wait_ge(x2_ready, 2 * NT)
            for m in range(KT):
                for c in range(2):
                    mm = pe.transpose(bank[2][:, (2 * m + c) * NE:(2 * m + c + 1) * NE],
                                      b_in_rows[:, m * CW + c:(m + 1) * CW:2], ident[0:NE, 0:NE])
            mm.then_inc(b_in_transposed, 1)
            token_list(0, 0)
            for i in range(NT):
                mm = pe.transpose(bank[3][0:NE, i * P:(i + 1) * P], gates[:, i, :], ident)
            mm.then_inc(gates_transposed, 1)
            pe.wait_ge(gateT_ready, 1)
            pe.wait_ge(late_loaded[3], 16)
            for i in range(NT):
                for f in range(2):
                    n = 2 * i + f
                    if n >= 2:
                        pe.wait_ge(bias_out_ready, n - 1)
                    pe.matmul(bank[4 + n % 2], gateT[:, i * P:(i + 1) * P], b_out_rows[:, f * 512:(f + 1) * 512],
                              start=True, stop=True).then_inc(bias_out_product, 1)
            x_transposes(0, 0)
            pe.wait_ge(classes_ready, 2)
            first = pe.value_load(at(classes, 0), min_val=0, max_val=2)
            by_class(pe, first, lambda c: more_blocks(0, c))

            def product_in(e, width):
                for m in range(KT):
                    pe.wait_ge(slot_full[m], 16 * (e + 2))
                    if m >= 2:
                        pe.wait_ge(h_read, KT * e + m - 1)
                    for c in range(2):
                        for k in range(KT):
                            mm = pe.matmul(pair[m % 2][:, c, 0:width], ring[:, m, k, c:CW:2],
                                           xT[:, k, 0:width], start=(k == 0), stop=(k == KT - 1))
                    mm.then_inc(h_ready, 1)

            def product_out(e, width):
                for t in range(KT):
                    s = IN_CHUNKS + t // 2
                    if t % 2 == 0:
                        pe.wait_ge(slot_full[s], 16 * (e + 3))
                    if t >= 2:
                        pe.wait_ge(y_evicted, KT * e + t - 1)
                    for k in range(KT):
                        if t == 0:
                            pe.wait_ge(act_ready, KT * e + k + 1)
                        mm = pe.matmul(bank[4 + t % 2][:, 0:width], ring[:, s, k, (t % 2) * P:(t % 2 + 1) * P],
                                       actT[:, k, 0:width], start=(k == 0), stop=(k == KT - 1))
                    mm.then_inc(y_ready, 1)

            def y_transposes(e, b):
                if b:
                    pe.wait_ge(rows_scaled[b - 1], e + 1)
                for t in range(KT):
                    mm = pe.transpose(bank[6 + t // 4][:, (t % 4) * P:(t % 4 + 1) * P],
                                      yT[:, t, b * P:(b + 1) * P], ident)
                mm.then_inc(rows_ready[b], 1)

            def more_rows(e, c):
                for b in range(1, NB):
                    if b < blocks_of(c):
                        y_transposes(e, b)
                    else:
                        pe.sem_inc(rows_ready[b], 1)

            pe.wait_ge(yT_cleared, 1)
            pe.wait_ge(b_in_evicted, 1)
            pe.wait_ge(bias_out_ready, 2 * NT)

            def expert(e, last):
                cur = pe.value_load(at(classes, e), min_val=0, max_val=2)
                for b in range(NB):
                    pe.wait_ge(xT_by_dve[b], e + 1)
                    pe.wait_ge(xT_by_act[b], e + 1)
                by_class(pe, cur, lambda c: product_in(e, WIDTHS[c]))
                if not last:
                    for b in range(NB):
                        wait(pe, rows_scaled[b], e)
                    token_list(e + 1, 0)
                by_class(pe, cur, lambda c: product_out(e, WIDTHS[c]))
                if not last:
                    nxt = pe.value_load(at(classes, e + 1), min_val=0, max_val=2)
                    x_transposes(e + 1, 0)
                    by_class(pe, nxt, lambda c: more_blocks(e + 1, c))
                    for b in range(NB):
                        pe.wait_ge(idx_ready[b], e + 2)
                else:
                    for b in range(NB):
                        wait(pe, rows_scaled[b], e)
                pe.wait_ge(y_evicted, KT * (e + 1))
                y_transposes(e, 0)
                by_class(pe, cur, lambda c: more_rows(e, c))

            expert(0, False)
            with pe.Fori(1, LAST) as e:
                expert(e, False)
            expert(LAST, True)

        @block.scalar
        def _(act):
            small = [(pos_i[:, :], positions.rearrange("a (i p) -> (a p) i", p=P)),
                     (g1_col[:, :], norm1_g.rearrange("a (k p) -> (a p) k", p=P))]
            for n, row in enumerate((lambda_q1, lambda_k1, lambda_q2, lambda_k2)):
                small.append((lam_rows[:, n, :], for_all_partitions(row[0])))
            for h in range(NH):
                small.append((gain_row[:, h * P:(h + 1) * P], for_all_partitions(diff_norm_g[0])))
            small.append((gain_row[:, 512:D], for_all_partitions(ret_norm_g.rearrange("a h c -> (a h c)"))))
            small.append((b_router_row[:, :], for_all_partitions(b_router[0])))
            assert len(small) == N_SMALL
            with nc.allow_non_contiguous_dma(reason="a few hundred words"):
                for dst, src in small:
                    act.dma_start(dst, src).then_inc(small_loaded, 16)
            def root(at, n, mean_of, ready):
                act.activation(stat[:, at:at + n], stat[:, at:at + n], ACT.Sqrt, bias=eps_col[:, 0:1],
                               scale=1.0 / mean_of).then_inc(ready, 1)

            for i in range(NT):
                act.wait_ge(x_loaded[i], 16)
                act.activation(junk1[:, i, :], resid[:, i, :], ACT.Square, accum_out=stat[:, i:i + 1]).then_inc(x_squared, 1)
            act.wait_ge(x_squared, NT)
            act.wait_ge(eps_set, 1)
            root(0, NT, D, x_root)
            act.wait_ge(small_loaded, 16 * N_SMALL)
            for k in range(0, KT, 2):
                act.wait_ge(xn_transposed, k + 1)
                act.activation(hT[:, k, :], bank[k], ACT.Copy, scale=g1_col[:, k:k + 1]).then_inc(hT_by_act, 1)
            act.wait_ge(ang_ready, 2)
            act.activation(cos_sin[:, 0], ang[:, 5], ACT.Sin).then_inc(trig_ready, 1)
            act.activation(cos_sin[:, 1], ang[:, 3], ACT.Sin).then_inc(trig_ready, 1)
            act.wait_ge(lam_dots, 1)
            act.activation(lam[:, 2:4], lam[:, 0:2], ACT.Exp).then_inc(lam_exp, 1)
            for c in range(NCHUNK):
                for i in range(0, NT, 2):
                    u = c * NT + i
                    act.wait_ge(proj_ready, u + 1)
                    act.copy(proj[:, i, c * CW:(c + 1) * CW], bank[u % 4][:, 0:CW]).then_inc(proj_by_act, 1)
            for g in range(0, 12, 2):
                act.wait_ge(qk_transposed, g + 1)
                act.copy(qkT[:, g, :], bank[4 + g % 4]).then_inc(qk_by_act, 1)
            act.wait_ge(qk_transposed, 12)
            act.wait_ge(proj_by_act, NCHUNK * NT // 2)
            act.wait_ge(proj_by_dve, NCHUNK * NT // 2)
            for i in range(NT):
                act.activation(mix[:, i, 512:D], proj[:, i, CRG:PROJ], ACT.Sigmoid).then_inc(silu_sig, 1)

            def head_squares(outputs, i, first_head):
                chain.settle()
                for h in range(NH):
                    col = 16 + 2 * NH * i + first_head + h
                    chain(act.activation(square_tmp[:, h, :], outputs[h], ACT.Square,
                                         accum_out=stat[:, col:col + 1]))

            chain = Chain(act, act_step)

            def exponentials(u):
                i, b, n = u // NH, u % 2, (u // NH + 1) * P
                act.wait_ge(bias_ready, u + 1)
                if u >= 2:
                    act.wait_ge(att_transposed, u - 1)
                for m in range(2):
                    act.activation(probs[:, b, m, 0:n], pair[b][:, m, 0:n], ACT.Exp, bias=row_bias[:, b, m:m + 1],
                                   scale=SCALE, accum_out=row_sum[:, b, m:m + 1]).then_inc(exp_done, 1)

            NU = NT * NH
            for s in range(NU + 3):
                if s < NU:
                    exponentials(s)
                if 2 <= s < NU + 2:
                    u = s - 2
                    n = (u // NH + 1) * P
                    act.wait_ge(att_transposed, u + 1)
                    if u >= 2:
                        act.wait_ge(av_ready, u - 1)
                    act.copy(attT[:, u % 2, 0:n], bank[4 + u % 2][:, 0:n]).then_inc(attT_ready, 1)
                if s >= 3 and (s - 3) % NH == NH - 1:
                    i = (s - 3) // NH
                    act.wait_ge(av_ready, s - 2)
                    head_squares([bank[6][:, h * P:(h + 1) * P] for h in range(NH)], i, 0)
                    act.copy(mix[:, i, 0:512], bank[6]).then_inc(av_evicted, 1)
            act.wait_ge(silu_done, 2 * NT)
            for i in range(NT):
                act.wait_ge(ret_out, i + 1)
                outputs = pair[2 + i % 2][:, :, 0:256].rearrange("p r (a c) -> p a r c", a=2)
                head_squares([outputs[:, h // 2, h % 2, :] for h in range(NH)], i, NH)
                act.copy(mix[:, i, 512:D].rearrange("p (a r c) -> p a r c", a=2, r=2), outputs).then_inc(ret_evicted, 1)

            act.wait_ge(ret_evicted, NT)
            chain.settle()
            root(16, 2 * NH * NT, P, head_root_ready)

            def mix_evict(i):
                act.wait_ge(mix_transposed, 2 * i + 1)
                act.copy(mixT[:, i % 2, 0:4, :], bank[0].rearrange("p (k t) -> p k t", k=4)).then_inc(mixT_by_act, 1)

            mix_evict(0)
            mix_evict(1)
            for i in range(NT):
                act.wait_ge(x2_ready, 2 * (i + 1))
                act.activation(junk2, resid[:, i, :], ACT.Square, accum_out=stat[:, 48 + i:49 + i]).then_inc(x2_squared, 1)
                act.wait_ge(x2_squared, i + 1)
                root(48 + i, 1, D, x2_root)
                act.wait_ge(h2_ready, i + 1)
                act.dma_start(h2_dram[i * P:(i + 1) * P, :], h2_row[:, i, :]).then_inc(h2_stored, 16)
                act.wait_ge(h2_transposed, 2 * i + 1)
                act.copy(mixT[:, i % 2, 0:4, :], bank[6].rearrange("p (k t) -> p k t", k=4)).then_inc(h2T_by_act, 1)
                act.wait_ge(max_ready, i + 1)
                act.activation(expo, logits, ACT.Exp, bias=rstat[:, 0:1]).then_inc(gate_exp, 1)
                if i + 2 < NT:
                    mix_evict(i + 2)
            act.wait_ge(b_in_transposed, 1)
            act.copy(bias_in.rearrange("p e c -> p c e"), bank[2].rearrange("p (c e) -> p c e", e=NE)).then_inc(b_in_evicted, 1)

            def xT_evict(x_e, b):
                act.wait_ge(x_transposed[b], x_e + 1)
                act.copy(xT[:, 4:8, b * P:(b + 1) * P], bank[1].rearrange("p (k t) -> p k t", k=4)).then_inc(xT_by_act[b], 1)

            def more_blocks(x_e, c):
                for b in range(1, NB):
                    if b < blocks_of(c):
                        xT_evict(x_e, b)
                    else:
                        act.sem_inc(xT_by_act[b], 1)

            def sigmoids(e, c):
                width = WIDTHS[c]
                for m in range(KT):
                    act.wait_ge(glu_ready, KT * e + m + 1)
                    act.activation(sig[:, 0:width], glu[:, 0:width], ACT.Sigmoid, scale=SWI_ALPHA).then_inc(sig_ready, 1)

            def y_evicts(e, c):
                width = WIDTHS[c]
                for t in range(KT):
                    act.wait_ge(y_ready, KT * e + t + 1)
                    act.copy(yT[:, t, 0:width], bank[4 + t % 2][:, 0:width]).then_inc(y_evicted, 1)

            def scale_rows(e, b):
                act.wait_ge(rows_ready[b], e + 1)
                if b == 1:
                    act.wait_ge(scattered, 16 * (e + 1))
                elif b:
                    act.wait_ge(scattered_more[b - 1], e + 1)
                act.activation(y_rows[:, 0:512], bank[6], ACT.Copy, scale=gate_cur[:, b:b + 1])
                act.activation(y_rows[:, 512:D], bank[7], ACT.Copy, scale=gate_cur[:, b:b + 1]).then_inc(rows_scaled[b], 1)

            def more_rows(e, c):
                for b in range(1, NB):
                    if b < blocks_of(c):
                        scale_rows(e, b)
                    else:
                        act.sem_inc(rows_scaled[b], 1)

            def expert(e, last):
                cur = act.value_load(at(classes, e), min_val=0, max_val=2)
                by_class(act, cur, lambda c: sigmoids(e, c))
                by_class(act, cur, lambda c: y_evicts(e, c))
                if not last:
                    nxt = act.value_load(at(classes, e + 1), min_val=0, max_val=2)
                    xT_evict(e + 1, 0)
                    by_class(act, nxt, lambda c: more_blocks(e + 1, c))
                act.wait_ge(cur_ready, e + 1)
                scale_rows(e, 0)
                by_class(act, cur, lambda c: more_rows(e, c))

            act.wait_ge(classes_ready, 2)
            first = act.value_load(at(classes, 0), min_val=0, max_val=2)
            xT_evict(0, 0)
            by_class(act, first, lambda c: more_blocks(0, c))
            act.wait_ge(yT_cleared, 1)
            expert(0, False)
            with act.Fori(1, LAST) as e:
                expert(e, False)
            expert(LAST, True)
            for i in range(NT):
                act.wait_ge(sum_ready, TOPK * NT - NT + i + 1)
                act.activation(junk_out, resid[:, i, :], ACT.Square, accum_out=stat[:, 52 + i:53 + i]).then_inc(sum_squared, 1)
                act.wait_ge(sum_squared, i + 1)
                root(52 + i, 1, D, sum_root)

        @block.vector
        def _(dve):
            chain = Chain(dve, dve_step)

            dve.memset(eps_col[:, :], EPS).then_inc(eps_set, 1)
            dve.wait_ge(x_root, 1)
            chain(dve.reciprocal(stat[:, 0:NT], stat[:, 0:NT]))
            chain.settle()
            for i in range(NT):
                dve.tensor_scalar(xn[:, i, :], resid[:, i, :], stat[:, i:i + 1], None, ALU.mult).then_inc(xn_ready, 1)
            dve.wait_ge(small_loaded, 16 * N_SMALL)
            dve.wait_ge(const_loaded, 48)
            chain(dve.tensor_copy(pos_f[:, :], pos_i[:, :]))
            chain.settle()
            for i in range(NT):
                chain(dve.tensor_scalar(ang[:, 0, i, :], cst[:, C_FREQ:C_FREQ + 32], pos_f[:, i:i + 1], None, ALU.mult))
            chain.settle()
            chain(dve.tensor_scalar(ang[:, 1], ang[:, 0], 1.0 / (2 * math.pi), MAGIC, ALU.mult, ALU.add))
            chain.settle()
            chain(dve.tensor_scalar(ang[:, 2], ang[:, 1], -MAGIC, None, ALU.add))
            chain.settle()
            chain(dve.scalar_tensor_tensor(ang[:, 3], ang[:, 2], -TWO_PI_A, ang[:, 0], ALU.mult, ALU.add))
            chain.settle()
            chain(dve.scalar_tensor_tensor(ang[:, 4], ang[:, 2], -TWO_PI_B, ang[:, 3], ALU.mult, ALU.add))
            chain.settle()
            chain(dve.scalar_tensor_tensor(ang[:, 1], ang[:, 2], -TWO_PI_C, ang[:, 4], ALU.mult, ALU.add))
            chain.settle()
            dve.tensor_scalar(ang[:, 3], ang[:, 1], PI_F, -PI_F, ALU.min, ALU.max).then_inc(ang_ready, 1)
            dve.wait_ge(ang_ready, 1)
            chain(dve.scalar_tensor_tensor(ang[:, 4], ang[:, 3], -1.0, ang[:, 3], ALU.mult, ALU.max))
            chain.settle()
            dve.tensor_scalar(ang[:, 5], ang[:, 4], -1.0, math.pi / 2, ALU.mult, ALU.add).then_inc(ang_ready, 1)
            for k in range(1, KT, 2):
                dve.wait_ge(xn_transposed, k + 1)
                dve.tensor_scalar(hT[:, k, :], bank[k], g1_col[:, k:k + 1], None, ALU.mult).then_inc(hT_by_dve, 1)
            chain(dve.tensor_tensor(lam_rows[:, 0::2], lam_rows[:, 0::2], lam_rows[:, 1::2], ALU.mult))
            chain.settle()
            dve.tensor_reduce(lam[:, 0:2], lam_rows[:, 0::2], AX_X, ALU.add).then_inc(lam_dots, 1)
            dve.tensor_copy(ident_bf[:, :], cst[:, C_IDENT:C_IDENT + P]).then_inc(cast_done, 1)
            dve.tensor_copy(causal_bf[:, :], raw_masks[:, 0:P]).then_inc(cast_done, 1)
            dve.tensor_copy(utri_bf[:, :], raw_masks[:, P:2 * P]).then_inc(cast_done, 1)
            dve.memset(ones_bf[:, :], 1.0).then_inc(cast_done, 1)
            dve.wait_ge(lam_exp, 1)
            chain(dve.tensor_tensor(lam[:, 4:5], lam[:, 3:4], lam[:, 2:3], ALU.subtract))
            chain.settle()
            chain(dve.tensor_scalar(lam[:, 5:6], lam[:, 4:5], -LAM_INIT, None, ALU.add))
            chain.settle()

            def rotary(c):
                cols = proj[:, :, c * CW:(c + 1) * CW].rearrange("p i (g a f) -> p i g a f", g=4, a=2)
                halves = [cols[:, :, :, a, :] for a in range(2)]
                cos, sin = (cos_sin[:, n].unsqueeze(2).to_broadcast([P, NT, 4, 32]) for n in range(2))
                dve.wait_ge(proj_by_act, 2 * (c + 1))
                dve.wait_ge(proj_by_dve, 2 * (c + 1))
                dve.wait_ge(trig_ready, 2)
                for n, (half, trig) in enumerate(((0, cos), (1, sin), (1, cos), (0, sin))):
                    chain(dve.tensor_tensor(rope_tmp[:, n], halves[half], trig, ALU.mult))
                chain.settle()
                chain(dve.tensor_tensor(halves[0], rope_tmp[:, 0], rope_tmp[:, 1], ALU.subtract))
                dve.tensor_tensor(halves[1], rope_tmp[:, 2], rope_tmp[:, 3], ALU.add).then_inc(rope_done, 1)
                chain.settle()

            for c in range(NCHUNK):
                for i in range(1, NT, 2):
                    u = c * NT + i
                    dve.wait_ge(proj_ready, u + 1)
                    dve.tensor_copy(proj[:, i, c * CW:(c + 1) * CW], bank[u % 4][:, 0:CW]).then_inc(proj_by_dve, 1)
                if c in ROPE_CHUNKS:
                    rotary(c)
            for g in range(1, 12, 2):
                dve.wait_ge(qk_transposed, g + 1)
                dve.tensor_copy(qkT[:, g, :], bank[4 + g % 4]).then_inc(qk_by_dve, 1)

            def maxima(u):
                b, n = u % 2, (u // NH + 1) * P
                dve.wait_ge(scores_ready, u + 1)
                chain(dve.tensor_reduce(row_max[:, b, :], pair[b][:, :, 0:n], AX_X, ALU.max))
                chain.settle()
                if u >= 2:
                    dve.wait_ge(exp_done, 2 * (u - 1))
                dve.tensor_scalar(row_bias[:, b, :], row_max[:, b, :], -SCALE, None, ALU.mult).then_inc(bias_ready, 1)

            def difference(u):
                b, n = u % 2, (u // NH + 1) * P
                dve.wait_ge(exp_done, 2 * (u + 1))
                chain(dve.reciprocal(row_rec[:, b, :], row_sum[:, b, :]))
                chain.settle()
                chain(dve.tensor_tensor(row_rec[:, b, 1:2], row_rec[:, b, 1:2], lam[:, 5:6], ALU.mult))
                chain.settle()
                chain(dve.tensor_scalar(probs[:, b, 1, 0:n], probs[:, b, 1, 0:n], row_rec[:, b, 1:2], None, ALU.mult))
                chain.settle()
                dve.scalar_tensor_tensor(probs[:, b, 0, 0:n], probs[:, b, 0, 0:n], row_rec[:, b, 0:1],
                                         probs[:, b, 1, 0:n], ALU.mult, ALU.add).then_inc(att_ready, 1)

            NU = NT * NH
            for s in range(NU + 1):
                if s < NU:
                    maxima(s)
                if s >= 1:
                    difference(s - 1)
            dve.wait_ge(av_ready, NU)
            for a in range(2):
                dve.tensor_tensor(qdT[:, a, :].rearrange("p (i t) -> p i t", i=NT),
                                  qkT[:, 8 + a, :].rearrange("p (i t) -> p i t", i=NT),
                                  cst[:, C_QDEC + a * P:C_QDEC + (a + 1) * P].unsqueeze(1).to_broadcast([P, NT, P]),
                                  ALU.mult).then_inc(qd_ready, 1)
            for i in range(NT):
                dve.wait_ge(ret_scores, i + 1)
                if i >= 2:
                    dve.wait_ge(ret_out, i - 1)
                dve.tensor_tensor(st_s[:, i % 2].rearrange("p r a n -> p r (a n)"), pair[i % 2][:, :, 0:256],
                                  cst[:, C_DECAY:C_DECAY + 512].rearrange("p (r n) -> p r n", r=2), ALU.mult)\
                    .then_inc(ret_decayed, 1)
                if i >= 1:
                    j = i - 1
                    dve.wait_ge(ret_kv, j + 1)
                    for a in range(2):
                        kv = pair[j % 2][:, 0, 256 + a * P:256 + (a + 1) * P]
                        if j == 0:
                            dve.tensor_copy(state[:, a, :], kv).then_inc(state_ready, 1)
                        else:
                            dve.wait_ge(state_ready, 2 * j)
                            dve.scalar_tensor_tensor(state[:, a, :], state[:, a, :], chunk_decay[:, a:a + 1], kv,
                                                     ALU.mult, ALU.add).then_inc(state_ready, 1)
            dve.wait_ge(mix_gained, 2 * NT)
            dve.wait_ge(head_root_ready, 1)
            chain(dve.reciprocal(stat[:, 16:48], stat[:, 16:48]))
            chain.settle()
            head_root = stat[:, 16:48].rearrange("p (i h) -> p i h", i=NT)
            chain(dve.tensor_scalar(head_root[:, :, 0:NH], head_root[:, :, 0:NH], 1.0 - LAM_INIT, None, ALU.mult))
            chain.settle()

            def mix_norm(i):
                m = mix[:, i, :].rearrange("p (h c) -> p h c", h=2 * NH)
                dve.tensor_tensor(m, m, head_root[:, i, :].unsqueeze(2).to_broadcast([P, 2 * NH, P]), ALU.mult)\
                    .then_inc(mix_ready, 1)

            def mix_evict(i):
                dve.wait_ge(mix_transposed, 2 * i + 2)
                dve.tensor_copy(mixT[:, i % 2, 4:8, :], bank[1].rearrange("p (k t) -> p k t", k=4)).then_inc(mixT_by_dve, 1)

            for i in range(NT):
                mix_norm(i)
            mix_evict(0)
            mix_evict(1)
            dve.wait_ge(tokens_named, 4)
            for i in range(NT):
                dve.wait_ge(wo_done, i + 1)
                for f in range(2):
                    half = resid[:, i, f * 512:(f + 1) * 512]
                    dve.tensor_tensor(half, half, pair[1 + i % 2][:, f, :], ALU.add).then_inc(x2_ready, 1)
                dve.wait_ge(x2_root, i + 1)
                chain(dve.reciprocal(stat[:, 48 + i:49 + i], stat[:, 48 + i:49 + i]))
                chain.settle()
                if i == 0:
                    dve.wait_ge(late_loaded[0], 16)
                dve.scalar_tensor_tensor(h2_row[:, i, :].rearrange("p (a c) -> p a c", a=NT),
                                         resid[:, i, :].rearrange("p (a c) -> p a c", a=NT),
                                         stat[:, 48 + i:49 + i], g2_row, ALU.mult, ALU.mult).then_inc(h2_ready, 1)
                dve.wait_ge(h2_transposed, 2 * i + 2)
                dve.tensor_copy(mixT[:, i % 2, 4:8, :], bank[7].rearrange("p (k t) -> p k t", k=4)).then_inc(h2T_by_dve, 1)
                dve.wait_ge(logits_ready, i + 1)
                if i:
                    dve.wait_ge(gate_exp, i)
                dve.tensor_tensor(logits, bank[6][:, 0:NE], b_router_row[:, :], ALU.add).then_inc(logits_read, 1)
                dve.wait_ge(logits_read, i + 1)
                chain(dve.max(top8, logits))
                chain.settle()
                dve.tensor_scalar(rstat[:, 0:1], top8[:, 0:1], -1.0, None, ALU.mult).then_inc(max_ready, 1)
                if i + 2 < NT:
                    mix_evict(i + 2)
                chain(dve.max_index(top8_i, top8, logits))
                chain.settle()
                chain(dve.tensor_copy(top8_f, top8_i))
                chain.settle()
                for k in range(TOPK):
                    if k == 0:
                        chain(dve.tensor_scalar(picked[:, i, :], expert_id, top8_f[:, 0:1], None, ALU.is_equal))
                    else:
                        chain(dve.scalar_tensor_tensor(picked[:, i, :], expert_id, top8_f[:, k:k + 1], picked[:, i, :],
                                                       ALU.is_equal, ALU.add))
                    chain.settle()
                dve.tensor_copy(picked_bf[:, i, :], picked[:, i, :]).then_inc(picked_ready, 1)
                dve.wait_ge(gate_exp, i + 1)
                chain(dve.tensor_tensor(gates[:, i, :], expo, picked[:, i, :], ALU.mult))
                chain(dve.tensor_tensor_scan(rank, ones_row, picked[:, i, :], 0.0, ALU.mult, ALU.add))
                chain.settle()
                chain(dve.tensor_reduce(rstat[:, 1:2], gates[:, i, :], AX_X, ALU.add))
                chain(dve.tensor_tensor(rank, rank, picked[:, i, :], ALU.subtract))
                chain.settle()
                chain(dve.reciprocal(rstat[:, 2:3], rstat[:, 1:2]))
                chain(dve.tensor_scalar(route[:, i, :, 0], rank, token_id[:, i:i + 1], -NOWHERE, ALU.add, ALU.add))
                chain(dve.tensor_scalar(route[:, i, :, 1], ones_row, token_id[:, i:i + 1], 1.0 / TOPK, ALU.mult, ALU.mult))
                chain(dve.tensor_scalar(route[:, i, :, 3], ones_row, 0.0, None, ALU.mult))
                chain.settle()
                chain(dve.tensor_scalar(gates[:, i, :], gates[:, i, :], rstat[:, 2:3], None, ALU.mult))
                chain.settle()
                chain(dve.tensor_copy(route[:, i, :, 2], gates[:, i, :]))
                dve.wait_ge(place_ready, i + 1)
                dve.scalar_tensor_tensor(slot_of[:, i, :], bank[7][:, 0:NE], 1.0, picked[:, i, :], ALU.add, ALU.mult)\
                    .then_inc(place_read, 1)
                dve.wait_ge(place_read, i + 1)
                chain(dve.tensor_scalar(slot_of[:, i, :], slot_of[:, i, :], -1.0, None, ALU.add))
                chain.settle()
            dve.wait_ge(place_ready, NT + 1)
            chain(dve.tensor_copy(counts[:, 0:NE], bank[7][0:1, 64:64 + NE]))
            chain.settle()
            chain(dve.tensor_scalar(counts[:, NE:2 * NE], counts[:, 0:NE], float(WIDTHS[0]), None, ALU.is_gt))
            chain.settle()
            dve.scalar_tensor_tensor(classes[:, :], counts[:, 0:NE], float(WIDTHS[1]), counts[:, NE:2 * NE],
                                     ALU.is_gt, ALU.add).then_inc(classes_ready, 1)
            chain(dve.tensor_scalar(counts[:, 0:NE], counts[:, 0:NE], float(WIDTHS[1]), float(NB - 2), ALU.is_gt, ALU.mult))
            chain.settle()
            chain(dve.tensor_tensor(counts[:, 0:NE], counts[:, 0:NE], counts[:, NE:2 * NE], ALU.add))
            chain.settle()
            chain(dve.tensor_tensor_scan(counts[:, NE:2 * NE], ones_row[0:1, :], counts[:, 0:NE], 0.0, ALU.mult, ALU.add))
            chain.settle()
            dve.tensor_tensor(extras_before[:, :], counts[:, NE:2 * NE], counts[:, 0:NE], ALU.subtract)\
                .then_inc(classes_ready, 1)

            def of(ap, e):
                return ap[:, :, e:e + 1] if isinstance(e, int) else ap[:, :, bass.ds(e, 1)]

            def slots_one_hot(x_e, b):
                if b:
                    dve.wait_ge(list_ready[b - 1], x_e + 1)
                for i in range(NT):
                    ins = dve.tensor_scalar(onehot[:, i, :], slot_id[:, b * P:(b + 1) * P], pos_cur[:, i:i + 1], None,
                                            ALU.is_equal)
                    if i < NT - 1:
                        chain(ins)
                ins.then_inc(onehot_ready[b], 1)

            def next_expert(x_e):
                chain(dve.tensor_copy(pos_cur[:, :].unsqueeze(2), of(slot_of, x_e)))
                chain(dve.tensor_copy(route_cur.unsqueeze(2), of(route, x_e)))
                chain.settle()
                slots_one_hot(x_e, 0)

            def read_list(x_e, b):
                dve.wait_ge(list_ready[b], x_e + 1)
                record = bank[6][:, b * 4:b * 4 + 4]
                chain(dve.tensor_scalar(dest_next[:, b:b + 1], record[:, 0:1], NOWHERE, None, ALU.add))
                chain(dve.tensor_copy(gate_next[:, b:b + 1], record[:, 2:3]))
                dve.tensor_copy(token_next[:, b:b + 1], record[:, 1:2]).then_inc(idx_ready[b], 1)

            def xT_evict(x_e, b):
                dve.wait_ge(x_transposed[b], x_e + 1)
                dve.tensor_copy(xT[:, 0:4, b * P:(b + 1) * P], bank[0].rearrange("p (k t) -> p k t", k=4))\
                    .then_inc(xT_by_dve[b], 1)

            def more_blocks(x_e, c):
                nonlocal chain
                loop_chain, chain = chain, extra_chain
                for b in range(1, NB):
                    if b < blocks_of(c):
                        slots_one_hot(x_e, b)
                        read_list(x_e, b)
                        xT_evict(x_e, b)
                    else:
                        dve.sem_inc(onehot_ready[b], 1)
                        dve.sem_inc(idx_ready[b], 1)
                        dve.sem_inc(xT_by_dve[b], 1)
                chain = loop_chain

            def swiglu(e, c):
                width = WIDTHS[c]
                for m in range(KT):
                    lin = lins[m % 2]
                    dve.wait_ge(h_ready, KT * e + m + 1)
                    dve.tensor_scalar(glu[:, 0:width], pair[m % 2][:, 0, 0:width], bias_cur[:, 2 * m:2 * m + 1], LIMIT,
                                      ALU.add, ALU.min).then_inc(glu_ready, 1)
                    dve.tensor_scalar(lin[:, 0:width], pair[m % 2][:, 1, 0:width], bias_cur[:, 2 * m + 1:2 * m + 2], LIMIT,
                                      ALU.add, ALU.min).then_inc(h_read, 1)
                    dve.wait_ge(h_read, KT * e + m + 1)
                    chain(dve.tensor_scalar(lin[:, 0:width], lin[:, 0:width], -LIMIT, 1.0, ALU.max, ALU.add))
                    dve.wait_ge(sig_ready, KT * e + m + 1)
                    chain(dve.tensor_tensor(gs[:, 0:width], glu[:, 0:width], sig[:, 0:width], ALU.mult))
                    chain.settle()
                    dve.tensor_tensor(actT[:, m, 0:width], gs[:, 0:width], lin[:, 0:width], ALU.mult).then_inc(act_ready, 1)

            def swiglu_by_class(e, cur):
                n = chain.n

                def body(c):
                    chain.n = n
                    swiglu(e, c)
                by_class(dve, cur, body)

            def expert(e, last):
                cur = dve.value_load(at(classes, e), min_val=0, max_val=2)
                chain(dve.tensor_copy(bias_cur[:, :].unsqueeze(1),
                                      bias_in[:, e:e + 1, :] if isinstance(e, int) else bias_in[:, bass.ds(e, 1), :]))
                chain.settle()
                if not last:
                    next_expert(e + 1)
                swiglu_by_class(e, cur)
                wait(dve, scattered, 16 * e)
                for b in range(1, NB):
                    wait(dve, scattered_more[b], e)
                chain(dve.tensor_copy(dest_cur[:, :], dest_next[:, :]))
                dve.tensor_copy(gate_cur[:, :], gate_next[:, :]).then_inc(cur_ready, 1)
                chain.settle()
                dve.wait_ge(cur_ready, e + 1)
                if not last:
                    nxt = dve.value_load(at(classes, e + 1), min_val=0, max_val=2)
                    read_list(e + 1, 0)
                    xT_evict(e + 1, 0)
                    by_class(dve, nxt, lambda c: more_blocks(e + 1, c))

            extra_chain = Chain(dve, extra_step)
            chain(dve.memset(gate_next[:, :], 0.0))
            chain(dve.memset(dest_next[:, :], 0.0))
            chain.settle()
            dve.wait_ge(b_in_evicted, 1)
            next_expert(0)
            dve.wait_ge(gates_transposed, 1)
            dve.tensor_copy(gateT, bank[3][0:NE, :]).then_inc(gateT_ready, 1)
            read_list(0, 0)
            for i in range(NT):
                for f in range(2):
                    n = 2 * i + f
                    dve.wait_ge(bias_out_product, n + 1)
                    half = resid[:, i, f * 512:(f + 1) * 512]
                    dve.tensor_tensor(half, half, bank[4 + n % 2], ALU.add).then_inc(bias_out_ready, 1)
            dve.wait_ge(classes_ready, 2)
            first = dve.value_load(at(classes, 0), min_val=0, max_val=2)
            xT_evict(0, 0)
            by_class(dve, first, lambda c: more_blocks(0, c))
            expert(0, False)
            start = chain.n
            chain.n = 0
            with dve.Fori(1, LAST) as e:
                chain.before = start + (e - 1) * STEPS_PER_EXPERT
                expert(e, False)
                assert chain.n == STEPS_PER_EXPERT, chain.n
            chain.before, chain.n = start + (LAST - 1) * STEPS_PER_EXPERT, 0
            expert(LAST, True)
            for r in range(TOPK):
                dve.wait_ge(parts_loaded[r], 16)
                for i in range(NT):
                    if r:
                        dve.wait_ge(sum_ready, (r - 1) * NT + i + 1)
                    else:
                        dve.wait_ge(bias_out_ready, 2 * NT)
                    dve.tensor_tensor(resid[:, i, :], resid[:, i, :], parts[r][:, i, :], ALU.add).then_inc(sum_ready, 1)
            dve.wait_ge(gf_loaded, 16)
            for i in range(NT):
                dve.wait_ge(sum_root, i + 1)
                chain(dve.reciprocal(stat[:, 52 + i:53 + i], stat[:, 52 + i:53 + i]))
                chain.settle()
                dve.scalar_tensor_tensor(parts[0][:, i, :], resid[:, i, :], stat[:, 52 + i:53 + i], gf_row,
                                         ALU.mult, ALU.mult).then_inc(out_ready, 1)

        @block.gpsimd
        def _(pool):
            pool.wait_ge(qk_transposed, 12)
            pool.wait_ge(const_loaded, 48)
            for h in range(NH):
                k_rows = proj[:, :, CRK + h * DQ:CRK + (h + 1) * DQ]
                pool.tensor_scalar(k_rows, k_rows, cst[:, C_KDEC + h:C_KDEC + h + 1], None, ALU.mult).then_inc(k_scaled, 1)
            for i in range(NT):
                g = proj[:, i, CRG:PROJ]
                pool.wait_ge(silu_sig, i + 1)
                pool.tensor_tensor(g, g, mix[:, i, 512:D], ALU.mult).then_inc(silu_done, 1)
                pool.wait_ge(silu_done, 2 * i + 1)
                pool.wait_ge(small_loaded, 16 * N_SMALL)
                pool.tensor_tensor(g, g, gain_row[:, 512:D], ALU.mult).then_inc(silu_done, 1)
            for i in range(NT):
                pool.wait_ge(av_evicted, i + 1)
                pool.tensor_tensor(mix[:, i, 0:512], mix[:, i, 0:512], gain_row[:, 0:512], ALU.mult).then_inc(mix_gained, 1)
            pool.wait_ge(silu_done, 2 * NT)
            for i in range(NT):
                pool.wait_ge(ret_evicted, i + 1)
                pool.tensor_tensor(mix[:, i, 512:D], mix[:, i, 512:D], proj[:, i, CRG:PROJ], ALU.mult).then_inc(mix_gained, 1)
            pool.wait_ge(mix_gained, 2 * NT)
            pool.wait_ge(ret_out, NT)
            pool.dma_start(g2_row, for_all_partitions(norm2_g[0]).rearrange("p (a c) -> p a c", a=NT))\
                .then_inc(late_loaded[0], 16)
            pool.dma_start(w_router_sb, w_router.rearrange("a (k p) e -> (a p) k e", p=P)).then_inc(late_loaded[1], 16)
            pool.dma_start(b_in_rows, b_moe_in[0]).then_inc(late_loaded[2], 16)
            pool.dma_start(b_out_rows, b_moe_out[0]).then_inc(late_loaded[3], 16)
            pool.iota(token_id, [[TOPK * P, NT]], base=0, channel_multiplier=TOPK,
                      allow_small_or_imprecise_dtypes=True).then_inc(tokens_named, 1)
            pool.iota(expert_id, [[1, NE]], base=0, channel_multiplier=0,
                      allow_small_or_imprecise_dtypes=True).then_inc(tokens_named, 1)
            pool.iota(slot_id, [[1, SEQ]], base=0, channel_multiplier=0,
                      allow_small_or_imprecise_dtypes=True).then_inc(tokens_named, 1)
            pool.memset(ones_row, 1.0).then_inc(tokens_named, 1)
            pool.wait_ge(logits_ready, NT)
            pool.wait_ge(h2_stored, 16 * NT)
            pool.memset(yT, 0.0).then_inc(yT_cleared, 1)
            pool.dma_start(gf_row, for_all_partitions(norm_f_g)).then_inc(gf_loaded, 16)

            def gather(x_e, b):
                pool.wait_ge(idx_ready[b], x_e + 1)
                if b:
                    pool.wait_ge(x_transposed[b - 1], x_e + 1)
                pool.sem_inc(pool_passed, 1)
                return pool.indirect_dma_start(out=x_rows, out_offset=None, in_=h2_dram,
                                               in_offset=bass.IndirectOffsetOnAxis(ap=token_next[:, b:b + 1], axis=0))

            def extra_dmas(e, c, transfer, landed, signal):
                if blocks_of(c) > 1:
                    before = pool.value_load(at(extras_before, e), min_val=0, max_val=NE * (NB - 1))
                for b in range(1, NB):
                    if b < blocks_of(c):
                        transfer(e, b).then_inc(landed, 16)
                        pool.wait_ge(landed, (before + b) * 16)
                    pool.sem_inc(signal[b], 1)

            def scatter(e, b):
                pool.wait_ge(rows_scaled[b], e + 1)
                pool.sem_inc(pool_passed, 1)
                return pool.indirect_dma_start(out=y_dram, in_=y_rows, in_offset=None,
                                               out_offset=bass.IndirectOffsetOnAxis(ap=dest_cur[:, b:b + 1], axis=0),
                                               bounds_check=SEQ * TOPK - 1, oob_is_err=False)

            def expert(e, last):
                if not last:
                    for b in range(NB):
                        pool.wait_ge(x_transposed[b], e + 1)
                    gather(e + 1, 0).then_inc(gathered, 16)
                    nxt = pool.value_load(at(classes, e + 1), min_val=0, max_val=2)
                    by_class(pool, nxt, lambda c: extra_dmas(e + 1, c, gather, extra_gathered, gathered_more))
                cur = pool.value_load(at(classes, e), min_val=0, max_val=2)
                scatter(e, 0).then_inc(scattered, 16)
                by_class(pool, cur, lambda c: extra_dmas(e, c, scatter, extra_scattered, scattered_more))

            pool.wait_ge(b_in_transposed, 1)
            gather(0, 0).then_inc(gathered, 16)
            pool.wait_ge(classes_ready, 2)
            first = pool.value_load(at(classes, 0), min_val=0, max_val=2)
            by_class(pool, first, lambda c: extra_dmas(0, c, gather, extra_gathered, gathered_more))
            expert(0, False)
            with pool.Fori(1, LAST) as e:
                expert(e, False)
            expert(LAST, True)

_INS = ["x", "positions", "norm1_g", "w_in", "lambda_q1", "lambda_k1", "lambda_q2", "lambda_k2", "diff_norm_g",
        "ret_norm_g", "w_o", "norm2_g", "w_router", "b_router", "w_moe_in", "b_moe_in", "w_moe_out", "b_moe_out",
        "norm_f_g"]


def kernel(**inputs):
    import numpy as _np
    import concourse.bacc as _bacc
    from concourse import mybir as _mybir
    from concourse.bass_utils import run_bass_kernel_spmd as _run

    nc = _bacc.Bacc("TRN2", target_bir_lowering=False, num_devices=1)
    arrays, args = {}, []
    for name in _INS:
        a = _np.ascontiguousarray(inputs[name])
        arrays[f"in_{name}"] = a
        args.append(nc.dram_tensor(f"in_{name}", a.shape, _mybir.dt.from_np(a.dtype), kind="ExternalInput").ap())
    out = nc.dram_tensor("out", (1, SEQ, D), F32, kind="ExternalOutput").ap()
    build(nc, *args, out)
    r = _run(nc, [arrays], core_ids=[0])
    return r.results[0]["out"]
```

```python
from contextlib import ExitStack
import math

import numpy as np

import concourse.bass as bass
from concourse import mybir

F32 = mybir.dt.float32
F32R = mybir.dt.float32r
BF16 = mybir.dt.bfloat16
I32 = mybir.dt.int32
U32 = mybir.dt.uint32
ALU = mybir.AluOpType
ACT = mybir.ActivationFunctionType
AX_X = mybir.AxisListType.X

P = 128
SEQ = 512
D = 1024
NT = SEQ // P
KT = D // P
PROJ = 3072
EPS = 1e-5
CW = 256
NCHUNK = PROJ // CW
CQ, CK, CV, CRQ, CRK, CRV, CRG = 0, 512, 1024, 1536, 1792, 2048, 2560
NH = 4
DQ = 64
SCALE = DQ ** -0.5
LAM_INIT = 0.8 - 0.6 * math.exp(-0.3 * 0)
NE = 32
TOPK = 4
FF = 1024
LIMIT = 7.0
SWI_ALPHA = 1.702
RING = 12
OUT_CHUNKS = D // CW
N_SMALL = 12
GW = 512
KH = KT // 2
CHUNKS = 12
IN_CHUNKS = 8
RAW = 6
PARTS = 3
DVE_K = 3
SLOTS = P
MAX_PASSES = SEQ * TOPK // SLOTS + NE - 1
AHEAD = 3
STEPS_PER_PASS = 13
NOWHERE = float(2 * TOPK * SEQ)
ROPE_CHUNKS = (0, 1, 2, 3, 6, 7)
TWO_PI_A = 6.28125
TWO_PI_B = round((2 * math.pi - TWO_PI_A) * 2.0 ** 20) / 2.0 ** 20
TWO_PI_C = 2 * math.pi - TWO_PI_A - TWO_PI_B
PI_F = 3.1415925
MAGIC = 12582912.0
MASKED = -1.0e30

C_IDENT, C_DECAY, C_QDEC, C_KDEC, C_FREQ = 0, 128, 640, 896, 900
C_N = 932


def shape_constants():
    f = np.float32
    c = np.zeros((P, C_N), f)
    r = np.arange(P)
    c[:, C_IDENT:C_IDENT + P] = np.eye(P)
    masks = np.concatenate([np.where(r[None, :] <= r[:, None], 0.0, MASKED), r[:, None] < r[None, :]], axis=1)
    log_decay = np.log(f(1.0) - f(2.0) ** (f(-5.0) - np.arange(NH, dtype=f))).astype(f)
    for h in range(NH):
        rel = (r[None, :] - r[:, None]).astype(f)
        at = C_DECAY + ((h % 2) * 2 + h // 2) * P
        c[:, at:at + P] = np.where(
            rel >= 0, np.exp(log_decay[h] * np.maximum(rel, 0)), 0.0) * SCALE
        rows = slice(64 * (h % 2), 64 * (h % 2) + 64)
        c[rows, C_QDEC + (h // 2) * P:C_QDEC + (h // 2 + 1) * P] = np.exp(log_decay[h] * (r[None, :] + f(1.0)))
        c[:, C_KDEC + h] = np.exp(log_decay[h] * (P - 1 - r)) * SCALE
    c[:, C_FREQ:C_FREQ + 32] = (f(1.0) / (f(10000.0) ** (np.arange(0, DQ, 2, dtype=f) / f(DQ))))[None, :]
    chunk = np.exp(log_decay * P).astype(f)
    return c, masks.astype(f), np.stack([np.repeat(chunk[0:2], 64), np.repeat(chunk[2:4], 64)], axis=1).astype(f)


def build(nc, x, positions, norm1_g, w_in, lambda_q1, lambda_k1, lambda_q2, lambda_k2, diff_norm_g,
          ret_norm_g, w_o, norm2_g, w_router, b_router, w_moe_in, b_moe_in, w_moe_out, b_moe_out,
          norm_f_g, out):
    ctx = ExitStack()
    with ctx:
        def sb(name, shape, dt=F32):
            return ctx.enter_context(nc.sbuf_tensor(name, shape, dt))

        def sem(name):
            return ctx.enter_context(nc.semaphore(name))

        def sems(name, n):
            return [sem(f"{name}{i}") for i in range(n)]

        def wait(eng, semaphore, value):
            if not (isinstance(value, int) and value <= 0):
                eng.wait_ge(semaphore, value)

        consts_np, masks_np, chunk_decay_np = shape_constants()
        consts_dram = nc.inline_tensor(consts_np, "shape_consts").ap()
        masks_dram = nc.inline_tensor(masks_np, "shape_masks").ap()
        chunk_decay_dram = nc.inline_tensor(chunk_decay_np, "chunk_decays").ap()
        h2_dram = nc.dram_tensor("h2_rows", [SEQ, D], F32, kind="Internal").ap()
        y_dram = nc.dram_tensor("expert_rows", [SEQ * TOPK, D], F32, kind="Internal").ap()

        ring = sb("ring", [P, RAW, KT, CW])
        with nc.sbuf_tensor("late_ring", [P, RING - RAW, KT, CW], F32) as late_ring:
            pass
        split = sb("split", [P, 2 * PARTS, KH * GW], F32R)
        resid = sb("resid", [P, NT, D])
        cst = sb("cst", [P, C_N])
        cos_sin = sb("cos_sin", [P, 2, NT, 32])
        gain_row = sb("gain_row", [P, D])
        ident_bf = sb("ident_bf", [P, P], BF16)
        causal_bf = sb("causal_bf", [P, P], BF16)
        utri_bf = sb("utri_bf", [P, P], BF16)
        ones_bf = sb("ones_bf", [P, P], BF16)
        g1_col = sb("g1_col", [P, KT])
        pos_i = sb("pos_i", [P, NT], I32)
        pos_f = sb("pos_f", [P, NT])
        lam = sb("lam", [P, 8])
        chunk_decay = sb("chunk_decay", [P, 2])
        b_router_row = sb("b_router_row", [P, NE])
        stat = sb("stat", [P, 56])
        eps_col = sb("eps_col", [P, 1])
        row_max = sb("row_max", [P, 2, 2])
        row_bias = sb("row_bias", [P, 2, 2])
        row_sum = sb("row_sum", [P, 2, 2])
        row_rec = sb("row_rec", [P, 2, 2])
        pass_expert = sb("pass_expert", [1, MAX_PASSES + 1], I32)
        passes_upto = sb("passes_upto", [1, NE], I32)
        pos_cur = sb("pos_cur", [P, NT])
        first_cur = sb("first_cur", [P, 1])
        dest_next = sb("dest_next", [P, 1], I32)
        dest_cur = sb("dest_cur", [P, 1], I32)
        token_next = sb("token_next", [P, 1], I32)
        gate_next = sb("gate_next", [P, 1])
        gate_cur = sb("gate_cur", [P, 1])

        with nc.sbuf_tensor("work", [P, 21504], F32) as work:
            pass
        operands = sb("operands", [P, 6272], F32R)

        def slot(n):
            return ring[:, n] if n < RAW else late_ring[:, n - RAW]

        def w(a, n, rows=P):
            return work[0:rows, a:a + n]

        proj = w(0, NT * PROJ).rearrange("p (i c) -> p i c", i=NT)
        xn = w(4096, NT * D).rearrange("p (i c) -> p i c", i=NT)
        junk1 = w(0, NT * D).rearrange("p (i c) -> p i c", i=NT)
        hT = w(12288, KT * SEQ).rearrange("p (k t) -> p k t", k=KT)
        qkT = w(12288, 12 * SEQ).rearrange("p (g t) -> p g t", g=12)
        rope_tmp = w(18432, 4 * 512).rearrange("p (a i g f) -> p a i g f", a=4, i=NT, g=4)
        ang = w(18432, 6 * 128).rearrange("p (a i f) -> p a i f", a=6, i=NT)
        lam_rows = w(19456, 4 * DQ).rearrange("p (a d) -> p a d", a=4)
        raw_masks = w(20480, 2 * P)
        probs = w(18432, 2 * 2 * SEQ).rearrange("p (b m t) -> p b m t", b=2, m=2)
        attT = w(20480, 2 * SEQ).rearrange("p (b t) -> p b t", b=2)
        mix = proj[:, :, 0:D]
        square_tmp = proj[:, :, CRQ:CRQ + P]
        g2_row = proj[:, :, CRQ:CRQ + 256]
        st_s = w(18432, 2 * 512).rearrange("p (b r a n) -> p b r a n", b=2, r=2, a=2)
        state = w(19456, 2 * P).rearrange("p (a n) -> p a n", a=2)
        qdT = w(20480, 2 * SEQ).rearrange("p (a t) -> p a t", a=2)
        mixT = w(12288, 2 * D).rearrange("p (b k t) -> p b k t", b=2, k=KT)
        b_in_rows = w(14336, 2 * FF, 2 * NE)
        w_router_sb = w(16384, KT * NE).rearrange("p (k e) -> p k e", k=KT)
        junk2 = w(16896, D)
        h2_row = proj[:, :, 0:D]
        b_out_rows = w(11008, D, NE)
        gateT = w(7168, SEQ, NE)
        route = w(18944, NT * NE * 4).rearrange("p (i e c) -> p i e c", i=NT, e=NE)
        slot_of = w(19456, NT * NE).rearrange("p (i e) -> p i e", i=NT)
        pass_first = w(19584, MAX_PASSES + 1)
        pass_id = w(19632, MAX_PASSES + 1)
        cum_passes = w(19680, NE)
        n_passes = w(19712, NE)
        expert_count = w(19744, NE)
        pass_e = w(19776, MAX_PASSES + 1)
        scatters_upto = w(19824, NE, 1).bitcast(I32)
        earlier = w(7680, (MAX_PASSES + 1) * NE).rearrange("p (n e) -> p n e", e=NE)
        logits = w(20096, NE)
        top8 = w(20128, 8)
        top8_f = w(20136, 8)
        top8_i = w(20144, 8).bitcast(U32)
        picked = w(20160, NT * NE).rearrange("p (i e) -> p i e", i=NT)
        expo = w(20288, NE)
        gates = w(20320, NT * NE).rearrange("p (i e) -> p i e", i=NT)
        rank = w(20448, NE)
        picked_bf = w(20480, NT * NE // 2).bitcast(BF16).rearrange("p (i e) -> p i e", i=NT)
        ones_row = w(20544, NE)
        token_id = w(20576, NT)
        expert_id = w(20608, NE)
        rstat = w(20640, 16)
        route_cur = w(20672, NT * 4).rearrange("p (i c) -> p i c", i=NT)
        slot_id = w(20992, SLOTS)
        junk_out = w(8192, D)
        def halves(a):
            return operands[:, a:a + KT * SLOTS].rearrange("p (k t) -> p k t", k=KT)

        xT_hi, xT_lo, actT_hi, actT_lo = (halves(n * KT * SLOTS) for n in range(4))
        y_rows = w(9216, D)
        glu, sig, lin, gs = (w(7680 + n * 256, 256) for n in range(4))
        act_rows = w(8704, 512).rearrange("p (b c) -> p b c", b=2)
        b_in_parts = operands[0:2 * NE, 4096:4096 + 2 * FF]
        gf_row = w(12288, D)
        x_rows = w(13312, D)
        onehot = w(16384, NT * P).rearrange("p (i s) -> p i s", i=NT)
        pick_bias = operands[0:2 * NE, 6144:6144 + SLOTS]
        raw = [ring[:, s].rearrange("p k c -> p (k c)").rearrange("p (k c) -> p k c", c=GW) for s in range(RAW)]
        hi, lo = ([split[:, s].rearrange("p (k c) -> p k c", c=GW) for s in range(a, a + PARTS)]
                  for a in (0, PARTS))
        parts = [(ring[:, 2 * r:2 * r + 2] if 2 * r < RAW else late_ring[:, 2 * r - RAW:2 * r - RAW + 2])
                 .rearrange("p a k c -> p (a k c)")
                 .rearrange("p (i c) -> p i c", i=NT) for r in range(TOPK)]

        pair = [ctx.enter_context(nc.psum_tensor(f"pair{i}", [P, 2, 512], F32)) for i in range(4)]
        bank = [pair[i // 2][:, i % 2, :] for i in range(8)]

        x_loaded = sems("x_loaded", NT)
        small_loaded = sem("small_loaded")
        const_loaded = sem("const_loaded")
        slot_full = sems("slot_full", RING)
        act_step = sem("act_step")
        tail_step = sem("tail_step")
        dve_step = sem("dve_step")
        x_squared = sem("x_squared")
        x_root = sem("x_root")
        head_root_ready = sem("head_root_ready")
        x2_root = sem("x2_root")
        sum_root = sem("sum_root")
        pool_passed = sem("pool_passed")
        eps_set = sem("eps_set")
        xn_ready = sem("xn_ready")
        xn_transposed = sem("xn_transposed")
        hT_by_act = sem("hT_by_act")
        hT_by_dve = sem("hT_by_dve")
        ang_ready = sem("ang_ready")
        trig_ready = sem("trig_ready")
        lam_dots = sem("lam_dots")
        lam_exp = sem("lam_exp")
        proj_ready = sem("proj_ready")
        proj_by_act = sem("proj_by_act")
        proj_by_dve = sem("proj_by_dve")
        rope_done = sem("rope_done")
        cast_done = sem("cast_done")
        qk_transposed = sem("qk_transposed")
        qk_by_act = sem("qk_by_act")
        qk_by_dve = sem("qk_by_dve")
        k_scaled = sem("k_scaled")
        silu_sig = sem("silu_sig")
        silu_done = sem("silu_done")
        scores_ready = sem("scores_ready")
        bias_ready = sem("bias_ready")
        exp_done = sem("exp_done")
        att_ready = sem("att_ready")
        att_transposed = sem("att_transposed")
        attT_ready = sem("attT_ready")
        av_ready = sem("av_ready")
        av_evicted = sem("av_evicted")
        ret_scores = sem("ret_scores")
        ret_decayed = sem("ret_decayed")
        qd_ready = sem("qd_ready")
        ret_out = sem("ret_out")
        ret_kv = sem("ret_kv")
        ret_evicted = sem("ret_evicted")
        state_ready = sem("state_ready")
        mix_gained = sem("mix_gained")
        late_loaded = sems("late_loaded", 4)
        mix_ready = sem("mix_ready")
        mix_transposed = sem("mix_transposed")
        mixT_by_act = sem("mixT_by_act")
        mixT_by_dve = sem("mixT_by_dve")
        wo_done = sem("wo_done")
        x2_ready = sem("x2_ready")
        x2_squared = sem("x2_squared")
        h2_ready = sem("h2_ready")
        h2_stored = sem("h2_stored")
        h2_transposed = sem("h2_transposed")
        h2T_by_act = sem("h2T_by_act")
        h2T_by_dve = sem("h2T_by_dve")
        logits_ready = sem("logits_ready")
        logits_read = sem("logits_read")
        max_ready = sem("max_ready")
        gate_exp = sem("gate_exp")
        picked_ready = sem("picked_ready")
        place_ready = sem("place_ready")
        place_read = sem("place_read")
        b_in_rounded = sem("b_in_rounded")
        b_in_split = sem("b_in_split")
        table_ready = sem("table_ready")
        gates_transposed = sem("gates_transposed")
        gateT_ready = sem("gateT_ready")
        bias_out_product = sem("bias_out_product")
        bias_out_ready = sem("bias_out_ready")
        tokens_named = sem("tokens_named")
        gf_loaded = sem("gf_loaded")
        raw_full = sems("raw_full", RAW)
        hi_made = sem("hi_made")
        lo_by_dve = sem("lo_by_dve")
        lo_by_pool = sem("lo_by_pool")
        chunk_used = sem("chunk_used")
        onehot_ready = sem("onehot_ready")
        list_ready = sem("list_ready")
        idx_ready = sem("idx_ready")
        gathered = sem("gathered")
        x_transposed = sem("x_transposed")
        xT_hi_made = sem("xT_hi_made")
        xT_lo_made = sem("xT_lo_made")
        pick_ready = sem("pick_ready")
        h_read = sem("h_read")
        glu_ready = sem("glu_ready")
        sig_ready = sem("sig_ready")
        act_ready = sem("act_ready")
        act_transposed = sem("act_transposed")
        actT_hi_made = sem("actT_hi_made")
        actT_lo_made = sem("actT_lo_made")
        y_scaled = sem("y_scaled")
        cur_ready = sem("cur_ready")
        scattered = sem("scattered")
        parts_loaded = sems("parts_loaded", TOPK)
        sum_ready = sem("sum_ready")
        sum_squared = sem("sum_squared")
        out_ready = sem("out_ready")
        out_stored = sem("out_stored")

        class Chain:
            def __init__(self, eng, semaphore):
                self.eng, self.sem, self.before, self.n = eng, semaphore, 0, 0

            def __call__(self, ins):
                ins.then_inc(self.sem, 1)
                self.n += 1

            def settle(self):
                wait(self.eng, self.sem, self.before + self.n)

        def for_all_partitions(row):
            return row.partition_broadcast(P)

        x_rows_dram = x.rearrange("a (i p) d -> (a i) p d", p=P)
        w_in_cols = w_in.rearrange("a (k p) c -> (a p) k c", p=P)
        w_o_cols = w_o.rearrange("a (k p) c -> (a p) k c", p=P)

        def at(row, e):
            return row[0:1, e:e + 1] if isinstance(e, int) else row[0:1, bass.ds(e, 1)]

        def of_expert(m, e):
            return m[0, e:e + 1] if isinstance(e, int) else m[0, bass.ds(e, 1)]

        def expert_chunk(e, j):
            m, n = (w_moe_in, j) if j < IN_CHUNKS else (w_moe_out, j - IN_CHUNKS)
            rows = of_expert(m, e).rearrange("e (a k p) c -> a (e p) k c", p=P, a=2)[n % 2]
            return rows[:, :, n // 2 * GW:(n // 2 + 1) * GW]

        def by_pass(eng, body):
            with eng.Fori(1, MAX_PASSES) as p:
                with eng.If(p < passes[eng]):
                    body(p)

        passes = {}

        def load_pass_count(eng):
            eng.wait_ge(table_ready, 2)
            passes[eng] = eng.value_load(at(passes_upto, NE - 1), min_val=1, max_val=MAX_PASSES)

        wo_slot = [RING - OUT_CHUNKS + q for q in range(OUT_CHUNKS)]
        block = ctx.enter_context(nc.Block())

        @block.sync
        def _(sp):
            for i in range(NT):
                sp.dma_start(resid[:, i, :], x_rows_dram[i]).then_inc(x_loaded[i], 16)
            sp.dma_start(cst[:, :], consts_dram).then_inc(const_loaded, 16)
            sp.dma_start(raw_masks, masks_dram).then_inc(const_loaded, 16)
            sp.dma_start(chunk_decay[:, :], chunk_decay_dram).then_inc(const_loaded, 16)
            for c in range(NCHUNK):
                sp.dma_start(slot(c), w_in_cols[:, :, c * CW:(c + 1) * CW]).then_inc(slot_full[c], 16)
            for q, s in enumerate(wo_slot):
                sp.wait_ge(proj_ready, NT * (s + 1))
                sp.dma_start(slot(s), w_o_cols[:, :, q * CW:(q + 1) * CW]).then_inc(slot_full[s], 16)

            def load(p, e, j):
                if isinstance(p, int) and p == 0 and j < RAW:
                    sp.wait_ge(proj_ready, NT * (j + 1))
                else:
                    for made in (hi_made, lo_by_dve, lo_by_pool):
                        sp.wait_ge(made, CHUNKS * p + j - RAW + 1)
                sp.dma_start(raw[j % RAW], expert_chunk(e, j)).then_inc(raw_full[j % RAW], 16)

            def expert_of(p):
                return sp.value_load(at(pass_expert, p), min_val=0, max_val=NE - 1)

            def one_pass(p):
                e, following = expert_of(p), expert_of(p + 1)
                for j in range(AHEAD, CHUNKS):
                    load(p, e, j)
                for j in range(AHEAD):
                    load(p + 1, following, j)

            load_pass_count(sp)
            first = expert_of(0)
            for j in range(AHEAD):
                load(0, first, j)
            one_pass(0)
            by_pass(sp, one_pass)
            rows_out = [sp.value_load(at(scatters_upto, NE - TOPK + r), min_val=0, max_val=16 * MAX_PASSES)
                        for r in range(TOPK)]
            all_split = sp.snap(passes[sp] * CHUNKS + AHEAD)
            all_used = sp.snap(passes[sp] * CHUNKS)
            for made in (hi_made, lo_by_dve, lo_by_pool):
                sp.wait_ge(made, all_split)
            for r in range(TOPK):
                sp.wait_ge(scattered, rows_out[r])
                if 2 * r + 1 >= RAW:
                    sp.wait_ge(chunk_used, all_used)
                sp.dma_start(parts[r], y_dram.rearrange("(i p r) c -> r p i c", p=P, r=TOPK)[r])\
                    .then_inc(parts_loaded[r], 16)
            for i in range(NT):
                sp.wait_ge(out_ready, i + 1)
                sp.dma_start(out.rearrange("a (i p) d -> (a i) p d", p=P)[i], parts[0][:, i, :])\
                    .then_inc(out_stored, 16)
            sp.wait_ge(out_stored, 16 * NT)
            sp.wait_ge(h2_stored, 16 * NT)

        @block.tensor
        def _(pe):
            ident = cst[:, C_IDENT:C_IDENT + P]
            pe.wait_ge(const_loaded, 48)
            pe.wait_ge(xn_ready, NT)
            for k in range(KT):
                for i in range(NT):
                    mm = pe.transpose(bank[k][:, i * P:(i + 1) * P], xn[:, i, k * P:(k + 1) * P], ident)
                mm.then_inc(xn_transposed, 1)
            pe.wait_ge(hT_by_act, KT // 2)
            pe.wait_ge(hT_by_dve, KT // 2)
            for c in range(NCHUNK):
                pe.wait_ge(slot_full[c], 16)
                for i in range(NT):
                    u = c * NT + i
                    if u >= 4:
                        pe.wait_ge(proj_by_act if u % 2 == 0 else proj_by_dve, (u - 4) // 2 + 1)
                    for k in range(KT):
                        mm = pe.matmul(bank[u % 4][:, 0:CW], hT[:, k, i * P:(i + 1) * P], slot(c)[:, k, :],
                                       start=(k == 0), stop=(k == KT - 1))
                    mm.then_inc(proj_ready, 1)
            for g in range(12):
                col = (CQ + g * P if g < 8 else CRQ + (g - 8) * P)
                if g == 0:
                    pe.wait_ge(rope_done, len(ROPE_CHUNKS))
                if g >= 4:
                    pe.wait_ge(qk_by_act if g % 2 == 0 else qk_by_dve, (g - 4) // 2 + 1)
                for i in range(NT):
                    mm = pe.transpose(bank[4 + g % 4][:, i * P:(i + 1) * P], proj[:, i, col:col + P], ident)
                mm.then_inc(qk_transposed, 1)
            pe.wait_ge(qk_by_act, 6)
            pe.wait_ge(qk_by_dve, 6)
            pe.wait_ge(proj_by_act, NCHUNK * NT // 2)
            pe.wait_ge(proj_by_dve, NCHUNK * NT // 2)
            pe.wait_ge(cast_done, 4)

            def scores(u):
                i, h = divmod(u, NH)
                if u >= 2:
                    pe.wait_ge(exp_done, 2 * (u - 1))
                for m in range(2):
                    rows = slice(64 * m, 64 * m + 64)
                    n = (i + 1) * P
                    dst = pair[u % 2][:, m, 0:n]
                    pe.matmul(dst, qkT[rows, h, i * P:(i + 1) * P], qkT[rows, 4 + h, 0:n],
                              start=True, stop=False, skip_group_check=True)
                for m in range(2):
                    mm = pe.matmul(pair[u % 2][:, m, i * P:(i + 1) * P], ident_bf[:, :], causal_bf[:, :],
                                   start=False, stop=True, skip_group_check=True)
                mm.then_inc(scores_ready, 1)

            def att_transposes(u):
                i, h = divmod(u, NH)
                pe.wait_ge(att_ready, u + 1)
                if u >= 2:
                    pe.wait_ge(attT_ready, u - 1)
                for j in range(i + 1):
                    mm = pe.transpose(bank[4 + u % 2][:, j * P:(j + 1) * P],
                                      probs[:, u % 2, 0, j * P:(j + 1) * P], ident)
                mm.then_inc(att_transposed, 1)

            def att_values(u):
                i, h = divmod(u, NH)
                pe.wait_ge(attT_ready, u + 1)
                if h == 0 and i >= 1:
                    pe.wait_ge(av_evicted, i)
                for j in range(i + 1):
                    mm = pe.matmul(bank[6][:, h * P:(h + 1) * P], attT[:, u % 2, j * P:(j + 1) * P],
                                   proj[:, j, CV + h * P:CV + (h + 1) * P], start=(j == 0), stop=(j == i))
                mm.then_inc(av_ready, 1)

            NU = NT * NH
            for s in range(NU + 3):
                if s < NU:
                    scores(s)
                if 2 <= s < NU + 2:
                    att_transposes(s - 2)
                if s >= 3:
                    att_values(s - 3)

            def ret_score(i):
                if i >= 2:
                    pe.wait_ge(state_ready, 2 * (i - 1))
                for h in range(NH):
                    rows = slice(64 * (h % 2), 64 * (h % 2) + 64)
                    mm = pe.matmul(pair[i % 2][:, h % 2, (h // 2) * P:(h // 2 + 1) * P],
                                   qkT[rows, 10 + h // 2, i * P:(i + 1) * P],
                                   qkT[rows, 8 + h // 2, i * P:(i + 1) * P], start=True, stop=True)
                mm.then_inc(ret_scores, 1)

            def ret_output(i):
                pe.wait_ge(ret_decayed, i + 1)
                if i >= 2:
                    pe.wait_ge(ret_evicted, i - 1)
                if i >= 1:
                    pe.wait_ge(state_ready, 2 * i)
                    pe.wait_ge(qd_ready, 2)
                for h in range(NH):
                    rows = slice(64 * (h % 2), 64 * (h % 2) + 64)
                    dst = pair[2 + i % 2][:, h % 2, (h // 2) * P:(h // 2 + 1) * P]
                    if i >= 1:
                        pe.matmul(dst, qdT[rows, h // 2, i * P:(i + 1) * P], state[rows, h // 2, :],
                                  start=True, stop=False)
                    mm = pe.matmul(dst, st_s[:, i % 2, h % 2, h // 2, :],
                                   proj[:, i, CRV + h * P:CRV + (h + 1) * P], start=(i == 0), stop=True)
                mm.then_inc(ret_out, 1)
                if i < NT - 1:
                    if i == 0:
                        pe.wait_ge(k_scaled, NT)
                    for h in range(NH):
                        rows = slice(64 * (h % 2), 64 * (h % 2) + 64)
                        mm = pe.matmul(pair[i % 2][rows, 0, 256 + (h // 2) * P:256 + (h // 2 + 1) * P],
                                       proj[:, i, CRK + h * DQ:CRK + (h + 1) * DQ],
                                       proj[:, i, CRV + h * P:CRV + (h + 1) * P], start=True, stop=True)
                    mm.then_inc(ret_kv, 1)

            pe.wait_ge(exp_done, 2 * NU)
            pe.wait_ge(attT_ready, NU)
            pe.wait_ge(av_evicted, NT)
            ret_score(0)
            for i in range(NT):
                if i + 1 < NT:
                    ret_score(i + 1)
                ret_output(i)

            def mix_product(i):
                pe.wait_ge(mix_ready, i + 1)
                for k in range(KT):
                    if k == 4:
                        mm.then_inc(mix_transposed, 1)
                    mm = pe.transpose(bank[k // 4][:, (k % 4) * P:(k % 4 + 1) * P],
                                      mix[:, i, k * P:(k + 1) * P], ident)
                mm.then_inc(mix_transposed, 1)
                pe.wait_ge(mixT_by_act, i + 1)
                pe.wait_ge(mixT_by_dve, i + 1)
                if i >= 2:
                    pe.wait_ge(x2_ready, 2 * (i - 1))
                for q, s in enumerate(wo_slot):
                    if i == 0:
                        pe.wait_ge(slot_full[s], 32)
                    dst = pair[1 + i % 2][:, q // 2, (q % 2) * CW:(q % 2 + 1) * CW]
                    for k in range(KT):
                        mm = pe.matmul(dst, mixT[:, i % 2, k, :], slot(s)[:, k, :],
                                       start=(k == 0), stop=(k == KT - 1))
                mm.then_inc(wo_done, 1)

            def router(i):
                pe.wait_ge(h2_ready, i + 1)
                if i >= 1:
                    pe.wait_ge(logits_read, i)
                    pe.wait_ge(place_read, i)
                for k in range(KT):
                    if k == 4:
                        mm.then_inc(h2_transposed, 1)
                    mm = pe.transpose(bank[6 + k // 4][:, (k % 4) * P:(k % 4 + 1) * P],
                                      h2_row[:, i, k * P:(k + 1) * P], ident)
                mm.then_inc(h2_transposed, 1)
                pe.wait_ge(h2T_by_act, i + 1)
                pe.wait_ge(h2T_by_dve, i + 1)
                if i == 0:
                    pe.wait_ge(late_loaded[1], 16)
                for k in range(KT):
                    mm = pe.matmul(bank[6][:, 0:NE], mixT[:, i % 2, k, :], w_router_sb[:, k, :],
                                   start=(k == 0), stop=(k == KT - 1))
                mm.then_inc(logits_ready, 1)

            def places(i):
                pe.wait_ge(picked_ready, i + 1)
                for j in range(i + 1):
                    mm = pe.matmul(bank[7][:, 0:NE], (utri_bf if j == i else ones_bf)[:, :], picked_bf[:, j, :],
                                   start=(j == 0), stop=(j == i))
                mm.then_inc(place_ready, 1)

            mix_product(0)
            mix_product(1)
            for i in range(NT):
                router(i)
                if i + 2 < NT:
                    mix_product(i + 2)
                places(i)
            pe.wait_ge(place_read, NT)
            for j in range(NT):
                mm = pe.matmul(bank[7][:, 64:64 + NE], ones_bf[:, :], picked_bf[:, j, :],
                               start=(j == 0), stop=(j == NT - 1))
            mm.then_inc(place_ready, 1)

            def token_list(p):
                pe.wait_ge(onehot_ready, p + 1)
                for i in range(NT):
                    mm = pe.matmul(bank[5][:, 0:4], onehot[:, i, :], route_cur[:, i, :],
                                   start=(i == 0), stop=(i == NT - 1))
                mm.then_inc(list_ready, 1)

            def x_transposes(p):
                pe.wait_ge(gathered, 16 * (p + 1))
                for k in range(KT):
                    mm = pe.transpose(bank[6 + k // KH][:, (k % KH) * P:(k % KH + 1) * P],
                                      x_rows[:, k * P:(k + 1) * P], ident)
                    if k % KH == KH - 1:
                        mm.then_inc(x_transposed, 1)

            pe.wait_ge(x2_ready, 2 * NT)
            token_list(0)
            for i in range(NT):
                mm = pe.transpose(bank[3][0:NE, i * P:(i + 1) * P], gates[:, i, :], ident)
            mm.then_inc(gates_transposed, 1)
            pe.wait_ge(gateT_ready, 1)
            pe.wait_ge(late_loaded[3], 16)
            for i in range(NT):
                for f in range(2):
                    n = 2 * i + f
                    if n == 1:
                        pe.wait_ge(idx_ready, 1)
                    if n >= 2:
                        pe.wait_ge(bias_out_ready, n - 1)
                    pe.matmul(bank[4 + n % 2], gateT[:, i * P:(i + 1) * P], b_out_rows[:, f * 512:(f + 1) * 512],
                              start=True, stop=True).then_inc(bias_out_product, 1)
            pe.wait_ge(table_ready, 1)
            x_transposes(0)
            load_pass_count(pe)
            pe.wait_ge(b_in_split, 1)
            pe.wait_ge(bias_out_ready, 2 * NT)

            def product(p, j, dst, left_hi, left_lo, start, stop, before_tile=None):
                n = CHUNKS * p + j + 1
                for made in (hi_made, lo_by_dve, lo_by_pool):
                    pe.wait_ge(made, n)
                s, k0 = j % PARTS, (j % 2) * KH
                for k in range(KH):
                    if before_tile:
                        before_tile(k0 + k)
                    pe.matmul(dst, left_hi[:, k0 + k, :], hi[s][:, k, :], start=(start and k == 0), stop=False)
                    pe.matmul(dst, left_hi[:, k0 + k, :], lo[s][:, k, :], start=False, stop=False)
                    mm = pe.matmul(dst, left_lo[:, k0 + k, :], hi[s][:, k, :], start=False,
                                   stop=(stop and k == KH - 1))
                mm.then_inc(chunk_used, 1)

            def act_transposes(p, g):
                pe.wait_ge(act_ready, 4 * p + g + 1)
                if g >= 2:
                    pe.wait_ge(actT_lo_made, 4 * p + g - 1)
                for n in range(2):
                    mm = pe.transpose(bank[6 + g % 2][:, n * P:(n + 1) * P],
                                      act_rows[:, g % 2, n * P:(n + 1) * P], ident)
                mm.then_inc(act_transposed, 1)

            def one_pass(p):
                pe.wait_ge(pick_ready, 2 * (p + 1))
                for g in range(4):
                    wait(pe, h_read, 4 * (p - 1) + g + 1)
                    pe.matmul(bank[g], pick_bias, b_in_parts[:, g * GW:(g + 1) * GW], start=True, stop=False)
                    for a in range(2):
                        if g == 0:
                            pe.wait_ge(xT_hi_made, 2 * p + a + 1)
                            pe.wait_ge(xT_lo_made, 2 * p + a + 1)
                        product(p, 2 * g + a, bank[g], xT_hi, xT_lo, False, a == 1)
                    if g >= 1:
                        act_transposes(p, g - 1)
                    if g == 1:
                        wait(pe, y_scaled, 2 * p)
                        token_list(p + 1)
                wait(pe, y_scaled, 2 * p)

                def act_tile_there(k):
                    if k % 2 == 0:
                        pe.wait_ge(actT_hi_made, 4 * p + k // 2 + 1)
                        pe.wait_ge(actT_lo_made, 4 * p + k // 2 + 1)

                product(p, 8, bank[4], actT_hi, actT_lo, True, False, act_tile_there)
                act_transposes(p, 3)
                product(p, 9, bank[4], actT_hi, actT_lo, False, True, act_tile_there)
                x_transposes(p + 1)
                pe.wait_ge(idx_ready, p + 2)
                product(p, 10, bank[5], actT_hi, actT_lo, True, False)
                product(p, 11, bank[5], actT_hi, actT_lo, False, True)

            one_pass(0)
            by_pass(pe, one_pass)

        @block.scalar
        def _(act):
            small = [(pos_i[:, :], positions.rearrange("a (i p) -> (a p) i", p=P)),
                     (g1_col[:, :], norm1_g.rearrange("a (k p) -> (a p) k", p=P))]
            for n, row in enumerate((lambda_q1, lambda_k1, lambda_q2, lambda_k2)):
                small.append((lam_rows[:, n, :], for_all_partitions(row[0])))
            for h in range(NH):
                small.append((gain_row[:, h * P:(h + 1) * P], for_all_partitions(diff_norm_g[0])))
            small.append((gain_row[:, 512:D], for_all_partitions(ret_norm_g.rearrange("a h c -> (a h c)"))))
            small.append((b_router_row[:, :], for_all_partitions(b_router[0])))
            assert len(small) == N_SMALL
            with nc.allow_non_contiguous_dma(reason="a few hundred words"):
                for dst, src in small:
                    act.dma_start(dst, src).then_inc(small_loaded, 16)
            def root(at, n, mean_of, ready):
                act.activation(stat[:, at:at + n], stat[:, at:at + n], ACT.Sqrt, bias=eps_col[:, 0:1],
                               scale=1.0 / mean_of).then_inc(ready, 1)

            for i in range(NT):
                act.wait_ge(x_loaded[i], 16)
                act.activation(junk1[:, i, :], resid[:, i, :], ACT.Square, accum_out=stat[:, i:i + 1]).then_inc(x_squared, 1)
            act.wait_ge(x_squared, NT)
            act.wait_ge(eps_set, 1)
            root(0, NT, D, x_root)
            act.wait_ge(small_loaded, 16 * N_SMALL)
            for k in range(0, KT, 2):
                act.wait_ge(xn_transposed, k + 1)
                act.activation(hT[:, k, :], bank[k], ACT.Copy, scale=g1_col[:, k:k + 1]).then_inc(hT_by_act, 1)
            act.wait_ge(ang_ready, 2)
            act.activation(cos_sin[:, 0], ang[:, 5], ACT.Sin).then_inc(trig_ready, 1)
            act.activation(cos_sin[:, 1], ang[:, 3], ACT.Sin).then_inc(trig_ready, 1)
            act.wait_ge(lam_dots, 1)
            act.activation(lam[:, 2:4], lam[:, 0:2], ACT.Exp).then_inc(lam_exp, 1)
            for c in range(NCHUNK):
                for i in range(0, NT, 2):
                    u = c * NT + i
                    act.wait_ge(proj_ready, u + 1)
                    act.copy(proj[:, i, c * CW:(c + 1) * CW], bank[u % 4][:, 0:CW]).then_inc(proj_by_act, 1)
            for g in range(0, 12, 2):
                act.wait_ge(qk_transposed, g + 1)
                act.copy(qkT[:, g, :], bank[4 + g % 4]).then_inc(qk_by_act, 1)
            act.wait_ge(qk_transposed, 12)
            act.wait_ge(proj_by_act, NCHUNK * NT // 2)
            act.wait_ge(proj_by_dve, NCHUNK * NT // 2)
            for i in range(NT):
                act.activation(mix[:, i, 512:D], proj[:, i, CRG:PROJ], ACT.Sigmoid).then_inc(silu_sig, 1)

            def head_squares(outputs, i, first_head):
                chain.settle()
                for h in range(NH):
                    col = 16 + 2 * NH * i + first_head + h
                    chain(act.activation(square_tmp[:, h, :], outputs[h], ACT.Square,
                                         accum_out=stat[:, col:col + 1]))

            chain = Chain(act, act_step)

            def exponentials(u):
                i, b, n = u // NH, u % 2, (u // NH + 1) * P
                act.wait_ge(bias_ready, u + 1)
                if u >= 2:
                    act.wait_ge(att_transposed, u - 1)
                for m in range(2):
                    act.activation(probs[:, b, m, 0:n], pair[b][:, m, 0:n], ACT.Exp, bias=row_bias[:, b, m:m + 1],
                                   scale=SCALE, accum_out=row_sum[:, b, m:m + 1]).then_inc(exp_done, 1)

            NU = NT * NH
            for s in range(NU + 3):
                if s < NU:
                    exponentials(s)
                if 2 <= s < NU + 2:
                    u = s - 2
                    n = (u // NH + 1) * P
                    act.wait_ge(att_transposed, u + 1)
                    if u >= 2:
                        act.wait_ge(av_ready, u - 1)
                    act.copy(attT[:, u % 2, 0:n], bank[4 + u % 2][:, 0:n]).then_inc(attT_ready, 1)
                if s >= 3 and (s - 3) % NH == NH - 1:
                    i = (s - 3) // NH
                    act.wait_ge(av_ready, s - 2)
                    head_squares([bank[6][:, h * P:(h + 1) * P] for h in range(NH)], i, 0)
                    act.copy(mix[:, i, 0:512], bank[6]).then_inc(av_evicted, 1)
            act.wait_ge(silu_done, 2 * NT)
            for i in range(NT):
                act.wait_ge(ret_out, i + 1)
                outputs = pair[2 + i % 2][:, :, 0:256].rearrange("p r (a c) -> p a r c", a=2)
                head_squares([outputs[:, h // 2, h % 2, :] for h in range(NH)], i, NH)
                act.copy(mix[:, i, 512:D].rearrange("p (a r c) -> p a r c", a=2, r=2), outputs).then_inc(ret_evicted, 1)

            act.wait_ge(ret_evicted, NT)
            chain.settle()
            root(16, 2 * NH * NT, P, head_root_ready)

            def mix_evict(i):
                act.wait_ge(mix_transposed, 2 * i + 1)
                act.copy(mixT[:, i % 2, 0:4, :], bank[0].rearrange("p (k t) -> p k t", k=4)).then_inc(mixT_by_act, 1)

            mix_evict(0)
            mix_evict(1)
            for i in range(NT):
                act.wait_ge(x2_ready, 2 * (i + 1))
                act.activation(junk2, resid[:, i, :], ACT.Square, accum_out=stat[:, 48 + i:49 + i]).then_inc(x2_squared, 1)
                act.wait_ge(x2_squared, i + 1)
                root(48 + i, 1, D, x2_root)
                act.wait_ge(h2_ready, i + 1)
                act.dma_start(h2_dram[i * P:(i + 1) * P, :], h2_row[:, i, :]).then_inc(h2_stored, 16)
                act.wait_ge(h2_transposed, 2 * i + 1)
                act.copy(mixT[:, i % 2, 0:4, :], bank[6].rearrange("p (k t) -> p k t", k=4)).then_inc(h2T_by_act, 1)
                act.wait_ge(max_ready, i + 1)
                act.activation(expo, logits, ACT.Exp, bias=rstat[:, 0:1]).then_inc(gate_exp, 1)
                if i + 2 < NT:
                    mix_evict(i + 2)
            act.wait_ge(late_loaded[2], 32)
            act.wait_ge(h2_ready, NT)
            act.wait_ge(h2_stored, 16 * NT)
            act.copy(b_in_parts, b_in_rows).then_inc(b_in_rounded, 1)

            def make_hi(p, j):
                act.wait_ge(raw_full[j % RAW], (p * (CHUNKS // RAW) + j // RAW + 1) * 16)
                if not (isinstance(p, int) and p == 0 and j < PARTS):
                    act.wait_ge(chunk_used, CHUNKS * p + j - PARTS + 1)
                act.copy(hi[j % PARTS], raw[j % RAW]).then_inc(hi_made, 1)

            def x_hi(p):
                for a in range(2):
                    act.wait_ge(x_transposed, 2 * p + a + 1)
                    act.copy(xT_hi[:, a * KH:(a + 1) * KH, :], bank[6 + a].rearrange("p (k t) -> p k t", k=KH))\
                        .then_inc(xT_hi_made, 1)

            def sigmoid(p, g):
                act.wait_ge(glu_ready, 4 * p + g + 1)
                act.activation(sig, glu, ACT.Sigmoid, scale=SWI_ALPHA).then_inc(sig_ready, 1)

            def act_hi(p, g):
                act.wait_ge(act_transposed, 4 * p + g + 1)
                act.copy(actT_hi[:, 2 * g:2 * g + 2, :], bank[6 + g % 2][:, 0:256].rearrange("p (k t) -> p k t", k=2))\
                    .then_inc(actT_hi_made, 1)

            def scale_rows(p, f):
                act.wait_ge(chunk_used, CHUNKS * p + IN_CHUNKS + 2 * (f + 1))
                if f == 0:
                    act.wait_ge(cur_ready, p + 1)
                    wait(act, scattered, 16 * p)
                act.activation(y_rows[:, f * GW:(f + 1) * GW], bank[4 + f], ACT.Copy, scale=gate_cur[:, 0:1])\
                    .then_inc(y_scaled, 1)

            def one_pass(p):
                for s in range(CHUNKS):
                    if s % 2 and s < IN_CHUNKS:
                        sigmoid(p, s // 2)
                    if s == 7:
                        act_hi(p, 2)
                    if s == 8:
                        act_hi(p, 3)
                    if s == 9:
                        act.wait_ge(chunk_used, CHUNKS * p + IN_CHUNKS)
                        x_hi(p + 1)
                    if s + AHEAD < CHUNKS:
                        make_hi(p, s + AHEAD)
                    else:
                        make_hi(p + 1, s + AHEAD - CHUNKS)
                    if s in (3, 5):
                        act_hi(p, (s - 3) // 2)
                    if s in (9, 11):
                        scale_rows(p, (s - 9) // 2)

            load_pass_count(act)
            act.wait_ge(wo_done, NT)
            for j in range(AHEAD):
                make_hi(0, j)
            x_hi(0)
            one_pass(0)
            by_pass(act, one_pass)
            for i in range(NT):
                act.wait_ge(sum_ready, TOPK * NT - NT + i + 1)
                act.activation(junk_out, resid[:, i, :], ACT.Square, accum_out=stat[:, 52 + i:53 + i]).then_inc(sum_squared, 1)
                act.wait_ge(sum_squared, i + 1)
                root(52 + i, 1, D, sum_root)

        @block.vector
        def _(dve):
            chain = Chain(dve, dve_step)

            dve.memset(eps_col[:, :], EPS).then_inc(eps_set, 1)
            dve.wait_ge(x_root, 1)
            chain(dve.reciprocal(stat[:, 0:NT], stat[:, 0:NT]))
            chain.settle()
            for i in range(NT):
                dve.tensor_scalar(xn[:, i, :], resid[:, i, :], stat[:, i:i + 1], None, ALU.mult).then_inc(xn_ready, 1)
            dve.wait_ge(small_loaded, 16 * N_SMALL)
            dve.wait_ge(const_loaded, 48)
            chain(dve.tensor_copy(pos_f[:, :], pos_i[:, :]))
            chain.settle()
            for i in range(NT):
                chain(dve.tensor_scalar(ang[:, 0, i, :], cst[:, C_FREQ:C_FREQ + 32], pos_f[:, i:i + 1], None, ALU.mult))
            chain.settle()
            chain(dve.tensor_scalar(ang[:, 1], ang[:, 0], 1.0 / (2 * math.pi), MAGIC, ALU.mult, ALU.add))
            chain.settle()
            chain(dve.tensor_scalar(ang[:, 2], ang[:, 1], -MAGIC, None, ALU.add))
            chain.settle()
            chain(dve.scalar_tensor_tensor(ang[:, 3], ang[:, 2], -TWO_PI_A, ang[:, 0], ALU.mult, ALU.add))
            chain.settle()
            chain(dve.scalar_tensor_tensor(ang[:, 4], ang[:, 2], -TWO_PI_B, ang[:, 3], ALU.mult, ALU.add))
            chain.settle()
            chain(dve.scalar_tensor_tensor(ang[:, 1], ang[:, 2], -TWO_PI_C, ang[:, 4], ALU.mult, ALU.add))
            chain.settle()
            dve.tensor_scalar(ang[:, 3], ang[:, 1], PI_F, -PI_F, ALU.min, ALU.max).then_inc(ang_ready, 1)
            dve.wait_ge(ang_ready, 1)
            chain(dve.scalar_tensor_tensor(ang[:, 4], ang[:, 3], -1.0, ang[:, 3], ALU.mult, ALU.max))
            chain.settle()
            dve.tensor_scalar(ang[:, 5], ang[:, 4], -1.0, math.pi / 2, ALU.mult, ALU.add).then_inc(ang_ready, 1)
            for k in range(1, KT, 2):
                dve.wait_ge(xn_transposed, k + 1)
                dve.tensor_scalar(hT[:, k, :], bank[k], g1_col[:, k:k + 1], None, ALU.mult).then_inc(hT_by_dve, 1)
            chain(dve.tensor_tensor(lam_rows[:, 0::2], lam_rows[:, 0::2], lam_rows[:, 1::2], ALU.mult))
            chain.settle()
            dve.tensor_reduce(lam[:, 0:2], lam_rows[:, 0::2], AX_X, ALU.add).then_inc(lam_dots, 1)
            dve.tensor_copy(ident_bf[:, :], cst[:, C_IDENT:C_IDENT + P]).then_inc(cast_done, 1)
            dve.tensor_copy(causal_bf[:, :], raw_masks[:, 0:P]).then_inc(cast_done, 1)
            dve.tensor_copy(utri_bf[:, :], raw_masks[:, P:2 * P]).then_inc(cast_done, 1)
            dve.memset(ones_bf[:, :], 1.0).then_inc(cast_done, 1)
            dve.wait_ge(lam_exp, 1)
            chain(dve.tensor_tensor(lam[:, 4:5], lam[:, 3:4], lam[:, 2:3], ALU.subtract))
            chain.settle()
            chain(dve.tensor_scalar(lam[:, 5:6], lam[:, 4:5], -LAM_INIT, None, ALU.add))
            chain.settle()

            def rotary(c):
                cols = proj[:, :, c * CW:(c + 1) * CW].rearrange("p i (g a f) -> p i g a f", g=4, a=2)
                halves = [cols[:, :, :, a, :] for a in range(2)]
                cos, sin = (cos_sin[:, n].unsqueeze(2).to_broadcast([P, NT, 4, 32]) for n in range(2))
                dve.wait_ge(proj_by_act, 2 * (c + 1))
                dve.wait_ge(proj_by_dve, 2 * (c + 1))
                dve.wait_ge(trig_ready, 2)
                for n, (half, trig) in enumerate(((0, cos), (1, sin), (1, cos), (0, sin))):
                    chain(dve.tensor_tensor(rope_tmp[:, n], halves[half], trig, ALU.mult))
                chain.settle()
                chain(dve.tensor_tensor(halves[0], rope_tmp[:, 0], rope_tmp[:, 1], ALU.subtract))
                dve.tensor_tensor(halves[1], rope_tmp[:, 2], rope_tmp[:, 3], ALU.add).then_inc(rope_done, 1)
                chain.settle()

            for c in range(NCHUNK):
                for i in range(1, NT, 2):
                    u = c * NT + i
                    dve.wait_ge(proj_ready, u + 1)
                    dve.tensor_copy(proj[:, i, c * CW:(c + 1) * CW], bank[u % 4][:, 0:CW]).then_inc(proj_by_dve, 1)
                if c in ROPE_CHUNKS:
                    rotary(c)
            for g in range(1, 12, 2):
                dve.wait_ge(qk_transposed, g + 1)
                dve.tensor_copy(qkT[:, g, :], bank[4 + g % 4]).then_inc(qk_by_dve, 1)

            def maxima(u):
                b, n = u % 2, (u // NH + 1) * P
                dve.wait_ge(scores_ready, u + 1)
                chain(dve.tensor_reduce(row_max[:, b, :], pair[b][:, :, 0:n], AX_X, ALU.max))
                chain.settle()
                if u >= 2:
                    dve.wait_ge(exp_done, 2 * (u - 1))
                dve.tensor_scalar(row_bias[:, b, :], row_max[:, b, :], -SCALE, None, ALU.mult).then_inc(bias_ready, 1)

            def difference(u):
                b, n = u % 2, (u // NH + 1) * P
                dve.wait_ge(exp_done, 2 * (u + 1))
                chain(dve.reciprocal(row_rec[:, b, :], row_sum[:, b, :]))
                chain.settle()
                chain(dve.tensor_tensor(row_rec[:, b, 1:2], row_rec[:, b, 1:2], lam[:, 5:6], ALU.mult))
                chain.settle()
                chain(dve.tensor_scalar(probs[:, b, 1, 0:n], probs[:, b, 1, 0:n], row_rec[:, b, 1:2], None, ALU.mult))
                chain.settle()
                dve.scalar_tensor_tensor(probs[:, b, 0, 0:n], probs[:, b, 0, 0:n], row_rec[:, b, 0:1],
                                         probs[:, b, 1, 0:n], ALU.mult, ALU.add).then_inc(att_ready, 1)

            NU = NT * NH
            for s in range(NU + 1):
                if s < NU:
                    maxima(s)
                if s >= 1:
                    difference(s - 1)
            dve.wait_ge(av_ready, NU)
            for a in range(2):
                dve.tensor_tensor(qdT[:, a, :].rearrange("p (i t) -> p i t", i=NT),
                                  qkT[:, 8 + a, :].rearrange("p (i t) -> p i t", i=NT),
                                  cst[:, C_QDEC + a * P:C_QDEC + (a + 1) * P].unsqueeze(1).to_broadcast([P, NT, P]),
                                  ALU.mult).then_inc(qd_ready, 1)
            for i in range(NT):
                dve.wait_ge(ret_scores, i + 1)
                if i >= 2:
                    dve.wait_ge(ret_out, i - 1)
                dve.tensor_tensor(st_s[:, i % 2].rearrange("p r a n -> p r (a n)"), pair[i % 2][:, :, 0:256],
                                  cst[:, C_DECAY:C_DECAY + 512].rearrange("p (r n) -> p r n", r=2), ALU.mult)\
                    .then_inc(ret_decayed, 1)
                if i >= 1:
                    j = i - 1
                    dve.wait_ge(ret_kv, j + 1)
                    for a in range(2):
                        kv = pair[j % 2][:, 0, 256 + a * P:256 + (a + 1) * P]
                        if j == 0:
                            dve.tensor_copy(state[:, a, :], kv).then_inc(state_ready, 1)
                        else:
                            dve.wait_ge(state_ready, 2 * j)
                            dve.scalar_tensor_tensor(state[:, a, :], state[:, a, :], chunk_decay[:, a:a + 1], kv,
                                                     ALU.mult, ALU.add).then_inc(state_ready, 1)
            dve.wait_ge(mix_gained, 2 * NT)
            dve.wait_ge(head_root_ready, 1)
            chain(dve.reciprocal(stat[:, 16:48], stat[:, 16:48]))
            chain.settle()
            head_root = stat[:, 16:48].rearrange("p (i h) -> p i h", i=NT)
            chain(dve.tensor_scalar(head_root[:, :, 0:NH], head_root[:, :, 0:NH], 1.0 - LAM_INIT, None, ALU.mult))
            chain.settle()

            def mix_norm(i):
                m = mix[:, i, :].rearrange("p (h c) -> p h c", h=2 * NH)
                dve.tensor_tensor(m, m, head_root[:, i, :].unsqueeze(2).to_broadcast([P, 2 * NH, P]), ALU.mult)\
                    .then_inc(mix_ready, 1)

            def mix_evict(i):
                dve.wait_ge(mix_transposed, 2 * i + 2)
                dve.tensor_copy(mixT[:, i % 2, 4:8, :], bank[1].rearrange("p (k t) -> p k t", k=4)).then_inc(mixT_by_dve, 1)

            for i in range(NT):
                mix_norm(i)
            mix_evict(0)
            mix_evict(1)
            dve.wait_ge(tokens_named, 5)
            for i in range(NT):
                dve.wait_ge(wo_done, i + 1)
                for f in range(2):
                    half = resid[:, i, f * 512:(f + 1) * 512]
                    dve.tensor_tensor(half, half, pair[1 + i % 2][:, f, :], ALU.add).then_inc(x2_ready, 1)
                dve.wait_ge(x2_root, i + 1)
                chain(dve.reciprocal(stat[:, 48 + i:49 + i], stat[:, 48 + i:49 + i]))
                chain.settle()
                if i == 0:
                    dve.wait_ge(late_loaded[0], 16)
                dve.scalar_tensor_tensor(h2_row[:, i, :].rearrange("p (a c) -> p a c", a=NT),
                                         resid[:, i, :].rearrange("p (a c) -> p a c", a=NT),
                                         stat[:, 48 + i:49 + i], g2_row, ALU.mult, ALU.mult).then_inc(h2_ready, 1)
                dve.wait_ge(h2_transposed, 2 * i + 2)
                dve.tensor_copy(mixT[:, i % 2, 4:8, :], bank[7].rearrange("p (k t) -> p k t", k=4)).then_inc(h2T_by_dve, 1)
                dve.wait_ge(logits_ready, i + 1)
                if i:
                    dve.wait_ge(gate_exp, i)
                dve.tensor_tensor(logits, bank[6][:, 0:NE], b_router_row[:, :], ALU.add).then_inc(logits_read, 1)
                dve.wait_ge(logits_read, i + 1)
                chain(dve.max(top8, logits))
                chain.settle()
                dve.tensor_scalar(rstat[:, 0:1], top8[:, 0:1], -1.0, None, ALU.mult).then_inc(max_ready, 1)
                if i + 2 < NT:
                    mix_evict(i + 2)
                chain(dve.max_index(top8_i, top8, logits))
                chain.settle()
                chain(dve.tensor_copy(top8_f, top8_i))
                chain.settle()
                for k in range(TOPK):
                    if k == 0:
                        chain(dve.tensor_scalar(picked[:, i, :], expert_id, top8_f[:, 0:1], None, ALU.is_equal))
                    else:
                        chain(dve.scalar_tensor_tensor(picked[:, i, :], expert_id, top8_f[:, k:k + 1], picked[:, i, :],
                                                       ALU.is_equal, ALU.add))
                    chain.settle()
                dve.tensor_copy(picked_bf[:, i, :], picked[:, i, :]).then_inc(picked_ready, 1)
                dve.wait_ge(gate_exp, i + 1)
                chain(dve.tensor_tensor(gates[:, i, :], expo, picked[:, i, :], ALU.mult))
                chain(dve.tensor_tensor_scan(rank, ones_row, picked[:, i, :], 0.0, ALU.mult, ALU.add))
                chain.settle()
                chain(dve.tensor_reduce(rstat[:, 1:2], gates[:, i, :], AX_X, ALU.add))
                chain(dve.tensor_tensor(rank, rank, picked[:, i, :], ALU.subtract))
                chain.settle()
                chain(dve.reciprocal(rstat[:, 2:3], rstat[:, 1:2]))
                chain(dve.tensor_scalar(route[:, i, :, 0], rank, token_id[:, i:i + 1], -NOWHERE, ALU.add, ALU.add))
                chain(dve.tensor_scalar(route[:, i, :, 1], ones_row, token_id[:, i:i + 1], 1.0 / TOPK, ALU.mult, ALU.mult))
                chain(dve.tensor_scalar(route[:, i, :, 3], ones_row, 0.0, None, ALU.mult))
                chain.settle()
                chain(dve.tensor_scalar(gates[:, i, :], gates[:, i, :], rstat[:, 2:3], None, ALU.mult))
                chain.settle()
                chain(dve.tensor_copy(route[:, i, :, 2], gates[:, i, :]))
                dve.wait_ge(place_ready, i + 1)
                dve.scalar_tensor_tensor(slot_of[:, i, :], bank[7][:, 0:NE], 1.0, picked[:, i, :], ALU.add, ALU.mult)\
                    .then_inc(place_read, 1)
                dve.wait_ge(place_read, i + 1)
                chain(dve.tensor_scalar(slot_of[:, i, :], slot_of[:, i, :], -1.0, None, ALU.add))
                chain.settle()
            dve.wait_ge(place_ready, NT + 1)
            dve.tensor_copy(expert_count, bank[7][:, 64:64 + NE]).then_inc(table_ready, 1)
            dve.wait_ge(table_ready, 1)
            chain(dve.tensor_scalar(n_passes, expert_count, 0.0, None, ALU.is_gt))
            chain.settle()
            for n in range(SLOTS, SEQ, SLOTS):
                chain(dve.scalar_tensor_tensor(n_passes, expert_count, float(n), n_passes, ALU.is_gt, ALU.add))
                chain.settle()
            chain(dve.tensor_tensor_scan(cum_passes, ones_row, n_passes, 0.0, ALU.mult, ALU.add))
            chain.settle()
            chain(dve.tensor_copy(passes_upto[:, :], cum_passes[0:1, :]))
            chain(dve.tensor_scalar(scatters_upto, cum_passes[0:1, :], 16.0, None, ALU.mult))
            dve.wait_ge(h2_ready, NT)
            up_to = cum_passes.unsqueeze(1).to_broadcast([P, MAX_PASSES + 1, NE])
            chain(dve.tensor_tensor(earlier, pass_id.unsqueeze(2).to_broadcast([P, MAX_PASSES + 1, NE]), up_to,
                                    ALU.is_ge))
            chain.settle()
            chain(dve.tensor_reduce(pass_e, earlier, AX_X, ALU.add))
            chain.settle()
            chain(dve.tensor_tensor(earlier, earlier, up_to, ALU.mult))
            chain.settle()
            chain(dve.tensor_reduce(pass_first, earlier, AX_X, ALU.max))
            chain.settle()
            chain(dve.tensor_tensor(pass_first, pass_id, pass_first, ALU.subtract))
            chain.settle()
            chain(dve.tensor_scalar(pass_first, pass_first, float(SLOTS), None, ALU.mult))
            chain.settle()
            dve.tensor_scalar(pass_expert[:, :], pass_e[0:1, :], float(NE - 1), None, ALU.min).then_inc(table_ready, 1)
            dve.wait_ge(table_ready, 2)

            def of(ap, e):
                return ap[:, :, e:e + 1] if isinstance(e, int) else ap[:, :, bass.ds(e, 1)]

            def expert_of(p):
                return dve.value_load(at(pass_expert, p), min_val=0, max_val=NE - 1)

            def col(m, n):
                return m[:, n:n + 1] if isinstance(n, int) else m[:, bass.ds(n, 1)]

            def slots_one_hot(p, e):
                wait(dve, list_ready, p)
                chain(dve.tensor_copy(first_cur[:, :], col(pass_first, p)))
                chain(dve.tensor_copy(pos_cur[:, :].unsqueeze(2), of(slot_of, e)))
                chain(dve.tensor_copy(route_cur.unsqueeze(2), of(route, e)))
                chain.settle()
                for i in range(NT):
                    ins = dve.tensor_scalar(onehot[:, i, :], slot_id, first_cur[:, 0:1], pos_cur[:, i:i + 1],
                                            ALU.add, ALU.is_equal)
                    if i < NT - 1:
                        chain(ins)
                chain.settle()
                ins.then_inc(onehot_ready, 1)

            def read_list(p):
                dve.wait_ge(list_ready, p + 1)
                wait(dve, gathered, 16 * p)
                chain(dve.tensor_scalar(dest_next[:, :], bank[5][:, 0:1], NOWHERE, None, ALU.add))
                chain(dve.tensor_copy(gate_next[:, :], bank[5][:, 2:3]))
                chain.settle()
                dve.tensor_copy(token_next[:, :], bank[5][:, 1:2]).then_inc(idx_ready, 1)

            def pick(p, e):
                wait(dve, chunk_used, CHUNKS * (p - 1) + IN_CHUNKS)
                for n in range(2):
                    rows = slice(n * NE, (n + 1) * NE)
                    at_e = cst[rows, C_IDENT + n * NE:C_IDENT + (n + 1) * NE]
                    dve.tensor_copy(pick_bias[rows, :], col(at_e, e).to_broadcast([NE, SLOTS])).then_inc(pick_ready, 1)

            def make_lo(p, j):
                dve.wait_ge(hi_made, CHUNKS * p + j + 1)
                dve.tensor_tensor(lo[j % PARTS][:, 0:DVE_K, :], raw[j % RAW][:, 0:DVE_K, :],
                                  hi[j % PARTS][:, 0:DVE_K, :].bitcast(F32), ALU.subtract).then_inc(lo_by_dve, 1)

            def x_lo(p):
                for a in range(2):
                    dve.wait_ge(xT_hi_made, 2 * p + a + 1)
                    tiles = slice(a * KH, (a + 1) * KH)
                    dve.tensor_tensor(xT_lo[:, tiles, :], bank[6 + a].rearrange("p (k t) -> p k t", k=KH),
                                      xT_hi[:, tiles, :].bitcast(F32), ALU.subtract).then_inc(xT_lo_made, 1)

            def swiglu(p, g):
                n = 4 * p + g
                h = bank[g].rearrange("p (c a) -> p a c", a=2)
                dve.wait_ge(chunk_used, CHUNKS * p + 2 * g + 2)
                dve.tensor_scalar(glu, h[:, 0, :], LIMIT, None, ALU.min).then_inc(glu_ready, 1)
                dve.tensor_scalar(lin, h[:, 1, :], LIMIT, -LIMIT, ALU.min, ALU.max).then_inc(h_read, 1)
                dve.wait_ge(sig_ready, n + 1)
                chain(dve.tensor_tensor(gs, glu, sig, ALU.mult))
                chain.settle()
                dve.wait_ge(h_read, n + 1)
                wait(dve, act_transposed, n - 1)
                dve.scalar_tensor_tensor(act_rows[:, g % 2, :], lin, 1.0, gs, ALU.add, ALU.mult)\
                    .then_inc(act_ready, 1)
                dve.wait_ge(act_ready, n + 1)

            def act_lo(p, g):
                dve.wait_ge(actT_hi_made, 4 * p + g + 1)
                tiles = slice(2 * g, 2 * g + 2)
                dve.tensor_tensor(actT_lo[:, tiles, :], bank[6 + g % 2][:, 0:256].rearrange("p (k t) -> p k t", k=2),
                                  actT_hi[:, tiles, :].bitcast(F32), ALU.subtract).then_inc(actT_lo_made, 1)

            def one_pass(p):
                following = expert_of(p + 1)
                for s in range(CHUNKS):
                    if s % 2 and s < IN_CHUNKS:
                        swiglu(p, s // 2)
                    if s == 7:
                        act_lo(p, 2)
                    if s == 8:
                        act_lo(p, 3)
                    if s == 9:
                        x_lo(p + 1)
                    if s + AHEAD < CHUNKS:
                        make_lo(p, s + AHEAD)
                    else:
                        make_lo(p + 1, s + AHEAD - CHUNKS)
                    if s in (3, 5):
                        act_lo(p, (s - 3) // 2)
                    if s == 0:
                        slots_one_hot(p + 1, following)
                    if s == 4:
                        wait(dve, scattered, 16 * p)
                        wait(dve, y_scaled, 2 * p)
                        chain(dve.tensor_copy(dest_cur[:, :], dest_next[:, :]))
                        dve.tensor_copy(gate_cur[:, :], gate_next[:, :]).then_inc(cur_ready, 1)
                        chain.settle()
                        dve.wait_ge(cur_ready, p + 1)
                        read_list(p + 1)
                    if s == 8:
                        pick(p + 1, following)

            dve.wait_ge(b_in_rounded, 1)
            low = slice(NE, 2 * NE)
            dve.tensor_tensor(b_in_parts[low, :], b_in_rows[low, :], b_in_parts[low, :].bitcast(F32), ALU.subtract)\
                .then_inc(b_in_split, 1)
            first = expert_of(0)
            slots_one_hot(0, first)
            pick(0, first)
            dve.wait_ge(gates_transposed, 1)
            dve.tensor_copy(gateT, bank[3][0:NE, :]).then_inc(gateT_ready, 1)
            read_list(0)
            for i in range(NT):
                for f in range(2):
                    n = 2 * i + f
                    dve.wait_ge(bias_out_product, n + 1)
                    half = resid[:, i, f * 512:(f + 1) * 512]
                    dve.tensor_tensor(half, half, bank[4 + n % 2], ALU.add).then_inc(bias_out_ready, 1)
            load_pass_count(dve)
            for j in range(AHEAD):
                make_lo(0, j)
            x_lo(0)
            one_pass(0)
            start = chain.n
            chain.n = 0

            def counted_pass(p):
                chain.before = start + (p - 1) * STEPS_PER_PASS
                one_pass(p)
                assert chain.n == STEPS_PER_PASS, chain.n

            by_pass(dve, counted_pass)
            chain = Chain(dve, tail_step)
            for r in range(TOPK):
                dve.wait_ge(parts_loaded[r], 16)
                for i in range(NT):
                    if r:
                        dve.wait_ge(sum_ready, (r - 1) * NT + i + 1)
                    else:
                        dve.wait_ge(bias_out_ready, 2 * NT)
                    dve.tensor_tensor(resid[:, i, :], resid[:, i, :], parts[r][:, i, :], ALU.add).then_inc(sum_ready, 1)
            dve.wait_ge(gf_loaded, 16)
            for i in range(NT):
                dve.wait_ge(sum_root, i + 1)
                chain(dve.reciprocal(stat[:, 52 + i:53 + i], stat[:, 52 + i:53 + i]))
                chain.settle()
                dve.scalar_tensor_tensor(parts[0][:, i, :], resid[:, i, :], stat[:, 52 + i:53 + i], gf_row,
                                         ALU.mult, ALU.mult).then_inc(out_ready, 1)

        @block.gpsimd
        def _(pool):
            pool.wait_ge(qk_transposed, 12)
            pool.wait_ge(const_loaded, 48)
            for h in range(NH):
                k_rows = proj[:, :, CRK + h * DQ:CRK + (h + 1) * DQ]
                pool.tensor_scalar(k_rows, k_rows, cst[:, C_KDEC + h:C_KDEC + h + 1], None, ALU.mult).then_inc(k_scaled, 1)
            for i in range(NT):
                g = proj[:, i, CRG:PROJ]
                pool.wait_ge(silu_sig, i + 1)
                pool.tensor_tensor(g, g, mix[:, i, 512:D], ALU.mult).then_inc(silu_done, 1)
                pool.wait_ge(silu_done, 2 * i + 1)
                pool.wait_ge(small_loaded, 16 * N_SMALL)
                pool.tensor_tensor(g, g, gain_row[:, 512:D], ALU.mult).then_inc(silu_done, 1)
            for i in range(NT):
                pool.wait_ge(av_evicted, i + 1)
                pool.tensor_tensor(mix[:, i, 0:512], mix[:, i, 0:512], gain_row[:, 0:512], ALU.mult).then_inc(mix_gained, 1)
            pool.wait_ge(silu_done, 2 * NT)
            for i in range(NT):
                pool.wait_ge(ret_evicted, i + 1)
                pool.tensor_tensor(mix[:, i, 512:D], mix[:, i, 512:D], proj[:, i, CRG:PROJ], ALU.mult).then_inc(mix_gained, 1)
            pool.wait_ge(mix_gained, 2 * NT)
            pool.wait_ge(ret_out, NT)
            pool.dma_start(g2_row, for_all_partitions(norm2_g[0]).rearrange("p (a c) -> p a c", a=NT))\
                .then_inc(late_loaded[0], 16)
            pool.dma_start(w_router_sb, w_router.rearrange("a (k p) e -> (a p) k e", p=P)).then_inc(late_loaded[1], 16)
            for n in range(2):
                pool.dma_start(b_in_rows[n * NE:(n + 1) * NE, :], b_moe_in[0]).then_inc(late_loaded[2], 16)
            pool.dma_start(b_out_rows, b_moe_out[0]).then_inc(late_loaded[3], 16)
            pool.iota(token_id, [[TOPK * P, NT]], base=0, channel_multiplier=TOPK,
                      allow_small_or_imprecise_dtypes=True).then_inc(tokens_named, 1)
            pool.iota(expert_id, [[1, NE]], base=0, channel_multiplier=0,
                      allow_small_or_imprecise_dtypes=True).then_inc(tokens_named, 1)
            pool.iota(slot_id, [[1, SLOTS]], base=0, channel_multiplier=0,
                      allow_small_or_imprecise_dtypes=True).then_inc(tokens_named, 1)
            pool.iota(pass_id, [[1, MAX_PASSES + 1]], base=0, channel_multiplier=0,
                      allow_small_or_imprecise_dtypes=True).then_inc(tokens_named, 1)
            pool.memset(ones_row, 1.0).then_inc(tokens_named, 1)
            pool.wait_ge(logits_ready, NT)
            pool.wait_ge(h2_stored, 16 * NT)
            pool.dma_start(gf_row, for_all_partitions(norm_f_g)).then_inc(gf_loaded, 16)


            def make_lo(p, j):
                pool.wait_ge(hi_made, CHUNKS * p + j + 1)
                pool.tensor_tensor(lo[j % PARTS][:, DVE_K:KH, :], raw[j % RAW][:, DVE_K:KH, :],
                                   hi[j % PARTS][:, DVE_K:KH, :].bitcast(F32), ALU.subtract).then_inc(lo_by_pool, 1)

            def gather(p):
                pool.wait_ge(idx_ready, p + 1)
                wait(pool, x_transposed, 2 * p)
                pool.sem_inc(pool_passed, 1)
                pool.indirect_dma_start(out=x_rows, out_offset=None, in_=h2_dram,
                                        in_offset=bass.IndirectOffsetOnAxis(ap=token_next[:, 0:1], axis=0))\
                    .then_inc(gathered, 16)

            def scatter(p):
                pool.wait_ge(y_scaled, 2 * (p + 1))
                pool.sem_inc(pool_passed, 1)
                pool.indirect_dma_start(out=y_dram, in_=y_rows, in_offset=None,
                                        out_offset=bass.IndirectOffsetOnAxis(ap=dest_cur[:, 0:1], axis=0),
                                        bounds_check=SEQ * TOPK - 1, oob_is_err=False).then_inc(scattered, 16)

            def one_pass(p):
                for s in range(CHUNKS):
                    if s + AHEAD < CHUNKS:
                        make_lo(p, s + AHEAD)
                    else:
                        make_lo(p + 1, s + AHEAD - CHUNKS)
                    if s == 5:
                        gather(p + 1)
                scatter(p)

            gather(0)
            load_pass_count(pool)
            for j in range(AHEAD):
                make_lo(0, j)
            one_pass(0)
            by_pass(pool, one_pass)


_INS = ["x", "positions", "norm1_g", "w_in", "lambda_q1", "lambda_k1", "lambda_q2", "lambda_k2", "diff_norm_g",
        "ret_norm_g", "w_o", "norm2_g", "w_router", "b_router", "w_moe_in", "b_moe_in", "w_moe_out", "b_moe_out",
        "norm_f_g"]


def kernel(**inputs):
    import numpy as _np
    import concourse.bacc as _bacc
    from concourse import mybir as _mybir
    from concourse.bass_utils import run_bass_kernel_spmd as _run

    nc = _bacc.Bacc("TRN2", target_bir_lowering=False, num_devices=1)
    arrays, args = {}, []
    for name in _INS:
        a = _np.ascontiguousarray(inputs[name])
        arrays[f"in_{name}"] = a
        args.append(nc.dram_tensor(f"in_{name}", a.shape, _mybir.dt.from_np(a.dtype), kind="ExternalInput").ap())
    out = nc.dram_tensor("out", (1, SEQ, D), F32, kind="ExternalOutput").ap()
    build(nc, *args, out)
    r = _run(nc, [arrays], core_ids=[0])
    return r.results[0]["out"]
```

```python
from contextlib import ExitStack
import math

import numpy as np

import concourse.bass as bass
from concourse import mybir

F32 = mybir.dt.float32
F32R = mybir.dt.float32r
BF16 = mybir.dt.bfloat16
I32 = mybir.dt.int32
U32 = mybir.dt.uint32
ALU = mybir.AluOpType
ACT = mybir.ActivationFunctionType
AX_X = mybir.AxisListType.X

P = 128
SEQ = 512
D = 1024
NT = SEQ // P
KT = D // P
PROJ = 3072
EPS = 1e-5
CW = 256
NCHUNK = PROJ // CW
CQ, CK, CV, CRQ, CRK, CRV, CRG = 0, 512, 1024, 1536, 1792, 2048, 2560
NH = 4
DQ = 64
SCALE = DQ ** -0.5
LAM_INIT = 0.8 - 0.6 * math.exp(-0.3 * 0)
NE = 32
TOPK = 4
FF = 1024
LIMIT = 7.0
SWI_ALPHA = 1.702
RING = 12
W_RAW = 5
W_DVE_K = 6
OUT_CHUNKS = D // CW
N_SMALL = 12
GW = 512
KH = KT // 2
CHUNKS = 12
IN_CHUNKS = 8
RAW = 6
PARTS = 3
DVE_K = 3
SLOTS = P
MAX_PASSES = SEQ * TOPK // SLOTS + NE - 1
AHEAD = 3
LO_AHEAD = 2
STEPS_PER_PASS = 13
NOWHERE = float(2 * TOPK * SEQ)
ROPE_CHUNKS = (0, 1, 2, 3, 6, 7)
TWO_PI_A = 6.28125
TWO_PI_B = round((2 * math.pi - TWO_PI_A) * 2.0 ** 20) / 2.0 ** 20
TWO_PI_C = 2 * math.pi - TWO_PI_A - TWO_PI_B
PI_F = 3.1415925
MAGIC = 12582912.0
MASKED = -1.0e30

C_IDENT, C_DECAY, C_QDEC, C_KDEC, C_FREQ = 0, 128, 640, 896, 900
C_N = 932


def shape_constants():
    f = np.float32
    c = np.zeros((P, C_N), f)
    r = np.arange(P)
    c[:, C_IDENT:C_IDENT + P] = np.eye(P)
    masks = np.concatenate([np.where(r[None, :] <= r[:, None], 0.0, MASKED), r[:, None] < r[None, :]], axis=1)
    log_decay = np.log(f(1.0) - f(2.0) ** (f(-5.0) - np.arange(NH, dtype=f))).astype(f)
    for h in range(NH):
        rel = (r[None, :] - r[:, None]).astype(f)
        at = C_DECAY + ((h % 2) * 2 + h // 2) * P
        c[:, at:at + P] = np.where(
            rel >= 0, np.exp(log_decay[h] * np.maximum(rel, 0)), 0.0) * SCALE
        rows = slice(64 * (h % 2), 64 * (h % 2) + 64)
        c[rows, C_QDEC + (h // 2) * P:C_QDEC + (h // 2 + 1) * P] = np.exp(log_decay[h] * (r[None, :] + f(1.0)))
        c[:, C_KDEC + h] = np.exp(log_decay[h] * (P - 1 - r)) * SCALE
    c[:, C_FREQ:C_FREQ + 32] = (f(1.0) / (f(10000.0) ** (np.arange(0, DQ, 2, dtype=f) / f(DQ))))[None, :]
    chunk = np.exp(log_decay * P).astype(f)
    return c, masks.astype(f), np.stack([np.repeat(chunk[0:2], 64), np.repeat(chunk[2:4], 64)], axis=1).astype(f)


def build(nc, x, positions, norm1_g, w_in, lambda_q1, lambda_k1, lambda_q2, lambda_k2, diff_norm_g,
          ret_norm_g, w_o, norm2_g, w_router, b_router, w_moe_in, b_moe_in, w_moe_out, b_moe_out,
          norm_f_g, out):
    ctx = ExitStack()
    with ctx:
        def sb(name, shape, dt=F32):
            return ctx.enter_context(nc.sbuf_tensor(name, shape, dt))

        def sem(name):
            return ctx.enter_context(nc.semaphore(name))

        def sems(name, n):
            return [sem(f"{name}{i}") for i in range(n)]

        def wait(eng, semaphore, value):
            if not (isinstance(value, int) and value <= 0):
                eng.wait_ge(semaphore, value)

        consts_np, masks_np, chunk_decay_np = shape_constants()
        consts_dram = nc.inline_tensor(consts_np, "shape_consts").ap()
        masks_dram = nc.inline_tensor(masks_np, "shape_masks").ap()
        chunk_decay_dram = nc.inline_tensor(chunk_decay_np, "chunk_decays").ap()
        h2_dram = nc.dram_tensor("h2_rows", [SEQ, D], F32, kind="Internal").ap()
        y_dram = nc.dram_tensor("expert_rows", [SEQ * TOPK, D], F32, kind="Internal").ap()

        ring = sb("ring", [P, RAW, KT, CW])
        with nc.sbuf_tensor("late_ring", [P, RING - RAW, KT, CW], F32) as late_ring:
            pass
        split = sb("split", [P, 2 * PARTS, KH * GW], F32R)
        resid = sb("resid", [P, NT, D])
        cst = sb("cst", [P, C_N])
        cos_sin = sb("cos_sin", [P, 2, NT, 32])
        gain_row = sb("gain_row", [P, D])
        ident_bf = sb("ident_bf", [P, P], BF16)
        causal_bf = sb("causal_bf", [P, P], BF16)
        utri_bf = sb("utri_bf", [P, P], BF16)
        ones_bf = sb("ones_bf", [P, P], BF16)
        g1_col = sb("g1_col", [P, KT])
        pos_i = sb("pos_i", [P, NT], I32)
        pos_f = sb("pos_f", [P, NT])
        lam = sb("lam", [P, 8])
        chunk_decay = sb("chunk_decay", [P, 2])
        b_router_row = sb("b_router_row", [P, NE])
        stat = sb("stat", [P, 56])
        eps_col = sb("eps_col", [P, 1])
        row_max = sb("row_max", [P, 2, 2])
        row_bias = sb("row_bias", [P, 2, 2])
        row_sum = sb("row_sum", [P, 2, 2])
        row_rec = sb("row_rec", [P, 2, 2])
        pass_expert = sb("pass_expert", [1, MAX_PASSES + 1], I32)
        passes_upto = sb("passes_upto", [1, NE], I32)
        pos_cur = sb("pos_cur", [P, NT])
        first_cur = sb("first_cur", [P, 1])
        dest_next = sb("dest_next", [P, 1], I32)
        dest_cur = sb("dest_cur", [P, 1], I32)
        token_next = sb("token_next", [P, 1], I32)
        gate_next = sb("gate_next", [P, 1])
        gate_cur = sb("gate_cur", [P, 1])

        with nc.sbuf_tensor("work", [P, 21504], F32) as work:
            pass
        operands = sb("operands", [P, 20480], F32R)

        def slot(n):
            return ring[:, n] if n < RAW else late_ring[:, n - RAW]

        def w(a, n, rows=P):
            return work[0:rows, a:a + n]

        proj = w(0, NT * PROJ).rearrange("p (i c) -> p i c", i=NT)
        xn = w(4096, NT * D).rearrange("p (i c) -> p i c", i=NT)
        junk1 = w(0, NT * D).rearrange("p (i c) -> p i c", i=NT)
        hT_hi, hT_lo = (operands[:, a:a + KT * SEQ].rearrange("p (k t) -> p k t", k=KT) for a in (12288, 16384))
        w_hi, w_lo = ([split[:, s].rearrange("p (k c) -> p k c", c=CW) for s in range(a, a + PARTS)]
                      for a in (0, PARTS))
        rope_space = ring[:, W_RAW].rearrange("p k c -> p (k c)")
        qkT = w(12288, 12 * SEQ).rearrange("p (g t) -> p g t", g=12)
        rope_tmp = rope_space.rearrange("p (a i g f) -> p a i g f", a=4, i=NT, g=4)
        ang = rope_space[:, 0:6 * 128].rearrange("p (a i f) -> p a i f", a=6, i=NT)
        lam_rows = rope_space[:, 1024:1024 + 4 * DQ].rearrange("p (a d) -> p a d", a=4)
        raw_masks = w(20480, 2 * P)
        probs = w(18432, 2 * 2 * SEQ).rearrange("p (b m t) -> p b m t", b=2, m=2)
        attT = w(20480, 2 * SEQ).rearrange("p (b t) -> p b t", b=2)
        mix = proj[:, :, 0:D]
        square_tmp = proj[:, :, CRQ:CRQ + P]
        g2_row = proj[:, :, CRQ:CRQ + 256]
        st_s = w(18432, 2 * 512).rearrange("p (b r a n) -> p b r a n", b=2, r=2, a=2)
        state = w(19456, 2 * P).rearrange("p (a n) -> p a n", a=2)
        qdT = w(20480, 2 * SEQ).rearrange("p (a t) -> p a t", a=2)
        mixT = w(12288, 2 * D).rearrange("p (b k t) -> p b k t", b=2, k=KT)
        b_in_rows = w(14336, 2 * FF, 2 * NE)
        w_router_sb = w(16384, KT * NE).rearrange("p (k e) -> p k e", k=KT)
        junk2 = w(16896, D)
        h2_row = proj[:, :, 0:D]
        b_out_rows = w(11008, D, NE)
        gateT = w(7168, SEQ, NE)
        route = w(18944, NT * NE * 4).rearrange("p (i e c) -> p i e c", i=NT, e=NE)
        slot_of = w(19456, NT * NE).rearrange("p (i e) -> p i e", i=NT)
        pass_first = w(19584, MAX_PASSES + 1)
        cum_passes = w(19680, NE)
        n_passes = w(19712, NE)
        expert_count = w(19744, NE)
        scatters_upto = w(19824, NE, 1).bitcast(I32)
        earlier = w(7680, NE)
        pass_col = w(7712, 4)
        pass_diag = w(7744, MAX_PASSES + 1).bitcast(BF16).rearrange("p (a n) -> p a n", a=2)
        logits = w(20096, NE)
        top8 = w(20128, 8)
        top8_f = w(20136, 8)
        top8_i = w(20144, 8).bitcast(U32)
        picked = w(20160, NT * NE).rearrange("p (i e) -> p i e", i=NT)
        expo = w(20288, NE)
        gates = w(20320, NT * NE).rearrange("p (i e) -> p i e", i=NT)
        rank = w(20448, NE)
        picked_bf = w(20480, NT * NE // 2).bitcast(BF16).rearrange("p (i e) -> p i e", i=NT)
        ones_row = w(20544, NE)
        token_id = w(20576, NT)
        expert_id = w(20608, NE)
        rstat = w(20640, 16)
        route_cur = w(20672, NT * 4).rearrange("p (i c) -> p i c", i=NT)
        slot_id = w(20992, SLOTS)
        pass_number = w(21120, 1)
        junk_out = w(8192, D)
        def halves(a):
            return operands[:, a:a + KT * SLOTS].rearrange("p (k t) -> p k t", k=KT)

        xT_hi, xT_lo, actT_hi, actT_lo = (halves(n * KT * SLOTS) for n in range(4))
        y_rows = w(9216, D)
        glu, sig, lin, gs = (w(7680 + n * 256, 256) for n in range(4))
        act_rows = w(8704, 512).rearrange("p (b c) -> p b c", b=2)
        b_in_parts = operands[0:2 * NE, 4096:4096 + 2 * FF]
        gf_row = w(12288, D)
        x_rows = w(13312, D)
        onehot = w(16384, NT * P).rearrange("p (i s) -> p i s", i=NT)
        pick_bias = operands[0:2 * NE, 6144:6144 + SLOTS]
        raw = [ring[:, s].rearrange("p k c -> p (k c)").rearrange("p (k c) -> p k c", c=GW) for s in range(RAW)]
        hi, lo = ([split[:, s].rearrange("p (k c) -> p k c", c=GW) for s in range(a, a + PARTS)]
                  for a in (0, PARTS))
        parts = [(ring[:, s:s + 2] if s < RAW else late_ring[:, s - RAW:s - RAW + 2])
                 .rearrange("p a k c -> p (a k c)")
                 .rearrange("p (i c) -> p i c", i=NT) for s in (4, 0, 2, 6)]

        pair = [ctx.enter_context(nc.psum_tensor(f"pair{i}", [P, 2, 512], F32)) for i in range(4)]
        bank = [pair[i // 2][:, i % 2, :] for i in range(8)]

        x_loaded = sems("x_loaded", NT)
        small_loaded = sem("small_loaded")
        const_loaded = sem("const_loaded")
        wo_full = sems("wo_full", OUT_CHUNKS)
        act_step = sem("act_step")
        tail_step = sem("tail_step")
        dve_step = sem("dve_step")
        x_squared = sem("x_squared")
        x_root = sem("x_root")
        head_root_ready = sem("head_root_ready")
        x2_root = sem("x2_root")
        sum_root = sem("sum_root")
        pool_passed = sem("pool_passed")
        early_loaded = sem("early_loaded")
        gather_started = sem("gather_started")
        sp_passed = sem("sp_passed")
        eps_set = sem("eps_set")
        xn_ready = sem("xn_ready")
        xn_transposed = sem("xn_transposed")
        hT_hi_made = sem("hT_hi_made")
        hT_lo_made = sem("hT_lo_made")
        w_full = sems("w_full", W_RAW)
        w_hi_made = sem("w_hi_made")
        w_lo_by_dve = sem("w_lo_by_dve")
        w_lo_by_pool = sem("w_lo_by_pool")
        ang_ready = sem("ang_ready")
        trig_ready = sem("trig_ready")
        lam_dots = sem("lam_dots")
        lam_exp = sem("lam_exp")
        proj_ready = sem("proj_ready")
        proj_by_act = sem("proj_by_act")
        proj_by_dve = sem("proj_by_dve")
        rope_done = sem("rope_done")
        cast_done = sem("cast_done")
        qk_transposed = sem("qk_transposed")
        qk_by_act = sem("qk_by_act")
        qk_by_dve = sem("qk_by_dve")
        k_scaled = sem("k_scaled")
        silu_sig = sem("silu_sig")
        silu_done = sem("silu_done")
        scores_ready = sem("scores_ready")
        bias_ready = sem("bias_ready")
        exp_done = sem("exp_done")
        att_ready = sem("att_ready")
        att_transposed = sem("att_transposed")
        attT_ready = sem("attT_ready")
        av_ready = sem("av_ready")
        av_evicted = sem("av_evicted")
        ret_scores = sem("ret_scores")
        ret_decayed = sem("ret_decayed")
        qd_ready = sem("qd_ready")
        ret_out = sem("ret_out")
        ret_kv = sem("ret_kv")
        ret_evicted = sem("ret_evicted")
        state_ready = sem("state_ready")
        mix_gained = sem("mix_gained")
        late_loaded = sems("late_loaded", 4)
        mix_ready = sem("mix_ready")
        mix_transposed = sem("mix_transposed")
        mixT_by_act = sem("mixT_by_act")
        mixT_by_dve = sem("mixT_by_dve")
        wo_done = sem("wo_done")
        x2_ready = sem("x2_ready")
        x2_squared = sem("x2_squared")
        h2_ready = sem("h2_ready")
        h2_stored = sem("h2_stored")
        h2_transposed = sem("h2_transposed")
        h2T_by_act = sem("h2T_by_act")
        h2T_by_dve = sem("h2T_by_dve")
        logits_ready = sem("logits_ready")
        logits_read = sem("logits_read")
        max_ready = sem("max_ready")
        gate_exp = sem("gate_exp")
        picked_ready = sem("picked_ready")
        place_ready = sem("place_ready")
        place_read = sem("place_read")
        b_in_rounded = sem("b_in_rounded")
        b_in_split = sem("b_in_split")
        table_ready = sem("table_ready")
        diag_ready = sem("diag_ready")
        pass_rows = sem("pass_rows")
        gates_ready = sem("gates_ready")
        gates_transposed = sem("gates_transposed")
        gateT_ready = sem("gateT_ready")
        bias_out_product = sem("bias_out_product")
        bias_out_ready = sem("bias_out_ready")
        tokens_named = sem("tokens_named")
        gf_loaded = sem("gf_loaded")
        raw_full = sems("raw_full", RAW)
        hi_made = sem("hi_made")
        lo_by_dve = sem("lo_by_dve")
        lo_by_pool = sem("lo_by_pool")
        chunk_used = sem("chunk_used")
        onehot_ready = sem("onehot_ready")
        list_ready = sem("list_ready")
        idx_ready = sem("idx_ready")
        gathered = sem("gathered")
        x_transposed = sem("x_transposed")
        xT_hi_made = sem("xT_hi_made")
        xT_lo_made = sem("xT_lo_made")
        pick_ready = sem("pick_ready")
        h_read = sem("h_read")
        glu_ready = sem("glu_ready")
        sig_ready = sem("sig_ready")
        act_ready = sem("act_ready")
        act_transposed = sem("act_transposed")
        actT_hi_made = sem("actT_hi_made")
        actT_lo_made = sem("actT_lo_made")
        y_scaled = sem("y_scaled")
        cur_ready = sem("cur_ready")
        scattered = sem("scattered")
        parts_loaded = sems("parts_loaded", TOPK - 1)
        last_part_loaded = sems("last_part_loaded", NT)
        sum_ready = sem("sum_ready")
        sum_squared = sem("sum_squared")
        out_ready = sem("out_ready")
        out_stored = sem("out_stored")

        class Chain:
            def __init__(self, eng, semaphore):
                self.eng, self.sem, self.before, self.n = eng, semaphore, 0, 0

            def __call__(self, ins):
                ins.then_inc(self.sem, 1)
                self.n += 1

            def settle(self):
                wait(self.eng, self.sem, self.before + self.n)

        def for_all_partitions(row):
            return row.partition_broadcast(P)

        x_rows_dram = x.rearrange("a (i p) d -> (a i) p d", p=P)
        w_in_cols = w_in.rearrange("a (k p) c -> (a p) k c", p=P)
        w_o_cols = w_o.rearrange("a (k p) c -> (a p) k c", p=P)

        def at(row, e):
            return row[0:1, e:e + 1] if isinstance(e, int) else row[0:1, bass.ds(e, 1)]

        def of_expert(m, e):
            return m[0, e:e + 1] if isinstance(e, int) else m[0, bass.ds(e, 1)]

        def expert_chunk(e, j):
            if j < IN_CHUNKS:
                m, group, half = w_moe_in, j // 2, j % 2
            else:
                m, group, half = w_moe_out, j % 2, (j - IN_CHUNKS) // 2
            rows = of_expert(m, e).rearrange("e (a k p) c -> a (e p) k c", p=P, a=2)[half]
            return rows[:, :, group * GW:(group + 1) * GW]

        def by_pass(eng, body):
            with eng.Fori(1, MAX_PASSES) as p:
                with eng.If(p < passes[eng]):
                    body(p)

        passes = {}

        def load_pass_count(eng):
            eng.wait_ge(table_ready, 2)
            passes[eng] = eng.value_load(at(passes_upto, NE - 1), min_val=1, max_val=MAX_PASSES)

        wo_slot = [RING - OUT_CHUNKS + q for q in range(OUT_CHUNKS)]
        block = ctx.enter_context(nc.Block())

        @block.sync
        def _(sp):
            for i in range(NT):
                sp.dma_start(resid[:, i, :], x_rows_dram[i]).then_inc(x_loaded[i], 16)
            sp.dma_start(cst[:, :], consts_dram).then_inc(const_loaded, 16)
            sp.dma_start(raw_masks, masks_dram).then_inc(const_loaded, 16)
            sp.dma_start(chunk_decay[:, :], chunk_decay_dram).then_inc(const_loaded, 16)
            for c in range(NCHUNK):
                if c >= W_RAW:
                    for made in (w_hi_made, w_lo_by_dve, w_lo_by_pool):
                        sp.wait_ge(made, c - W_RAW + 1)
                sp.dma_start(ring[:, c % W_RAW], w_in_cols[:, :, c * CW:(c + 1) * CW]).then_inc(w_full[c % W_RAW], 16)
            for q, s in enumerate(wo_slot):
                sp.wait_ge(proj_ready, NT * NCHUNK)
                sp.dma_start(slot(s), w_o_cols[:, :, q * CW:(q + 1) * CW]).then_inc(wo_full[q], 16)

            def slot_free(p, j):
                if isinstance(p, int) and p == 0 and j < RAW:
                    for made in (w_hi_made, w_lo_by_dve, w_lo_by_pool):
                        sp.wait_ge(made, NCHUNK)
                    sp.wait_ge(rope_done, len(ROPE_CHUNKS))
                else:
                    for made in (hi_made, lo_by_dve, lo_by_pool):
                        sp.wait_ge(made, CHUNKS * p + j - RAW + 1)

            def load(p, e, j):
                slot_free(p, j)
                sp.dma_start(raw[j % RAW], expert_chunk(e, j)).then_inc(raw_full[j % RAW], 16)

            def expert_of(p):
                return sp.value_load(at(pass_expert, p), min_val=0, max_val=NE - 1)

            def one_pass(p):
                e, following = expert_of(p), expert_of(p + 1)
                for j in range(RAW if isinstance(p, int) else AHEAD, CHUNKS):
                    load(p, e, j)
                with sp.If((p + 1) < passes[sp]):
                    for j in range(AHEAD):
                        load(p + 1, following, j)
                with sp.Else():
                    for j in range(AHEAD):
                        slot_free(p + 1, j)
                        sp.sem_inc(raw_full[j], 16)

            for j in range(RAW):
                slot_free(0, j)
                sp.dma_start(raw[j], expert_chunk(0, j)).then_inc(early_loaded, 16)
            load_pass_count(sp)
            first = expert_of(0)
            sp.wait_ge(early_loaded, 16 * RAW)
            with sp.If(first < 1):
                for j in range(RAW):
                    sp.sem_inc(raw_full[j], 16)
            with sp.Else():
                for j in range(RAW):
                    sp.dma_start(raw[j], expert_chunk(first, j)).then_inc(raw_full[j], 16)
            sp.wait_ge(gather_started, 1)
            one_pass(0)
            by_pass(sp, one_pass)
            rows_out = [sp.value_load(at(scatters_upto, NE - TOPK + r), min_val=0, max_val=16 * MAX_PASSES)
                        for r in range(TOPK)]
            all_used = sp.snap(passes[sp] * CHUNKS)
            for r in range(TOPK):
                if r < TOPK - 1:
                    for made in (hi_made, lo_by_dve, lo_by_pool):
                        ahead = (0, 2, LO_AHEAD if made is lo_by_dve else AHEAD)[r]
                        sp.wait_ge(made, all_used + ahead)
                        sp.sem_inc(sp_passed, 1)
                else:
                    sp.wait_ge(chunk_used, all_used)
                sp.wait_ge(scattered, rows_out[r])
                rows = y_dram.rearrange("(i p r) c -> r p i c", p=P, r=TOPK)[r]
                if r < TOPK - 1:
                    sp.dma_start(parts[r], rows).then_inc(parts_loaded[r], 16)
                else:
                    for i in range(NT):
                        sp.dma_start(parts[r][:, i, :], rows[:, i, :]).then_inc(last_part_loaded[i], 16)
            for i in range(NT):
                sp.wait_ge(out_ready, i + 1)
                sp.dma_start(out.rearrange("a (i p) d -> (a i) p d", p=P)[i], parts[0][:, i, :])\
                    .then_inc(out_stored, 16)
            sp.wait_ge(out_stored, 16 * NT)
            sp.wait_ge(h2_stored, 16 * NT)

        @block.tensor
        def _(pe):
            ident = cst[:, C_IDENT:C_IDENT + P]
            pe.wait_ge(const_loaded, 48)
            pe.wait_ge(xn_ready, NT)
            for k in range(KT):
                for i in range(NT):
                    mm = pe.transpose(bank[k][:, i * P:(i + 1) * P], xn[:, i, k * P:(k + 1) * P], ident)
                mm.then_inc(xn_transposed, 1)
            pe.wait_ge(hT_hi_made, KT)
            pe.wait_ge(hT_lo_made, KT)
            for c in range(NCHUNK):
                pe.wait_ge(w_hi_made, c + 1)
                for i in range(NT):
                    u = c * NT + i
                    if u >= 4:
                        pe.wait_ge(proj_by_act if u % 2 == 0 else proj_by_dve, (u - 4) // 2 + 1)
                    dst, at_i, s = bank[u % 4][:, 0:CW], slice(i * P, (i + 1) * P), c % PARTS
                    for k in range(KT):
                        pe.matmul(dst, hT_hi[:, k, at_i], w_hi[s][:, k, :], start=(k == 0), stop=False)
                        pe.matmul(dst, hT_lo[:, k, at_i], w_hi[s][:, k, :], start=False, stop=False)
                    if i == 0:
                        pe.wait_ge(w_lo_by_dve, c + 1)
                        pe.wait_ge(w_lo_by_pool, c + 1)
                    for k in range(KT):
                        mm = pe.matmul(dst, hT_hi[:, k, at_i], w_lo[s][:, k, :], start=False, stop=(k == KT - 1))
                    mm.then_inc(proj_ready, 1)
            for g in range(12):
                col = (CQ + g * P if g < 8 else CRQ + (g - 8) * P)
                if g == 0:
                    pe.wait_ge(rope_done, len(ROPE_CHUNKS))
                if g >= 4:
                    pe.wait_ge(qk_by_act if g % 2 == 0 else qk_by_dve, (g - 4) // 2 + 1)
                for i in range(NT):
                    mm = pe.transpose(bank[4 + g % 4][:, i * P:(i + 1) * P], proj[:, i, col:col + P], ident)
                mm.then_inc(qk_transposed, 1)
            pe.wait_ge(qk_by_act, 6)
            pe.wait_ge(qk_by_dve, 6)
            pe.wait_ge(proj_by_act, NCHUNK * NT // 2)
            pe.wait_ge(proj_by_dve, NCHUNK * NT // 2)
            pe.wait_ge(cast_done, 4)

            def scores(u):
                i, h = divmod(u, NH)
                if u >= 2:
                    pe.wait_ge(exp_done, 2 * (u - 1))
                for m in range(2):
                    rows = slice(64 * m, 64 * m + 64)
                    n = (i + 1) * P
                    dst = pair[u % 2][:, m, 0:n]
                    pe.matmul(dst, qkT[rows, h, i * P:(i + 1) * P], qkT[rows, 4 + h, 0:n],
                              start=True, stop=False, skip_group_check=True)
                for m in range(2):
                    mm = pe.matmul(pair[u % 2][:, m, i * P:(i + 1) * P], ident_bf[:, :], causal_bf[:, :],
                                   start=False, stop=True, skip_group_check=True)
                mm.then_inc(scores_ready, 1)

            def att_transposes(u):
                i, h = divmod(u, NH)
                pe.wait_ge(att_ready, u + 1)
                if u >= 2:
                    pe.wait_ge(attT_ready, u - 1)
                for j in range(i + 1):
                    mm = pe.transpose(bank[4 + u % 2][:, j * P:(j + 1) * P],
                                      probs[:, u % 2, 0, j * P:(j + 1) * P], ident)
                mm.then_inc(att_transposed, 1)

            def att_values(u):
                i, h = divmod(u, NH)
                pe.wait_ge(attT_ready, u + 1)
                if h == 0 and i >= 1:
                    pe.wait_ge(av_evicted, i)
                for j in range(i + 1):
                    mm = pe.matmul(bank[6][:, h * P:(h + 1) * P], attT[:, u % 2, j * P:(j + 1) * P],
                                   proj[:, j, CV + h * P:CV + (h + 1) * P], start=(j == 0), stop=(j == i))
                mm.then_inc(av_ready, 1)

            NU = NT * NH
            for s in range(NU + 3):
                if s < NU:
                    scores(s)
                if 2 <= s < NU + 2:
                    att_transposes(s - 2)
                if s >= 3:
                    att_values(s - 3)

            def ret_score(i):
                if i >= 2:
                    pe.wait_ge(state_ready, 2 * (i - 1))
                for h in range(NH):
                    rows = slice(64 * (h % 2), 64 * (h % 2) + 64)
                    mm = pe.matmul(pair[i % 2][:, h % 2, (h // 2) * P:(h // 2 + 1) * P],
                                   qkT[rows, 10 + h // 2, i * P:(i + 1) * P],
                                   qkT[rows, 8 + h // 2, i * P:(i + 1) * P], start=True, stop=True)
                mm.then_inc(ret_scores, 1)

            def ret_output(i):
                pe.wait_ge(ret_decayed, i + 1)
                if i >= 2:
                    pe.wait_ge(ret_evicted, i - 1)
                if i >= 1:
                    pe.wait_ge(state_ready, 2 * i)
                    pe.wait_ge(qd_ready, 2)
                for h in range(NH):
                    rows = slice(64 * (h % 2), 64 * (h % 2) + 64)
                    dst = pair[2 + i % 2][:, h % 2, (h // 2) * P:(h // 2 + 1) * P]
                    if i >= 1:
                        pe.matmul(dst, qdT[rows, h // 2, i * P:(i + 1) * P], state[rows, h // 2, :],
                                  start=True, stop=False)
                    mm = pe.matmul(dst, st_s[:, i % 2, h % 2, h // 2, :],
                                   proj[:, i, CRV + h * P:CRV + (h + 1) * P], start=(i == 0), stop=True)
                mm.then_inc(ret_out, 1)
                if i < NT - 1:
                    if i == 0:
                        pe.wait_ge(k_scaled, NT)
                    for h in range(NH):
                        rows = slice(64 * (h % 2), 64 * (h % 2) + 64)
                        mm = pe.matmul(pair[i % 2][rows, 0, 256 + (h // 2) * P:256 + (h // 2 + 1) * P],
                                       proj[:, i, CRK + h * DQ:CRK + (h + 1) * DQ],
                                       proj[:, i, CRV + h * P:CRV + (h + 1) * P], start=True, stop=True)
                    mm.then_inc(ret_kv, 1)

            pe.wait_ge(exp_done, 2 * NU)
            pe.wait_ge(attT_ready, NU)
            pe.wait_ge(av_evicted, NT)
            ret_score(0)
            for i in range(NT):
                if i + 1 < NT:
                    ret_score(i + 1)
                ret_output(i)

            def mix_product(i):
                pe.wait_ge(mix_ready, i + 1)
                for k in range(KT):
                    if k == 4:
                        mm.then_inc(mix_transposed, 1)
                    mm = pe.transpose(bank[k // 4][:, (k % 4) * P:(k % 4 + 1) * P],
                                      mix[:, i, k * P:(k + 1) * P], ident)
                mm.then_inc(mix_transposed, 1)
                pe.wait_ge(mixT_by_act, i + 1)
                pe.wait_ge(mixT_by_dve, i + 1)
                if i >= 2:
                    pe.wait_ge(x2_ready, 2 * (i - 1))
                for q, s in enumerate(wo_slot):
                    if i == 0:
                        pe.wait_ge(wo_full[q], 16)
                    dst = pair[1 + i % 2][:, q // 2, (q % 2) * CW:(q % 2 + 1) * CW]
                    for k in range(KT):
                        mm = pe.matmul(dst, mixT[:, i % 2, k, :], slot(s)[:, k, :],
                                       start=(k == 0), stop=(k == KT - 1))
                mm.then_inc(wo_done, 1)

            def router(i):
                pe.wait_ge(h2_ready, i + 1)
                if i >= 1:
                    pe.wait_ge(logits_read, i)
                    pe.wait_ge(place_read, i)
                for k in range(KT):
                    if k == 4:
                        mm.then_inc(h2_transposed, 1)
                    mm = pe.transpose(bank[6 + k // 4][:, (k % 4) * P:(k % 4 + 1) * P],
                                      h2_row[:, i, k * P:(k + 1) * P], ident)
                mm.then_inc(h2_transposed, 1)
                pe.wait_ge(h2T_by_act, i + 1)
                pe.wait_ge(h2T_by_dve, i + 1)
                if i == 0:
                    pe.wait_ge(late_loaded[1], 16)
                for k in range(KT):
                    mm = pe.matmul(bank[6][:, 0:NE], mixT[:, i % 2, k, :], w_router_sb[:, k, :],
                                   start=(k == 0), stop=(k == KT - 1))
                mm.then_inc(logits_ready, 1)

            def places(i):
                pe.wait_ge(picked_ready, i + 1)
                for j in range(i + 1):
                    mm = pe.matmul(bank[7][:, 0:NE], (utri_bf if j == i else ones_bf)[:, :], picked_bf[:, j, :],
                                   start=(j == 0), stop=(j == i))
                mm.then_inc(place_ready, 1)

            def gate_transpose(i):
                pe.wait_ge(gates_ready, i + 1)
                pe.transpose(bank[2][0:NE, i * P:(i + 1) * P], gates[:, i, :], ident).then_inc(gates_transposed, 1)

            def bias_product(i):
                pe.wait_ge(gateT_ready, i // 2 + 1)
                pe.wait_ge(late_loaded[3], 16)
                for f in range(2):
                    n = 2 * i + f
                    if n >= 2:
                        pe.wait_ge(bias_out_ready, n - 1)
                    pe.matmul(bank[n % 2], gateT[:, i * P:(i + 1) * P], b_out_rows[:, f * 512:(f + 1) * 512],
                              start=True, stop=True).then_inc(bias_out_product, 1)

            mix_product(0)
            mix_product(1)
            for i in range(NT):
                router(i)
                if i + 2 < NT:
                    mix_product(i + 2)
                if i == 2:
                    pe.wait_ge(x2_ready, 2 * 3)
                    gate_transpose(0)
                    gate_transpose(1)
                    pe.wait_ge(mixT_by_act, NT)
                    pe.wait_ge(mixT_by_dve, NT)
                    bias_product(0)
                if i == 3:
                    bias_product(1)
                places(i)
            pe.wait_ge(place_read, NT)
            for j in range(NT):
                mm = pe.matmul(bank[7][:, 64:64 + NE], ones_bf[:, :], picked_bf[:, j, :],
                               start=(j == 0), stop=(j == NT - 1))
            mm.then_inc(place_ready, 1)

            def token_list(p):
                pe.wait_ge(onehot_ready, p + 1)
                for i in range(NT):
                    mm = pe.matmul(bank[5][:, 0:4], onehot[:, i, :], route_cur[:, i, :],
                                   start=(i == 0), stop=(i == NT - 1))
                mm.then_inc(list_ready, 1)

            def x_transposes(p):
                pe.wait_ge(gathered, 16 * (p + 1))
                for k in range(KT):
                    mm = pe.transpose(bank[6 + k // KH][:, (k % KH) * P:(k % KH + 1) * P],
                                      x_rows[:, k * P:(k + 1) * P], ident)
                    if k % KH == KH - 1:
                        mm.then_inc(x_transposed, 1)

            gate_transpose(2)
            gate_transpose(3)
            pe.wait_ge(diag_ready, 1)
            pe.matmul(bank[7][:, 128:128 + 2 * (MAX_PASSES + 1)], ones_bf[:, :],
                      pass_diag.rearrange("p a n -> p (a n)"), start=True, stop=True).then_inc(pass_rows, 1)
            token_list(0)
            bias_product(2)
            bias_product(3)
            pe.wait_ge(table_ready, 2)
            x_transposes(0)
            load_pass_count(pe)
            pe.wait_ge(b_in_split, 1)
            pe.wait_ge(bias_out_ready, 2 * NT)

            def product(p, j, dst, k0, left_hi, left_lo, start, stop):
                n, s = CHUNKS * p + j + 1, j % PARTS
                pe.wait_ge(hi_made, n)
                for k in range(KH):
                    pe.matmul(dst, left_hi[:, k0 + k, :], hi[s][:, k, :], start=(start and k == 0), stop=False)
                    pe.matmul(dst, left_lo[:, k0 + k, :], hi[s][:, k, :], start=False, stop=False)
                pe.wait_ge(lo_by_dve, n)
                pe.wait_ge(lo_by_pool, n)
                for k in range(KH):
                    mm = pe.matmul(dst, left_hi[:, k0 + k, :], lo[s][:, k, :], start=False,
                                   stop=(stop and k == KH - 1))
                mm.then_inc(chunk_used, 1)

            def act_transposes(p, g):
                pe.wait_ge(act_ready, 4 * p + g + 1)
                if g >= 2:
                    pe.wait_ge(actT_lo_made, 4 * p + g - 1)
                for n in range(2):
                    mm = pe.transpose(bank[6 + g % 2][:, n * P:(n + 1) * P],
                                      act_rows[:, g % 2, n * P:(n + 1) * P], ident)
                mm.then_inc(act_transposed, 1)

            def one_pass(p):
                pe.wait_ge(pick_ready, 2 * (p + 1))
                for g in range(4):
                    wait(pe, h_read, 4 * (p - 1) + g + 1)
                    pe.matmul(bank[g], pick_bias, b_in_parts[:, g * GW:(g + 1) * GW], start=True, stop=False)
                    for a in range(2):
                        if g == 0:
                            pe.wait_ge(xT_hi_made, 2 * p + a + 1)
                            pe.wait_ge(xT_lo_made, 2 * p + a + 1)
                        product(p, 2 * g + a, bank[g], a * KH, xT_hi, xT_lo, False, a == 1)
                    if g >= 1:
                        act_transposes(p, g - 1)
                    if g == 1:
                        wait(pe, y_scaled, 2 * p)
                        token_list(p + 1)
                wait(pe, y_scaled, 2 * p)

                pe.wait_ge(actT_hi_made, 4 * p + 2)
                pe.wait_ge(actT_lo_made, 4 * p + 2)
                product(p, 8, bank[4], 0, actT_hi, actT_lo, True, False)
                act_transposes(p, 3)
                pe.wait_ge(idx_ready, p + 2)
                product(p, 9, bank[5], 0, actT_hi, actT_lo, True, False)
                pe.wait_ge(actT_hi_made, 4 * (p + 1))
                pe.wait_ge(actT_lo_made, 4 * (p + 1))
                x_transposes(p + 1)
                product(p, 10, bank[4], KH, actT_hi, actT_lo, False, True)
                product(p, 11, bank[5], KH, actT_hi, actT_lo, False, True)

            one_pass(0)
            by_pass(pe, one_pass)

        @block.scalar
        def _(act):
            small = [(pos_i[:, :], positions.rearrange("a (i p) -> (a p) i", p=P)),
                     (g1_col[:, :], norm1_g.rearrange("a (k p) -> (a p) k", p=P))]
            for n, row in enumerate((lambda_q1, lambda_k1, lambda_q2, lambda_k2)):
                small.append((lam_rows[:, n, :], for_all_partitions(row[0])))
            for h in range(NH):
                small.append((gain_row[:, h * P:(h + 1) * P], for_all_partitions(diff_norm_g[0])))
            small.append((gain_row[:, 512:D], for_all_partitions(ret_norm_g.rearrange("a h c -> (a h c)"))))
            small.append((b_router_row[:, :], for_all_partitions(b_router[0])))
            assert len(small) == N_SMALL
            with nc.allow_non_contiguous_dma(reason="a few hundred words"):
                for dst, src in small:
                    act.dma_start(dst, src).then_inc(small_loaded, 16)
            def root(at, n, mean_of, ready):
                act.activation(stat[:, at:at + n], stat[:, at:at + n], ACT.Sqrt, bias=eps_col[:, 0:1],
                               scale=1.0 / mean_of).then_inc(ready, 1)

            for i in range(NT):
                act.wait_ge(x_loaded[i], 16)
                act.activation(junk1[:, i, :], resid[:, i, :], ACT.Square, accum_out=stat[:, i:i + 1]).then_inc(x_squared, 1)
            act.wait_ge(x_squared, NT)
            act.wait_ge(eps_set, 1)
            root(0, NT, D, x_root)

            def w_in_hi(c):
                act.wait_ge(w_full[c % W_RAW], 16 * (c // W_RAW + 1))
                if c >= PARTS:
                    act.wait_ge(proj_ready, NT * (c - PARTS + 1))
                act.copy(w_hi[c % PARTS], ring[:, c % W_RAW]).then_inc(w_hi_made, 1)

            w_in_hi(0)
            w_in_hi(1)
            act.wait_ge(small_loaded, 16 * N_SMALL)
            for k in range(KT):
                act.wait_ge(xn_transposed, k + 1)
                act.activation(hT_hi[:, k, :], bank[k], ACT.Copy, scale=g1_col[:, k:k + 1]).then_inc(hT_hi_made, 1)
            act.wait_ge(ang_ready, 2)
            act.activation(cos_sin[:, 0], ang[:, 5], ACT.Sin).then_inc(trig_ready, 1)
            act.activation(cos_sin[:, 1], ang[:, 3], ACT.Sin).then_inc(trig_ready, 1)
            act.wait_ge(lam_dots, 1)
            act.activation(lam[:, 2:4], lam[:, 0:2], ACT.Exp).then_inc(lam_exp, 1)
            for c in range(NCHUNK):
                if c + 2 < NCHUNK:
                    w_in_hi(c + 2)
                for i in range(0, NT, 2):
                    u = c * NT + i
                    act.wait_ge(proj_ready, u + 1)
                    act.copy(proj[:, i, c * CW:(c + 1) * CW], bank[u % 4][:, 0:CW]).then_inc(proj_by_act, 1)
            for g in range(0, 12, 2):
                act.wait_ge(qk_transposed, g + 1)
                act.copy(qkT[:, g, :], bank[4 + g % 4]).then_inc(qk_by_act, 1)
            act.wait_ge(qk_transposed, 12)
            act.wait_ge(proj_by_act, NCHUNK * NT // 2)
            act.wait_ge(proj_by_dve, NCHUNK * NT // 2)
            for i in range(NT):
                act.activation(mix[:, i, 512:D], proj[:, i, CRG:PROJ], ACT.Sigmoid).then_inc(silu_sig, 1)

            def head_squares(outputs, i, first_head):
                chain.settle()
                for h in range(NH):
                    col = 16 + 2 * NH * i + first_head + h
                    chain(act.activation(square_tmp[:, h, :], outputs[h], ACT.Square,
                                         accum_out=stat[:, col:col + 1]))

            chain = Chain(act, act_step)

            def exponentials(u):
                i, b, n = u // NH, u % 2, (u // NH + 1) * P
                act.wait_ge(bias_ready, u + 1)
                if u >= 2:
                    act.wait_ge(att_transposed, u - 1)
                for m in range(2):
                    act.activation(probs[:, b, m, 0:n], pair[b][:, m, 0:n], ACT.Exp, bias=row_bias[:, b, m:m + 1],
                                   scale=SCALE, accum_out=row_sum[:, b, m:m + 1]).then_inc(exp_done, 1)

            NU = NT * NH
            for s in range(NU + 3):
                if s < NU:
                    exponentials(s)
                if 2 <= s < NU + 2:
                    u = s - 2
                    n = (u // NH + 1) * P
                    act.wait_ge(att_transposed, u + 1)
                    if u >= 2:
                        act.wait_ge(av_ready, u - 1)
                    act.copy(attT[:, u % 2, 0:n], bank[4 + u % 2][:, 0:n]).then_inc(attT_ready, 1)
                if s >= 3 and (s - 3) % NH == NH - 1:
                    i = (s - 3) // NH
                    act.wait_ge(av_ready, s - 2)
                    head_squares([bank[6][:, h * P:(h + 1) * P] for h in range(NH)], i, 0)
                    act.copy(mix[:, i, 0:512], bank[6]).then_inc(av_evicted, 1)
            act.wait_ge(silu_done, 2 * NT)
            for i in range(NT):
                act.wait_ge(ret_out, i + 1)
                outputs = pair[2 + i % 2][:, :, 0:256].rearrange("p r (a c) -> p a r c", a=2)
                head_squares([outputs[:, h // 2, h % 2, :] for h in range(NH)], i, NH)
                act.copy(mix[:, i, 512:D].rearrange("p (a r c) -> p a r c", a=2, r=2), outputs).then_inc(ret_evicted, 1)

            act.wait_ge(ret_evicted, NT)
            chain.settle()
            root(16, 2 * NH * NT, P, head_root_ready)

            def mix_evict(i):
                act.wait_ge(mix_transposed, 2 * i + 1)
                act.copy(mixT[:, i % 2, 0:4, :], bank[0].rearrange("p (k t) -> p k t", k=4)).then_inc(mixT_by_act, 1)

            mix_evict(0)
            mix_evict(1)

            def x2_norm(i):
                act.wait_ge(x2_ready, 2 * (i + 1))
                act.activation(junk2, resid[:, i, :], ACT.Square, accum_out=stat[:, 48 + i:49 + i]).then_inc(x2_squared, 1)
                act.wait_ge(x2_squared, i + 1)
                root(48 + i, 1, D, x2_root)

            def store_h2(i):
                act.wait_ge(h2_ready, i + 1)
                act.dma_start(h2_dram[i * P:(i + 1) * P, :], h2_row[:, i, :]).then_inc(h2_stored, 16)

            for i in range(NT):
                if i < NT - 1:
                    x2_norm(i)
                    store_h2(i)
                act.wait_ge(h2_transposed, 2 * i + 1)
                act.copy(mixT[:, i % 2, 0:4, :], bank[6].rearrange("p (k t) -> p k t", k=4)).then_inc(h2T_by_act, 1)
                if i == NT - 2:
                    x2_norm(i + 1)
                    store_h2(i + 1)
                act.wait_ge(max_ready, i + 1)
                act.activation(expo, logits, ACT.Exp, bias=rstat[:, 0:1]).then_inc(gate_exp, 1)
                if i + 2 < NT:
                    mix_evict(i + 2)
            act.wait_ge(late_loaded[2], 32)
            act.wait_ge(h2_ready, NT)
            act.wait_ge(h2_stored, 16 * NT)
            act.copy(b_in_parts, b_in_rows).then_inc(b_in_rounded, 1)

            def make_hi(p, j):
                act.wait_ge(raw_full[j % RAW], (p * (CHUNKS // RAW) + j // RAW + 1) * 16)
                if not (isinstance(p, int) and p == 0 and j < PARTS):
                    act.wait_ge(chunk_used, CHUNKS * p + j - PARTS + 1)
                act.copy(hi[j % PARTS], raw[j % RAW]).then_inc(hi_made, 1)

            def x_hi(p):
                for a in range(2):
                    act.wait_ge(x_transposed, 2 * p + a + 1)
                    act.copy(xT_hi[:, a * KH:(a + 1) * KH, :], bank[6 + a].rearrange("p (k t) -> p k t", k=KH))\
                        .then_inc(xT_hi_made, 1)

            def sigmoid(p, g):
                act.wait_ge(glu_ready, 4 * p + g + 1)
                act.activation(sig, glu, ACT.Sigmoid, scale=SWI_ALPHA).then_inc(sig_ready, 1)

            def act_hi(p, g):
                act.wait_ge(act_transposed, 4 * p + g + 1)
                act.copy(actT_hi[:, 2 * g:2 * g + 2, :], bank[6 + g % 2][:, 0:256].rearrange("p (k t) -> p k t", k=2))\
                    .then_inc(actT_hi_made, 1)

            def scale_rows(p, f):
                act.wait_ge(chunk_used, CHUNKS * p + CHUNKS - 1 + f)
                if f == 0:
                    act.wait_ge(cur_ready, p + 1)
                    wait(act, scattered, 16 * p)
                act.activation(y_rows[:, f * GW:(f + 1) * GW], bank[4 + f], ACT.Copy, scale=gate_cur[:, 0:1])\
                    .then_inc(y_scaled, 1)

            def one_pass(p):
                for s in range(CHUNKS):
                    if s % 2 and s < IN_CHUNKS:
                        sigmoid(p, s // 2)
                    if s in (3, 5, 7, 8):
                        act_hi(p, (s - 2) // 2)
                    if s == 9:
                        act.wait_ge(chunk_used, CHUNKS * p + IN_CHUNKS)
                        x_hi(p + 1)
                    if s + AHEAD < CHUNKS:
                        make_hi(p, s + AHEAD)
                    else:
                        make_hi(p + 1, s + AHEAD - CHUNKS)
                    if s in (10, 11):
                        scale_rows(p, s - 10)

            load_pass_count(act)
            act.wait_ge(wo_done, NT)
            for j in range(AHEAD):
                make_hi(0, j)
            x_hi(0)
            one_pass(0)
            by_pass(act, one_pass)
            for i in range(NT):
                act.wait_ge(sum_ready, TOPK * NT - NT + i + 1)
                act.activation(junk_out, resid[:, i, :], ACT.Square, accum_out=stat[:, 52 + i:53 + i]).then_inc(sum_squared, 1)
                act.wait_ge(sum_squared, i + 1)
                root(52 + i, 1, D, sum_root)

        @block.vector
        def _(dve):
            chain = Chain(dve, dve_step)

            dve.memset(eps_col[:, :], EPS).then_inc(eps_set, 1)
            dve.wait_ge(x_root, 1)
            chain(dve.reciprocal(stat[:, 0:NT], stat[:, 0:NT]))
            chain.settle()
            for i in range(NT):
                dve.tensor_scalar(xn[:, i, :], resid[:, i, :], stat[:, i:i + 1], None, ALU.mult).then_inc(xn_ready, 1)

            def w_in_lo(c):
                dve.wait_ge(w_hi_made, c + 1)
                s, tiles = c % PARTS, slice(0, W_DVE_K)
                dve.tensor_tensor(w_lo[s][:, tiles, :], ring[:, c % W_RAW, tiles, :],
                                  w_hi[s][:, tiles, :].bitcast(F32), ALU.subtract).then_inc(w_lo_by_dve, 1)

            w_in_lo(0)
            w_in_lo(1)
            dve.wait_ge(small_loaded, 16 * N_SMALL)
            for k in range(KT):
                dve.wait_ge(hT_hi_made, k + 1)
                dve.scalar_tensor_tensor(hT_lo[:, k, :], bank[k], g1_col[:, k:k + 1], hT_hi[:, k, :].bitcast(F32),
                                         ALU.mult, ALU.subtract).then_inc(hT_lo_made, 1)
            dve.wait_ge(const_loaded, 48)
            chain(dve.tensor_copy(pos_f[:, :], pos_i[:, :]))
            chain.settle()
            for i in range(NT):
                chain(dve.tensor_scalar(ang[:, 0, i, :], cst[:, C_FREQ:C_FREQ + 32], pos_f[:, i:i + 1], None, ALU.mult))
            chain.settle()
            chain(dve.tensor_scalar(ang[:, 1], ang[:, 0], 1.0 / (2 * math.pi), MAGIC, ALU.mult, ALU.add))
            chain.settle()
            chain(dve.tensor_scalar(ang[:, 2], ang[:, 1], -MAGIC, None, ALU.add))
            chain.settle()
            chain(dve.scalar_tensor_tensor(ang[:, 3], ang[:, 2], -TWO_PI_A, ang[:, 0], ALU.mult, ALU.add))
            chain.settle()
            chain(dve.scalar_tensor_tensor(ang[:, 4], ang[:, 2], -TWO_PI_B, ang[:, 3], ALU.mult, ALU.add))
            chain.settle()
            chain(dve.scalar_tensor_tensor(ang[:, 1], ang[:, 2], -TWO_PI_C, ang[:, 4], ALU.mult, ALU.add))
            chain.settle()
            dve.tensor_scalar(ang[:, 3], ang[:, 1], PI_F, -PI_F, ALU.min, ALU.max).then_inc(ang_ready, 1)
            dve.wait_ge(ang_ready, 1)
            chain(dve.scalar_tensor_tensor(ang[:, 4], ang[:, 3], -1.0, ang[:, 3], ALU.mult, ALU.max))
            chain.settle()
            dve.tensor_scalar(ang[:, 5], ang[:, 4], -1.0, math.pi / 2, ALU.mult, ALU.add).then_inc(ang_ready, 1)
            chain(dve.tensor_tensor(lam_rows[:, 0::2], lam_rows[:, 0::2], lam_rows[:, 1::2], ALU.mult))
            chain.settle()
            dve.tensor_reduce(lam[:, 0:2], lam_rows[:, 0::2], AX_X, ALU.add).then_inc(lam_dots, 1)
            dve.tensor_copy(ident_bf[:, :], cst[:, C_IDENT:C_IDENT + P]).then_inc(cast_done, 1)
            dve.tensor_copy(causal_bf[:, :], raw_masks[:, 0:P]).then_inc(cast_done, 1)
            dve.tensor_copy(utri_bf[:, :], raw_masks[:, P:2 * P]).then_inc(cast_done, 1)
            dve.memset(ones_bf[:, :], 1.0).then_inc(cast_done, 1)
            dve.wait_ge(lam_exp, 1)
            chain(dve.tensor_tensor(lam[:, 4:5], lam[:, 3:4], lam[:, 2:3], ALU.subtract))
            chain.settle()
            chain(dve.tensor_scalar(lam[:, 5:6], lam[:, 4:5], -LAM_INIT, None, ALU.add))
            chain.settle()

            def rotary(c):
                cols = proj[:, :, c * CW:(c + 1) * CW].rearrange("p i (g a f) -> p i g a f", g=4, a=2)
                halves = [cols[:, :, :, a, :] for a in range(2)]
                cos, sin = (cos_sin[:, n].unsqueeze(2).to_broadcast([P, NT, 4, 32]) for n in range(2))
                dve.wait_ge(proj_by_act, 2 * (c + 1))
                dve.wait_ge(proj_by_dve, 2 * (c + 1))
                dve.wait_ge(trig_ready, 2)
                for n, (half, trig) in enumerate(((0, cos), (1, sin), (1, cos), (0, sin))):
                    chain(dve.tensor_tensor(rope_tmp[:, n], halves[half], trig, ALU.mult))
                chain.settle()
                chain(dve.tensor_tensor(halves[0], rope_tmp[:, 0], rope_tmp[:, 1], ALU.subtract))
                dve.tensor_tensor(halves[1], rope_tmp[:, 2], rope_tmp[:, 3], ALU.add).then_inc(rope_done, 1)
                chain.settle()

            for c in range(NCHUNK):
                for i in range(1, NT, 2):
                    u = c * NT + i
                    dve.wait_ge(proj_ready, u + 1)
                    dve.tensor_copy(proj[:, i, c * CW:(c + 1) * CW], bank[u % 4][:, 0:CW]).then_inc(proj_by_dve, 1)
                    if i == 1 and c + 2 < NCHUNK:
                        w_in_lo(c + 2)
                if c in ROPE_CHUNKS:
                    rotary(c)
            for g in range(1, 12, 2):
                dve.wait_ge(qk_transposed, g + 1)
                dve.tensor_copy(qkT[:, g, :], bank[4 + g % 4]).then_inc(qk_by_dve, 1)

            def maxima(u):
                b, n = u % 2, (u // NH + 1) * P
                dve.wait_ge(scores_ready, u + 1)
                chain(dve.tensor_reduce(row_max[:, b, :], pair[b][:, :, 0:n], AX_X, ALU.max))
                chain.settle()
                if u >= 2:
                    dve.wait_ge(exp_done, 2 * (u - 1))
                dve.tensor_scalar(row_bias[:, b, :], row_max[:, b, :], -SCALE, None, ALU.mult).then_inc(bias_ready, 1)

            def difference(u):
                b, n = u % 2, (u // NH + 1) * P
                dve.wait_ge(exp_done, 2 * (u + 1))
                chain(dve.reciprocal(row_rec[:, b, :], row_sum[:, b, :]))
                chain.settle()
                chain(dve.tensor_tensor(row_rec[:, b, 1:2], row_rec[:, b, 1:2], lam[:, 5:6], ALU.mult))
                chain.settle()
                chain(dve.tensor_scalar(probs[:, b, 1, 0:n], probs[:, b, 1, 0:n], row_rec[:, b, 1:2], None, ALU.mult))
                chain.settle()
                dve.scalar_tensor_tensor(probs[:, b, 0, 0:n], probs[:, b, 0, 0:n], row_rec[:, b, 0:1],
                                         probs[:, b, 1, 0:n], ALU.mult, ALU.add).then_inc(att_ready, 1)

            NU = NT * NH
            for s in range(NU + 1):
                if s < NU:
                    maxima(s)
                if s >= 1:
                    difference(s - 1)
            dve.wait_ge(av_ready, NU)
            for a in range(2):
                dve.tensor_tensor(qdT[:, a, :].rearrange("p (i t) -> p i t", i=NT),
                                  qkT[:, 8 + a, :].rearrange("p (i t) -> p i t", i=NT),
                                  cst[:, C_QDEC + a * P:C_QDEC + (a + 1) * P].unsqueeze(1).to_broadcast([P, NT, P]),
                                  ALU.mult).then_inc(qd_ready, 1)
            for i in range(NT):
                dve.wait_ge(ret_scores, i + 1)
                if i >= 2:
                    dve.wait_ge(ret_out, i - 1)
                dve.tensor_tensor(st_s[:, i % 2].rearrange("p r a n -> p r (a n)"), pair[i % 2][:, :, 0:256],
                                  cst[:, C_DECAY:C_DECAY + 512].rearrange("p (r n) -> p r n", r=2), ALU.mult)\
                    .then_inc(ret_decayed, 1)
                if i >= 1:
                    j = i - 1
                    dve.wait_ge(ret_kv, j + 1)
                    for a in range(2):
                        kv = pair[j % 2][:, 0, 256 + a * P:256 + (a + 1) * P]
                        if j == 0:
                            dve.tensor_copy(state[:, a, :], kv).then_inc(state_ready, 1)
                        else:
                            dve.wait_ge(state_ready, 2 * j)
                            dve.scalar_tensor_tensor(state[:, a, :], state[:, a, :], chunk_decay[:, a:a + 1], kv,
                                                     ALU.mult, ALU.add).then_inc(state_ready, 1)
            dve.wait_ge(mix_gained, 2 * NT)
            dve.wait_ge(head_root_ready, 1)
            chain(dve.reciprocal(stat[:, 16:48], stat[:, 16:48]))
            chain.settle()
            head_root = stat[:, 16:48].rearrange("p (i h) -> p i h", i=NT)
            chain(dve.tensor_scalar(head_root[:, :, 0:NH], head_root[:, :, 0:NH], 1.0 - LAM_INIT, None, ALU.mult))
            chain.settle()

            def mix_norm(i):
                m = mix[:, i, :].rearrange("p (h c) -> p h c", h=2 * NH)
                dve.tensor_tensor(m, m, head_root[:, i, :].unsqueeze(2).to_broadcast([P, 2 * NH, P]), ALU.mult)\
                    .then_inc(mix_ready, 1)

            def mix_evict(i):
                dve.wait_ge(mix_transposed, 2 * i + 2)
                dve.tensor_copy(mixT[:, i % 2, 4:8, :], bank[1].rearrange("p (k t) -> p k t", k=4)).then_inc(mixT_by_dve, 1)

            def read_places(i):
                dve.wait_ge(place_ready, i + 1)
                dve.scalar_tensor_tensor(slot_of[:, i, :], bank[7][:, 0:NE], 1.0, picked[:, i, :], ALU.add, ALU.mult)\
                    .then_inc(place_read, 1)
                dve.wait_ge(place_read, i + 1)
                chain(dve.tensor_scalar(slot_of[:, i, :], slot_of[:, i, :], -1.0, None, ALU.add))
                chain.settle()

            def copy_gates(n):
                dve.wait_ge(gates_transposed, 2 * n + 2)
                cols = slice(2 * n * P, 2 * (n + 1) * P)
                dve.tensor_copy(gateT[:, cols], bank[2][0:NE, cols]).then_inc(gateT_ready, 1)

            def add_bias(i):
                for f in range(2):
                    n = 2 * i + f
                    dve.wait_ge(bias_out_product, n + 1)
                    dve.wait_ge(x2_ready, 2 * (i + 1))
                    half = resid[:, i, f * 512:(f + 1) * 512]
                    dve.tensor_tensor(half, half, bank[n % 2], ALU.add).then_inc(bias_out_ready, 1)

            for i in range(NT):
                mix_norm(i)
            mix_evict(0)
            mix_evict(1)
            dve.wait_ge(tokens_named, 5)
            def add_to_residual(i):
                dve.wait_ge(wo_done, i + 1)
                for f in range(2):
                    half = resid[:, i, f * 512:(f + 1) * 512]
                    dve.tensor_tensor(half, half, pair[1 + i % 2][:, f, :], ALU.add).then_inc(x2_ready, 1)

            def h2_norm(i):
                dve.wait_ge(x2_root, i + 1)
                chain(dve.reciprocal(stat[:, 48 + i:49 + i], stat[:, 48 + i:49 + i]))
                chain.settle()
                if i == 0:
                    dve.wait_ge(late_loaded[0], 16)
                dve.scalar_tensor_tensor(h2_row[:, i, :].rearrange("p (a c) -> p a c", a=NT),
                                         resid[:, i, :].rearrange("p (a c) -> p a c", a=NT),
                                         stat[:, 48 + i:49 + i], g2_row, ALU.mult, ALU.mult).then_inc(h2_ready, 1)

            for i in range(NT):
                if i < NT - 1:
                    add_to_residual(i)
                    h2_norm(i)
                if i:
                    read_places(i - 1)
                dve.wait_ge(h2_transposed, 2 * i + 2)
                dve.tensor_copy(mixT[:, i % 2, 4:8, :], bank[7].rearrange("p (k t) -> p k t", k=4)).then_inc(h2T_by_dve, 1)
                if i == NT - 2:
                    add_to_residual(i + 1)
                    h2_norm(i + 1)
                    copy_gates(0)
                if i == 3:
                    add_bias(0)
                dve.wait_ge(logits_ready, i + 1)
                if i:
                    dve.wait_ge(gate_exp, i)
                dve.tensor_tensor(logits, bank[6][:, 0:NE], b_router_row[:, :], ALU.add).then_inc(logits_read, 1)
                dve.wait_ge(logits_read, i + 1)
                chain(dve.max(top8, logits))
                chain.settle()
                dve.tensor_scalar(rstat[:, 0:1], top8[:, 0:1], -1.0, None, ALU.mult).then_inc(max_ready, 1)
                if i + 2 < NT:
                    mix_evict(i + 2)
                chain(dve.max_index(top8_i, top8, logits))
                chain.settle()
                chain(dve.tensor_copy(top8_f, top8_i))
                chain.settle()
                for k in range(TOPK):
                    if k == 0:
                        chain(dve.tensor_scalar(picked[:, i, :], expert_id, top8_f[:, 0:1], None, ALU.is_equal))
                    else:
                        chain(dve.scalar_tensor_tensor(picked[:, i, :], expert_id, top8_f[:, k:k + 1], picked[:, i, :],
                                                       ALU.is_equal, ALU.add))
                    chain.settle()
                dve.tensor_copy(picked_bf[:, i, :], picked[:, i, :]).then_inc(picked_ready, 1)
                dve.wait_ge(gate_exp, i + 1)
                chain(dve.tensor_tensor(gates[:, i, :], expo, picked[:, i, :], ALU.mult))
                chain(dve.tensor_tensor_scan(rank, ones_row, picked[:, i, :], 0.0, ALU.mult, ALU.add))
                chain.settle()
                chain(dve.tensor_reduce(rstat[:, 1:2], gates[:, i, :], AX_X, ALU.add))
                chain(dve.tensor_tensor(rank, rank, picked[:, i, :], ALU.subtract))
                chain.settle()
                chain(dve.reciprocal(rstat[:, 2:3], rstat[:, 1:2]))
                chain(dve.tensor_scalar(route[:, i, :, 0], rank, token_id[:, i:i + 1], -NOWHERE, ALU.add, ALU.add))
                chain(dve.tensor_scalar(route[:, i, :, 1], ones_row, token_id[:, i:i + 1], 1.0 / TOPK, ALU.mult, ALU.mult))
                chain(dve.tensor_scalar(route[:, i, :, 3], ones_row, 0.0, None, ALU.mult))
                chain.settle()
                dve.tensor_scalar(gates[:, i, :], gates[:, i, :], rstat[:, 2:3], None, ALU.mult).then_inc(gates_ready, 1)
                dve.wait_ge(gates_ready, i + 1)
                chain(dve.tensor_copy(route[:, i, :, 2], gates[:, i, :]))
                chain.settle()
            read_places(NT - 1)
            dve.wait_ge(place_ready, NT + 1)
            dve.tensor_copy(expert_count, bank[7][:, 64:64 + NE]).then_inc(table_ready, 1)
            dve.wait_ge(table_ready, 1)
            chain(dve.tensor_scalar(n_passes, expert_count, 0.0, None, ALU.is_gt))
            chain.settle()
            for n in range(SLOTS, SEQ, SLOTS):
                chain(dve.scalar_tensor_tensor(n_passes, expert_count, float(n), n_passes, ALU.is_gt, ALU.add))
                chain.settle()
            chain(dve.tensor_tensor_scan(cum_passes, ones_row, n_passes, 0.0, ALU.mult, ALU.add))
            chain.settle()
            chain(dve.tensor_copy(passes_upto[:, :], cum_passes[0:1, :]))
            chain(dve.tensor_scalar(scatters_upto, cum_passes[0:1, :], 16.0, None, ALU.mult))
            dve.wait_ge(h2_ready, NT)
            chain(dve.tensor_scalar(earlier, cum_passes, pass_number, None, ALU.is_le))
            chain.settle()
            chain(dve.tensor_reduce(pass_col[:, 0:1], earlier, AX_X, ALU.add))
            chain(dve.tensor_tensor(n_passes, earlier, cum_passes, ALU.mult))
            chain.settle()
            chain(dve.tensor_reduce(pass_col[:, 1:2], n_passes, AX_X, ALU.max))
            chain.settle()
            chain(dve.tensor_tensor(pass_col[:, 2:3], pass_number, pass_col[:, 1:2], ALU.subtract))
            chain.settle()
            near = cst[:, C_IDENT:C_IDENT + MAX_PASSES + 1]
            chain(dve.tensor_scalar(pass_diag[:, 0, :], near, pass_col[:, 0:1], None, ALU.mult))
            dve.tensor_scalar(pass_diag[:, 1, :], near, pass_col[:, 2:3], None, ALU.mult).then_inc(diag_ready, 1)
            dve.wait_ge(pass_rows, 1)
            chain(dve.tensor_scalar(pass_first, bank[7][:, 128 + MAX_PASSES + 1:128 + 2 * (MAX_PASSES + 1)],
                                    float(SLOTS), None, ALU.mult))
            dve.tensor_scalar(pass_expert[:, :], bank[7][0:1, 128:128 + MAX_PASSES + 1], float(NE - 1), None, ALU.min).then_inc(table_ready, 1)
            dve.wait_ge(table_ready, 2)
            chain.settle()

            def of(ap, e):
                return ap[:, :, e:e + 1] if isinstance(e, int) else ap[:, :, bass.ds(e, 1)]

            def expert_of(p):
                return dve.value_load(at(pass_expert, p), min_val=0, max_val=NE - 1)

            def col(m, n):
                return m[:, n:n + 1] if isinstance(n, int) else m[:, bass.ds(n, 1)]

            def slots_one_hot(p, e):
                wait(dve, list_ready, p)
                chain(dve.tensor_copy(first_cur[:, :], col(pass_first, p)))
                chain(dve.tensor_copy(pos_cur[:, :].unsqueeze(2), of(slot_of, e)))
                chain(dve.tensor_copy(route_cur.unsqueeze(2), of(route, e)))
                chain.settle()
                for i in range(NT):
                    ins = dve.tensor_scalar(onehot[:, i, :], slot_id, first_cur[:, 0:1], pos_cur[:, i:i + 1],
                                            ALU.add, ALU.is_equal)
                    if i < NT - 1:
                        chain(ins)
                chain.settle()
                ins.then_inc(onehot_ready, 1)

            def read_list(p):
                dve.wait_ge(list_ready, p + 1)
                wait(dve, gathered, 16 * p)
                chain(dve.tensor_scalar(dest_next[:, :], bank[5][:, 0:1], NOWHERE, None, ALU.add))
                chain(dve.tensor_copy(gate_next[:, :], bank[5][:, 2:3]))
                chain.settle()
                dve.tensor_copy(token_next[:, :], bank[5][:, 1:2]).then_inc(idx_ready, 1)

            def pick(p, e):
                wait(dve, chunk_used, CHUNKS * (p - 1) + IN_CHUNKS)
                for n in range(2):
                    rows = slice(n * NE, (n + 1) * NE)
                    at_e = cst[rows, C_IDENT + n * NE:C_IDENT + (n + 1) * NE]
                    dve.tensor_copy(pick_bias[rows, :], col(at_e, e).to_broadcast([NE, SLOTS])).then_inc(pick_ready, 1)

            def make_lo(p, j):
                dve.wait_ge(hi_made, CHUNKS * p + j + 1)
                dve.tensor_tensor(lo[j % PARTS][:, 0:DVE_K, :], raw[j % RAW][:, 0:DVE_K, :],
                                  hi[j % PARTS][:, 0:DVE_K, :].bitcast(F32), ALU.subtract).then_inc(lo_by_dve, 1)

            def x_lo(p):
                for a in range(2):
                    dve.wait_ge(xT_hi_made, 2 * p + a + 1)
                    tiles = slice(a * KH, (a + 1) * KH)
                    dve.tensor_tensor(xT_lo[:, tiles, :], bank[6 + a].rearrange("p (k t) -> p k t", k=KH),
                                      xT_hi[:, tiles, :].bitcast(F32), ALU.subtract).then_inc(xT_lo_made, 1)

            def swiglu(p, g):
                n = 4 * p + g
                h = bank[g].rearrange("p (c a) -> p a c", a=2)
                dve.wait_ge(chunk_used, CHUNKS * p + 2 * g + 2)
                dve.tensor_scalar(glu, h[:, 0, :], LIMIT, None, ALU.min).then_inc(glu_ready, 1)
                dve.tensor_scalar(lin, h[:, 1, :], LIMIT, -LIMIT, ALU.min, ALU.max).then_inc(h_read, 1)
                dve.wait_ge(sig_ready, n + 1)
                chain(dve.tensor_tensor(gs, glu, sig, ALU.mult))
                chain.settle()
                dve.wait_ge(h_read, n + 1)
                wait(dve, act_transposed, n - 1)
                dve.scalar_tensor_tensor(act_rows[:, g % 2, :], lin, 1.0, gs, ALU.add, ALU.mult)\
                    .then_inc(act_ready, 1)
                dve.wait_ge(act_ready, n + 1)

            def act_lo(p, g):
                dve.wait_ge(actT_hi_made, 4 * p + g + 1)
                tiles = slice(2 * g, 2 * g + 2)
                dve.tensor_tensor(actT_lo[:, tiles, :], bank[6 + g % 2][:, 0:256].rearrange("p (k t) -> p k t", k=2),
                                  actT_hi[:, tiles, :].bitcast(F32), ALU.subtract).then_inc(actT_lo_made, 1)

            def one_pass(p):
                following = expert_of(p + 1)
                for s in range(CHUNKS):
                    if s % 2 and s < IN_CHUNKS:
                        swiglu(p, s // 2)
                    if s in (3, 5, 7, 8):
                        act_lo(p, (s - 2) // 2)
                    if s == 9:
                        x_lo(p + 1)
                    if s + LO_AHEAD < CHUNKS:
                        make_lo(p, s + LO_AHEAD)
                    else:
                        make_lo(p + 1, s + LO_AHEAD - CHUNKS)
                    if s == 0:
                        slots_one_hot(p + 1, following)
                    if s == 4:
                        wait(dve, scattered, 16 * p)
                        wait(dve, y_scaled, 2 * p)
                        chain(dve.tensor_copy(dest_cur[:, :], dest_next[:, :]))
                        dve.tensor_copy(gate_cur[:, :], gate_next[:, :]).then_inc(cur_ready, 1)
                        chain.settle()
                        dve.wait_ge(cur_ready, p + 1)
                        read_list(p + 1)
                    if s == 8:
                        pick(p + 1, following)

            dve.wait_ge(b_in_rounded, 1)
            first = expert_of(0)
            slots_one_hot(0, first)
            pick(0, first)
            copy_gates(1)
            read_list(0)
            add_bias(1)
            add_bias(2)
            add_bias(3)
            low = slice(NE, 2 * NE)
            dve.tensor_tensor(b_in_parts[low, :], b_in_rows[low, :], b_in_parts[low, :].bitcast(F32), ALU.subtract)\
                .then_inc(b_in_split, 1)
            load_pass_count(dve)
            for j in range(LO_AHEAD):
                make_lo(0, j)
            x_lo(0)
            one_pass(0)
            start = chain.n
            chain.n = 0

            def counted_pass(p):
                chain.before = start + (p - 1) * STEPS_PER_PASS
                one_pass(p)
                assert chain.n == STEPS_PER_PASS, chain.n

            by_pass(dve, counted_pass)
            chain = Chain(dve, tail_step)
            for r in range(TOPK):
                for i in range(NT):
                    dve.wait_ge(parts_loaded[r] if r < TOPK - 1 else last_part_loaded[i], 16)
                    if r:
                        dve.wait_ge(sum_ready, (r - 1) * NT + i + 1)
                    else:
                        dve.wait_ge(bias_out_ready, 2 * NT)
                    dve.tensor_tensor(resid[:, i, :], resid[:, i, :], parts[r][:, i, :], ALU.add).then_inc(sum_ready, 1)
            dve.wait_ge(gf_loaded, 16)
            for i in range(NT):
                dve.wait_ge(sum_root, i + 1)
                chain(dve.reciprocal(stat[:, 52 + i:53 + i], stat[:, 52 + i:53 + i]))
                chain.settle()
                dve.scalar_tensor_tensor(parts[0][:, i, :], resid[:, i, :], stat[:, 52 + i:53 + i], gf_row,
                                         ALU.mult, ALU.mult).then_inc(out_ready, 1)

        @block.gpsimd
        def _(pool):
            for c in range(NCHUNK):
                pool.wait_ge(w_hi_made, c + 1)
                s, tiles = c % PARTS, slice(W_DVE_K, KT)
                pool.tensor_tensor(w_lo[s][:, tiles, :], ring[:, c % W_RAW, tiles, :],
                                   w_hi[s][:, tiles, :].bitcast(F32), ALU.subtract).then_inc(w_lo_by_pool, 1)
            pool.wait_ge(qk_transposed, 12)
            pool.wait_ge(const_loaded, 48)
            for h in range(NH):
                k_rows = proj[:, :, CRK + h * DQ:CRK + (h + 1) * DQ]
                pool.tensor_scalar(k_rows, k_rows, cst[:, C_KDEC + h:C_KDEC + h + 1], None, ALU.mult).then_inc(k_scaled, 1)
            for i in range(NT):
                g = proj[:, i, CRG:PROJ]
                pool.wait_ge(silu_sig, i + 1)
                pool.tensor_tensor(g, g, mix[:, i, 512:D], ALU.mult).then_inc(silu_done, 1)
                pool.wait_ge(silu_done, 2 * i + 1)
                pool.wait_ge(small_loaded, 16 * N_SMALL)
                pool.tensor_tensor(g, g, gain_row[:, 512:D], ALU.mult).then_inc(silu_done, 1)
            for i in range(NT):
                pool.wait_ge(av_evicted, i + 1)
                pool.tensor_tensor(mix[:, i, 0:512], mix[:, i, 0:512], gain_row[:, 0:512], ALU.mult).then_inc(mix_gained, 1)
            pool.wait_ge(silu_done, 2 * NT)
            for i in range(NT):
                pool.wait_ge(ret_evicted, i + 1)
                pool.tensor_tensor(mix[:, i, 512:D], mix[:, i, 512:D], proj[:, i, CRG:PROJ], ALU.mult).then_inc(mix_gained, 1)
            pool.wait_ge(mix_gained, 2 * NT)
            pool.wait_ge(ret_out, NT)
            pool.dma_start(g2_row, for_all_partitions(norm2_g[0]).rearrange("p (a c) -> p a c", a=NT))\
                .then_inc(late_loaded[0], 16)
            pool.dma_start(w_router_sb, w_router.rearrange("a (k p) e -> (a p) k e", p=P)).then_inc(late_loaded[1], 16)
            for n in range(2):
                pool.dma_start(b_in_rows[n * NE:(n + 1) * NE, :], b_moe_in[0]).then_inc(late_loaded[2], 16)
            pool.dma_start(b_out_rows, b_moe_out[0]).then_inc(late_loaded[3], 16)
            pool.iota(token_id, [[TOPK * P, NT]], base=0, channel_multiplier=TOPK,
                      allow_small_or_imprecise_dtypes=True).then_inc(tokens_named, 1)
            pool.iota(expert_id, [[1, NE]], base=0, channel_multiplier=0,
                      allow_small_or_imprecise_dtypes=True).then_inc(tokens_named, 1)
            pool.iota(slot_id, [[1, SLOTS]], base=0, channel_multiplier=0,
                      allow_small_or_imprecise_dtypes=True).then_inc(tokens_named, 1)
            pool.iota(pass_number, [[1, 1]], base=0, channel_multiplier=1,
                      allow_small_or_imprecise_dtypes=True).then_inc(tokens_named, 1)
            pool.memset(ones_row, 1.0).then_inc(tokens_named, 1)
            pool.wait_ge(logits_ready, NT)
            pool.wait_ge(h2_stored, 16 * NT)
            pool.dma_start(gf_row, for_all_partitions(norm_f_g)).then_inc(gf_loaded, 16)


            def make_lo(p, j):
                pool.wait_ge(hi_made, CHUNKS * p + j + 1)
                pool.tensor_tensor(lo[j % PARTS][:, DVE_K:KH, :], raw[j % RAW][:, DVE_K:KH, :],
                                   hi[j % PARTS][:, DVE_K:KH, :].bitcast(F32), ALU.subtract).then_inc(lo_by_pool, 1)

            def gather(p):
                pool.wait_ge(idx_ready, p + 1)
                wait(pool, x_transposed, 2 * p)
                pool.sem_inc(pool_passed, 1)
                pool.indirect_dma_start(out=x_rows, out_offset=None, in_=h2_dram,
                                        in_offset=bass.IndirectOffsetOnAxis(ap=token_next[:, 0:1], axis=0))\
                    .then_inc(gathered, 16)

            def scatter(p):
                pool.wait_ge(y_scaled, 2 * (p + 1))
                pool.sem_inc(pool_passed, 1)
                pool.indirect_dma_start(out=y_dram, in_=y_rows, in_offset=None,
                                        out_offset=bass.IndirectOffsetOnAxis(ap=dest_cur[:, 0:1], axis=0),
                                        bounds_check=SEQ * TOPK - 1, oob_is_err=False).then_inc(scattered, 16)

            def one_pass(p):
                for s in range(CHUNKS):
                    if s + AHEAD < CHUNKS:
                        make_lo(p, s + AHEAD)
                    else:
                        make_lo(p + 1, s + AHEAD - CHUNKS)
                    if s == 5:
                        gather(p + 1)
                scatter(p)

            gather(0)
            pool.sem_inc(gather_started, 1)
            load_pass_count(pool)
            for j in range(AHEAD):
                make_lo(0, j)
            one_pass(0)
            by_pass(pool, one_pass)


_INS = ["x", "positions", "norm1_g", "w_in", "lambda_q1", "lambda_k1", "lambda_q2", "lambda_k2", "diff_norm_g",
        "ret_norm_g", "w_o", "norm2_g", "w_router", "b_router", "w_moe_in", "b_moe_in", "w_moe_out", "b_moe_out",
        "norm_f_g"]


def kernel(**inputs):
    import numpy as _np
    import concourse.bacc as _bacc
    from concourse import mybir as _mybir
    from concourse.bass_utils import run_bass_kernel_spmd as _run

    nc = _bacc.Bacc("TRN2", target_bir_lowering=False, num_devices=1)
    arrays, args = {}, []
    for name in _INS:
        a = _np.ascontiguousarray(inputs[name])
        arrays[f"in_{name}"] = a
        args.append(nc.dram_tensor(f"in_{name}", a.shape, _mybir.dt.from_np(a.dtype), kind="ExternalInput").ap())
    out = nc.dram_tensor("out", (1, SEQ, D), F32, kind="ExternalOutput").ap()
    build(nc, *args, out)
    r = _run(nc, [arrays], core_ids=[0])
    return r.results[0]["out"]
```
